# Optimizing a Trainium2 kernel written in Bass

```python
import math
import jax
import jax.numpy as jnp
from jax import lax
import numpy as np

D_MODEL = 1024
BATCH = 1
SEQ = 1024
DEPTH = 2
DEC_BATCH = 8
DEC_SEQ = 1
PAST_LEN = 4096
PAGE_SIZE = 128

N_AB = (DEPTH + 1) // 2
N_C = DEPTH // 2
SB_HEADS = 8
SB_HEAD_DIM = 64
SB_WIDTH = SB_HEADS * SB_HEAD_DIM
SB_BLOCK = 128
SB_LOGIT_BIAS_INIT = -8.0
GDN_HEADS = 4
GDN_DK = 128
GDN_DV = 128
GDN_WIDTH = GDN_HEADS * GDN_DV
GDN_CONV_DIM = GDN_HEADS * (2 * GDN_DK + GDN_DV)
CONV_W = 4
GDN_CHUNK = 64
AB_SIZES = (SB_WIDTH, SB_WIDTH, SB_WIDTH, SB_WIDTH, GDN_CONV_DIM, GDN_WIDTH, GDN_HEADS, GDN_HEADS)
AB_IN = 4 * SB_WIDTH + GDN_CONV_DIM + GDN_WIDTH + 2 * GDN_HEADS
AB_OUT = SB_WIDTH + GDN_WIDTH
RET_HEADS = 4
RET_DK = D_MODEL // RET_HEADS
RET_DV = 2 * D_MODEL // RET_HEADS
RET_WIDTH = RET_HEADS * RET_DV
RET_CHUNK = 128
ROPE_BASE = 10000.0
C_SIZES = (RET_HEADS * RET_DK, RET_HEADS * RET_DK, RET_WIDTH, RET_WIDTH)
C_IN = 2 * RET_HEADS * RET_DK + 2 * RET_WIDTH
MEM_LEN = 256
XA_HEADS = 4
XA_HEAD_DIM = D_MODEL // XA_HEADS
NORM_EPS = 1e-6

kernel_name = 'hybrid_stickbreak_gdn_retention_memxattn_step'

def rms_norm(x, g):
    xf = x.astype(jnp.float32)
    y = xf * lax.rsqrt(jnp.mean(xf * xf, axis=-1, keepdims=True) + NORM_EPS)
    return y.astype(x.dtype) * g

def l2_normalize(x):
    return x * lax.rsqrt(jnp.sum(x * x, axis=-1, keepdims=True) + NORM_EPS)

def split_last(x, sizes):
    return jnp.split(x, np.cumsum(sizes)[:-1].tolist(), axis=-1)

def to_chunks(a, c):
    b, t = a.shape[0], a.shape[1]
    a = a.reshape((b, t // c, c) + a.shape[2:])
    return jnp.moveaxis(a, (1, 2), (0, 3))

def from_chunks(a):
    n, b, h, c = a.shape[:4]
    return jnp.moveaxis(a, (0, 3), (1, 2)).reshape((b, n * c, h) + a.shape[4:])

def rotary(x, pos):
    half = x.shape[-1] // 2
    inv = ROPE_BASE ** (-jnp.arange(half, dtype=jnp.float32) / half)
    ang = pos.astype(jnp.float32)[:, None] * inv[None, :]
    cos = jnp.cos(ang)[None, :, None, :]
    sin = jnp.sin(ang)[None, :, None, :]
    x1, x2 = x[..., :half], x[..., half:]
    return jnp.concatenate([x1 * cos - x2 * sin, x2 * cos + x1 * sin], axis=-1)

def causal_conv(x_new, buf, w):
    xx = jnp.concatenate([buf.astype(x_new.dtype), x_new], axis=1)
    y = lax.conv_general_dilated(xx, w[:, None, :].astype(xx.dtype), window_strides=(1,), padding='VALID',
                                 dimension_numbers=('NWC', 'WIO', 'NWC'), feature_group_count=xx.shape[-1])
    return y, xx[:, xx.shape[1] - (CONV_W - 1):]

def stick_breaking_block(q, k, v, bias, q_pos, k_pos):
    z = (jnp.einsum('bqhd,bkhd->bhqk', q, k).astype(jnp.float32) * (SB_HEAD_DIM ** -0.5)
         + bias.astype(jnp.float32)[None, :, None, None])
    mask = k_pos[None, :] < q_pos[:, None]
    log_keep = jnp.where(mask, jax.nn.log_sigmoid(-z), 0.0)
    between = lax.cumsum(log_keep, axis=3, reverse=True) - log_keep
    a = jnp.where(mask, jnp.exp(jax.nn.log_sigmoid(z) + between), 0.0)
    return jnp.einsum('bhqk,bkhd->bqhd', a.astype(v.dtype), v)

def stick_breaking(q, k_all, v_all, bias, q_pos):
    b, t, h, d = q.shape
    k_pos = jnp.arange(k_all.shape[1])
    if t <= SB_BLOCK:
        return stick_breaking_block(q, k_all, v_all, bias, q_pos, k_pos)
    nb = t // SB_BLOCK
    qb = jnp.moveaxis(q.reshape(b, nb, SB_BLOCK, h, d), 1, 0)
    pb = q_pos.reshape(nb, SB_BLOCK)
    ob = lax.map(lambda xs: stick_breaking_block(xs[0], k_all, v_all, bias, xs[1], k_pos), (qb, pb))
    return jnp.moveaxis(ob, 0, 1).reshape(b, t, h, d)

def gated_delta_chunked(q, k, v, g, beta, s0, chunk):
    qc, kc, vc = to_chunks(q, chunk), to_chunks(k, chunk), to_chunks(v, chunk)
    gc = jnp.cumsum(to_chunks(g, chunk), axis=-1)
    bc = to_chunks(beta, chunk)
    tril = jnp.tril(jnp.ones((chunk, chunk), dtype=bool))
    stril = jnp.tril(jnp.ones((chunk, chunk), dtype=bool), -1)
    decay = jnp.exp(jnp.where(tril, gc[..., :, None] - gc[..., None, :], -jnp.inf))
    kb = kc * bc[..., None]
    eye = jnp.eye(chunk, dtype=jnp.float32)
    lower = eye + jnp.where(stril, jnp.einsum('nbhid,nbhjd->nbhij', kb, kc) * decay, 0.0)
    tmat = lax.linalg.triangular_solve(lower, jnp.broadcast_to(eye, lower.shape), left_side=True,
                                       lower=True, unit_diagonal=True)
    u = jnp.einsum('nbhij,nbhje->nbhie', tmat, vc * bc[..., None])
    w = jnp.einsum('nbhij,nbhjd->nbhid', tmat, kb * jnp.exp(gc)[..., None])

    def step(s, xs):
        qi, ki, ui, wi, gi, di = xs
        v_new = ui - jnp.einsum('bhcd,bhde->bhce', wi, s)
        attn = jnp.einsum('bhid,bhjd->bhij', qi, ki) * di
        o = (jnp.einsum('bhcd,bhde->bhce', qi * jnp.exp(gi)[..., None], s)
             + jnp.einsum('bhij,bhje->bhie', attn, v_new))
        g_last = gi[..., -1:]
        s = (s * jnp.exp(g_last)[..., None]
             + jnp.einsum('bhcd,bhce->bhde', ki * jnp.exp(g_last - gi)[..., None], v_new))
        return s, o

    s, o = lax.scan(step, s0, (qc, kc, u, w, gc, decay))
    return from_chunks(o), s

def retention_chunked(q, k, v, s0, chunk):
    h = q.shape[2]
    lg = jnp.log1p(-jnp.exp2(-5.0 - jnp.arange(h, dtype=jnp.float32)))
    idx = jnp.arange(chunk, dtype=jnp.float32)
    diff = idx[:, None] - idx[None, :]
    dmask = jnp.where(diff >= 0, jnp.exp(lg[:, None, None] * jnp.maximum(diff, 0.0)), 0.0)
    xi = jnp.exp(lg[:, None] * (idx + 1.0))[..., None]
    zeta = jnp.exp(lg[:, None] * (chunk - 1.0 - idx))[..., None]
    g_chunk = jnp.exp(lg * chunk)[:, None, None]
    qc, kc, vc = to_chunks(q, chunk), to_chunks(k, chunk), to_chunks(v, chunk)

    def step(s, xs):
        qi, ki, vi = xs
        inner = jnp.einsum('bhid,bhjd->bhij', qi, ki) * dmask
        o = jnp.einsum('bhij,bhje->bhie', inner, vi) + jnp.einsum('bhcd,bhde->bhce', qi * xi, s)
        s = g_chunk * s + jnp.einsum('bhcd,bhce->bhde', ki * zeta, vi)
        return s, o

    s, o = lax.scan(step, s0, (qc, kc, vc))
    return from_chunks(o), s

def mem_xattn(h, mk, mv, wq, wo):
    b, t, _ = h.shape
    q = (h @ wq).reshape(b, t, XA_HEADS, XA_HEAD_DIM)
    s = jnp.einsum('bthd,bmhd->bhtm', q, mk).astype(jnp.float32) * (XA_HEAD_DIM ** -0.5)
    p = jax.nn.softmax(s, axis=-1).astype(mv.dtype)
    o = jnp.einsum('bhtm,bmhd->bthd', p, mv).reshape(b, t, XA_HEADS * XA_HEAD_DIM)
    return o @ wo

def ab_mixer(h, pos, past_k, past_v, conv_buf, s0, w_in, sb_bias, conv_w, a_log, dt_bias, norm_g, w_out):
    b, t, _ = h.shape
    sb_q, sb_k, sb_v, sb_z, qkv, g_z, g_a, g_b = split_last(h @ w_in, AB_SIZES)
    shp = (b, t, SB_HEADS, SB_HEAD_DIM)
    k_rows, v_rows = sb_k.reshape(shp), sb_v.reshape(shp)
    k_all = jnp.concatenate([past_k.astype(k_rows.dtype), k_rows], axis=1)
    v_all = jnp.concatenate([past_v.astype(v_rows.dtype), v_rows], axis=1)
    o_sb = stick_breaking(sb_q.reshape(shp), k_all, v_all, sb_bias, pos).reshape(b, t, SB_WIDTH) * jax.nn.silu(sb_z)
    conv_out, conv_tail = causal_conv(qkv, conv_buf, conv_w)
    gq, gk, gv = jnp.split(jax.nn.silu(conv_out).astype(jnp.float32), [GDN_HEADS * GDN_DK, 2 * GDN_HEADS * GDN_DK], axis=-1)
    gq = l2_normalize(gq.reshape(b, t, GDN_HEADS, GDN_DK)) * (GDN_DK ** -0.5)
    gk = l2_normalize(gk.reshape(b, t, GDN_HEADS, GDN_DK))
    gv = gv.reshape(b, t, GDN_HEADS, GDN_DV)
    beta = jax.nn.sigmoid(g_b.astype(jnp.float32))
    g = -jnp.exp(a_log.astype(jnp.float32)) * jax.nn.softplus(g_a.astype(jnp.float32) + dt_bias.astype(jnp.float32))
    o_g, s_new = gated_delta_chunked(gq, gk, gv, g, beta, s0.astype(jnp.float32), min(GDN_CHUNK, t))
    o_g = rms_norm(o_g, norm_g.astype(jnp.float32)).reshape(b, t, GDN_WIDTH).astype(h.dtype) * jax.nn.silu(g_z)
    y = jnp.concatenate([o_sb, o_g], axis=-1) @ w_out
    return y, k_rows, v_rows, conv_tail, s_new.astype(s0.dtype)

def c_mixer(h, pos, s0, w_in, norm_g, w_out):
    b, t, _ = h.shape
    q, k, v, z = split_last(h @ w_in, C_SIZES)
    q = rotary(q.reshape(b, t, RET_HEADS, RET_DK).astype(jnp.float32), pos)
    k = rotary(k.reshape(b, t, RET_HEADS, RET_DK).astype(jnp.float32), pos) * (RET_DK ** -0.5)
    v = v.reshape(b, t, RET_HEADS, RET_DV).astype(jnp.float32)
    o, s_new = retention_chunked(q, k, v, s0.astype(jnp.float32), min(RET_CHUNK, t))
    o = rms_norm(o, norm_g.astype(jnp.float32)).reshape(b, t, RET_WIDTH).astype(h.dtype) * jax.nn.silu(z)
    return o @ w_out, s_new.astype(s0.dtype)

def trunk(x, sb_past_k, sb_past_v, conv_bufs, gdn_states, ret_states, mem_k, mem_v,
          norm_mix_g, norm_xa_g, w_in_ab, sb_logit_bias, conv_w_gdn, gdn_a_log, gdn_dt_bias, gdn_norm_g, w_out_ab,
          w_in_c, ret_norm_g, w_out_c, xa_wq, xa_wo, norm_final_g):
    pos = sb_past_k.shape[2] + jnp.arange(x.shape[1])
    ks, vs, convs, gdns, rets = [], [], [], [], []
    for layer in range(DEPTH):
        i = layer // 2
        h = rms_norm(x, norm_mix_g[layer])
        if layer % 2 == 0:
            y, k_rows, v_rows, conv_tail, s_gdn = ab_mixer(
                h, pos, sb_past_k[i], sb_past_v[i], conv_bufs[i], gdn_states[i], w_in_ab[i], sb_logit_bias[i],
                conv_w_gdn[i], gdn_a_log[i], gdn_dt_bias[i], gdn_norm_g[i], w_out_ab[i])
            ks.append(k_rows)
            vs.append(v_rows)
            convs.append(conv_tail)
            gdns.append(s_gdn)
        else:
            y, s_ret = c_mixer(h, pos, ret_states[i], w_in_c[i], ret_norm_g[i], w_out_c[i])
            rets.append(s_ret)
        x = x + y
        x = x + mem_xattn(rms_norm(x, norm_xa_g[layer]), mem_k[layer], mem_v[layer], xa_wq[layer], xa_wo[layer])
    return (rms_norm(x, norm_final_g), jnp.stack(ks), jnp.stack(vs), jnp.stack(gdns), jnp.stack(convs), jnp.stack(rets))

def setup_inputs(seed: int = 0) -> dict:
    key = jax.random.key(seed)
    keys = iter(jax.random.split(key, 40))
    f32 = jnp.float32
    n_pages = PAST_LEN // PAGE_SIZE
    n_phys = (DEC_BATCH * n_pages * 5) // 4

    def nrm(shape, scale):
        return jax.random.normal(next(keys), shape, f32) * scale

    inp = {}
    inp['x_prompt'] = nrm((BATCH, SEQ, D_MODEL), 1.0)
    inp['x_sample'] = nrm((DEC_BATCH, DEC_SEQ, D_MODEL), 1.0)
    inp['mem_prompt'] = nrm((BATCH, MEM_LEN, D_MODEL), 1.0)
    inp['cache_sb_k'] = nrm((N_AB, n_phys, PAGE_SIZE, SB_HEADS, SB_HEAD_DIM), 1.0)
    inp['cache_sb_v'] = nrm((N_AB, n_phys, PAGE_SIZE, SB_HEADS, SB_HEAD_DIM), 1.0)
    inp['state_gdn'] = nrm((N_AB, DEC_BATCH, GDN_HEADS, GDN_DK, GDN_DV), GDN_DK ** -0.5)
    inp['state_gdn_conv'] = nrm((N_AB, DEC_BATCH, CONV_W - 1, GDN_CONV_DIM), 1.0)
    inp['state_ret'] = nrm((N_C, DEC_BATCH, RET_HEADS, RET_DK, RET_DV), 0.5)
    inp['cache_mem_k'] = nrm((DEPTH, DEC_BATCH, MEM_LEN, XA_HEADS, XA_HEAD_DIM), 1.0)
    inp['cache_mem_v'] = nrm((DEPTH, DEC_BATCH, MEM_LEN, XA_HEADS, XA_HEAD_DIM), 1.0)
    perm = jax.random.permutation(next(keys), n_phys)
    inp['page_table'] = perm[:DEC_BATCH * n_pages].reshape(DEC_BATCH, n_pages).astype(jnp.int32)
    inp['norm_mix_g'] = 1.0 + nrm((DEPTH, D_MODEL), 0.02)
    inp['norm_xa_g'] = 1.0 + nrm((DEPTH, D_MODEL), 0.02)
    inp['w_in_ab'] = nrm((N_AB, D_MODEL, AB_IN), D_MODEL ** -0.5)
    inp['sb_logit_bias'] = SB_LOGIT_BIAS_INIT + nrm((N_AB, SB_HEADS), 0.25)
    inp['conv_w_gdn'] = nrm((N_AB, CONV_W, GDN_CONV_DIM), CONV_W ** -0.5)
    inp['gdn_a_log'] = jnp.log(jax.random.uniform(next(keys), (N_AB, GDN_HEADS), f32, 1.0, 16.0))
    dt = jnp.exp(jax.random.uniform(next(keys), (N_AB, GDN_HEADS), f32, math.log(1e-3), math.log(1e-1)))
    inp['gdn_dt_bias'] = dt + jnp.log(-jnp.expm1(-dt))
    inp['gdn_norm_g'] = 1.0 + nrm((N_AB, GDN_DV), 0.02)
    inp['w_out_ab'] = nrm((N_AB, AB_OUT, D_MODEL), AB_OUT ** -0.5)
    inp['w_in_c'] = nrm((N_C, D_MODEL, C_IN), D_MODEL ** -0.5)
    inp['ret_norm_g'] = 1.0 + nrm((N_C, RET_DV), 0.02)
    inp['w_out_c'] = nrm((N_C, RET_WIDTH, D_MODEL), RET_WIDTH ** -0.5)
    inp['xa_wq'] = nrm((DEPTH, D_MODEL, D_MODEL), D_MODEL ** -0.5)
    inp['xa_wk'] = nrm((DEPTH, D_MODEL, D_MODEL), D_MODEL ** -0.5)
    inp['xa_wv'] = nrm((DEPTH, D_MODEL, D_MODEL), D_MODEL ** -0.5)
    inp['xa_wo'] = nrm((DEPTH, D_MODEL, D_MODEL), D_MODEL ** -0.5)
    inp['norm_final_g'] = 1.0 + nrm((D_MODEL,), 0.02)
    return inp

def reference(x_prompt, x_sample, mem_prompt, cache_sb_k, cache_sb_v, state_gdn, state_gdn_conv, state_ret,
              cache_mem_k, cache_mem_v, page_table, norm_mix_g, norm_xa_g, w_in_ab, sb_logit_bias, conv_w_gdn,
              gdn_a_log, gdn_dt_bias, gdn_norm_g, w_out_ab, w_in_c, ret_norm_g, w_out_c, xa_wq, xa_wk, xa_wv,
              xa_wo, norm_final_g):
    bp, mlen = mem_prompt.shape[0], mem_prompt.shape[1]
    mem_k_prompt = jnp.einsum('bmd,lde->lbme', mem_prompt, xa_wk).reshape(DEPTH, bp, mlen, XA_HEADS, XA_HEAD_DIM)
    mem_v_prompt = jnp.einsum('bmd,lde->lbme', mem_prompt, xa_wv).reshape(DEPTH, bp, mlen, XA_HEADS, XA_HEAD_DIM)
    dt = x_prompt.dtype
    empty_kv = jnp.zeros((N_AB, bp, 0, SB_HEADS, SB_HEAD_DIM), dt)
    conv0 = jnp.zeros((N_AB, bp, CONV_W - 1, GDN_CONV_DIM), dt)
    gdn0 = jnp.zeros((N_AB, bp, GDN_HEADS, GDN_DK, GDN_DV), dt)
    ret0 = jnp.zeros((N_C, bp, RET_HEADS, RET_DK, RET_DV), dt)
    y_prompt, sb_k_prompt, sb_v_prompt, gdn_state_prompt, gdn_conv_prompt, ret_state_prompt = trunk(
        x_prompt, empty_kv, empty_kv, conv0, gdn0, ret0, mem_k_prompt, mem_v_prompt,
        norm_mix_g, norm_xa_g, w_in_ab, sb_logit_bias, conv_w_gdn, gdn_a_log, gdn_dt_bias, gdn_norm_g, w_out_ab,
        w_in_c, ret_norm_g, w_out_c, xa_wq, xa_wo, norm_final_g)
    n_seq, n_pages = page_table.shape
    past_k = cache_sb_k[:, page_table].reshape(N_AB, n_seq, n_pages * PAGE_SIZE, SB_HEADS, SB_HEAD_DIM)
    past_v = cache_sb_v[:, page_table].reshape(N_AB, n_seq, n_pages * PAGE_SIZE, SB_HEADS, SB_HEAD_DIM)
    y_sample, sb_k_sample, sb_v_sample, gdn_state_sample, gdn_conv_sample, ret_state_sample = trunk(
        x_sample, past_k, past_v, state_gdn_conv, state_gdn, state_ret, cache_mem_k, cache_mem_v,
        norm_mix_g, norm_xa_g, w_in_ab, sb_logit_bias, conv_w_gdn, gdn_a_log, gdn_dt_bias, gdn_norm_g, w_out_ab,
        w_in_c, ret_norm_g, w_out_c, xa_wq, xa_wo, norm_final_g)
    return (y_prompt, y_sample, sb_k_prompt, sb_v_prompt, gdn_state_prompt, gdn_conv_prompt, ret_state_prompt,
            mem_k_prompt, mem_v_prompt, sb_k_sample, sb_v_sample, gdn_state_sample, gdn_conv_sample, ret_state_sample)


_drawn_inputs = setup_inputs


def setup_inputs(seed=0):
    import zlib

    import numpy as np

    out = dict(_drawn_inputs(seed))
    spreads = {}
    factors = {'cache_sb_k': 5.942,
     'cache_sb_v': 4.908,
     'norm_xa_g': 8.0,
     'sb_logit_bias': 8.0,
     'gdn_norm_g': 5.293,
     'ret_norm_g': 6.082,
     'norm_final_g': 3.102}
    for name, (base, spread) in spreads.items():
        noise = np.random.default_rng([zlib.crc32(name.encode()), seed]).standard_normal(out[name].shape)
        drawn = base * np.exp(spread * noise) if base else spread * noise
        out[name] = jnp.asarray(drawn.astype(out[name].dtype))
    for name, factor in factors.items():
        out[name] = (out[name] * factor).astype(out[name].dtype)
    return out
```

```python
import concourse.bass as bass
import numpy as np
from concourse import mybir
from contextlib import ExitStack

D = 1024
T = 1024
S = 8
NT = T + S
MEM = 256
PAST_PAGES = 32
PAGE = 128
N_PHYS = 320
SBH, SBD = 8, 64
GH = 4
XH, XD = 4, 256
RH = 4
KT = D // 128
NCH = 3
CH = NT // NCH
CHUNK = 128
NCK = T // CHUNK
EPS = 1e-6
CLIP = 40.0
GDN_SCALE = 128 ** -0.5

AB_Q, AB_K, AB_GATES, AB_V, AB_QKV = 0, 4, 8, 9, 13
AB_Z = 25
AB_GZ = 29
AB_TILES = 33
C_Q, C_K, C_V, C_PLAIN, C_Z, C_TILES = 0, 8, 16, 32, 32, 48

CONST = {}
_at = 0
for _name, _n in (("ident", 128), ("ones", 128), ("neg_ones", 128), ("neg_tri", 128), ("tri", 128),
                  ("strict_up", 128), ("levels", 7 * 128), ("sb_diag", 512), ("xa_diag", 1024), ("eps", 1),
                  ("gq_scale", 2)):
    CONST[_name] = (_at, _at + _n)
    _at += _n
CONST_W = _at


def constants():
    c = np.zeros((128, CONST_W), np.float32)
    p = np.arange(128)[:, None]
    f = np.arange(128)[None, :]

    def put(name, value):
        a, b = CONST[name]
        c[:value.shape[0], a:b] = value

    put("ident", (p == f).astype(np.float32))
    put("ones", np.ones((128, 128), np.float32))
    put("neg_ones", -np.ones((128, 128), np.float32))
    put("neg_tri", -(p >= f).astype(np.float32))
    put("tri", (p <= f).astype(np.float32))
    put("strict_up", (p < f).astype(np.float32))
    lv = []
    for n in range(7):
        b = 1 << n
        lv.append(((p // (2 * b) == f // (2 * b)) & (p // b % 2 == 1) & (f // b % 2 == 0)).astype(np.float32))
    put("levels", np.concatenate(lv, axis=1))
    on = (p // 32 == p % 32 // 8) & (np.arange(512)[None, :] // 64 == p % 8)
    put("sb_diag", on.astype(np.float32))
    h = np.arange(4)[:, None]
    put("xa_diag", (np.arange(1024)[None, :] // 256 == h).astype(np.float32))
    put("eps", np.full((128, 1), EPS, np.float32))
    put("gq_scale", np.broadcast_to(np.array([128 ** -0.5, 1.0], np.float32), (128, 2)))
    return c


def rope_tables():
    inv = np.float32(10000.0) ** (-np.arange(128, dtype=np.float32) / np.float32(128))
    pos = np.concatenate([np.arange(T), np.full(S, PAST_PAGES * PAGE)]).astype(np.float32)
    ang = inv.astype(np.float32)[:, None] * pos[None, :]
    return np.stack([np.cos(ang), np.sin(ang)], axis=1).astype(np.float32)


RETC_W = 128 + 128 + 3


def retention_tables():
    out = np.zeros((RH, 128, RETC_W), np.float32)
    lg = np.log1p(-np.exp2(-5.0 - np.arange(RH))).astype(np.float32)
    i = np.arange(128, dtype=np.float32)
    scale = np.float32(XD ** -0.5)
    for h in range(RH):
        diff = i[None, :] - i[:, None]
        out[h, :, 0:128] = np.where(diff >= 0, np.exp(lg[h] * np.maximum(diff, 0)), 0) * scale
        out[h, :, 128:256] = np.exp(lg[h] * (i + 1))[None, :]
        out[h, :, 256] = np.exp(lg[h] * (127 - i)) * scale
        out[h, :, 257] = np.exp(lg[h] * 128)
        out[h, :, 258] = np.exp(lg[h])
    return out


class Kit:

    used = ()

    def semaphore(self, name):
        s = self.nc.alloc_semaphore(name)
        self.used = (*self.used, s)
        return s

    def recycle(self, most=100):
        if len(self.used) > most:
            self.nc.all_engine_barrier()
            self.nc.clear_and_free_semaphores(list(self.used))
            self.nc.all_engine_barrier()
            self.used = ()


def seq(eng, n_tiles, body):
    n = n_tiles // 2
    body(0, True, (0, 1))
    if n > 1:
        with eng.Fori(1, n) as i:
            body(i, False, (0, 1))
    if n_tiles % 2:
        body(n, False, (0,))


def loop(eng, n, body):
    body(0, True)
    if n > 1:
        with eng.Fori(1, n) as i:
            body(i, False)


def dram_tile(ap, t):
    return ap[bass.ds(t, 1)].rearrange("o p n -> (o p) n")


def linear(k, w, w0, n_tiles, hi, lo, tokens, n_chunks, func=None, out=None, out0=0, resid=None):
    k.recycle()
    nc, ALU, f32, f32r = k.nc, k.ALU, k.f32, k.f32r
    ch = tokens // n_chunks
    with ExitStack() as ctx:
        def sb(name, shape, dt=f32):
            return ctx.enter_context(nc.sbuf_tensor(k.name(name), shape, dt))

        def sem(name):
            return [k.semaphore(k.name(f"{name}{u}")) for u in range(2)]

        raw = sb("w_raw", [128, 2, KT * 128])
        w_hi = sb("w_hi", [128, 2, KT * 128], f32r)
        w_lo = sb("w_lo", [128, 2, KT * 128], f32r)
        stage = sb("stage", [128, 2, tokens]) if resid is None else None
        loaded, hi_done, lo_done = sem("w_loaded"), sem("w_hi_done"), sem("w_lo_done")
        mm_done, evac_done, stored = sem("mm_done"), sem("evac_done"), sem("stored")
        ps = k.ps

        def acc(u):
            return ps[:, 3 * u:3 * u + n_chunks, 0:ch]

        block = ctx.enter_context(nc.Block())

        @block.sync
        def _(sp):
            def store(i, u):
                sp.wait_ge(evac_done[u], i + 1)
                sp.dma_start(dram_tile(out, out0 + 2 * i + u), stage[:, u, :]).then_inc(stored[u], 16)

            def body(i, first, us):
                for u in us:
                    if not first:
                        sp.wait_ge(lo_done[u], i)
                    sp.dma_start(raw[:, u, :], dram_tile(w, w0 + 2 * i + u)).then_inc(loaded[u], 16)
                if out is not None and not first:
                    for u in (0, 1):
                        store(i - 1, u)

            seq(sp, n_tiles, body)
            if out is not None:
                last = (n_tiles - 1) // 2
                for u in range(2 if n_tiles % 2 == 0 else 1):
                    store(last, u)
                sp.wait_ge(stored[0], 16 * ((n_tiles + 1) // 2))
                sp.wait_ge(stored[1], 16 * (n_tiles // 2))

        def split_hi(eng, copy):
            def body(i, first, us):
                for u in us:
                    eng.wait_ge(loaded[u], 16 * (i + 1))
                    if not first:
                        eng.wait_ge(mm_done[u], i)
                    copy(w_hi[:, u, :], raw[:, u, :]).then_inc(hi_done[u], 1)
            return body

        def split_lo(eng, i, u, first):
            eng.wait_ge(hi_done[u], i + 1)
            eng.tensor_tensor(w_lo[:, u, :], raw[:, u, :], w_hi[:, u, :].bitcast(f32),
                              ALU.subtract).then_inc(lo_done[u], 1)

        if resid is None:
            @block.vector
            def _(dve):
                hi_of = split_hi(dve, dve.tensor_copy)

                def body(i, first, us):
                    for u in us:
                        hi_of(i, first, (u,))
                        split_lo(dve, i, u, first)

                seq(dve, n_tiles, body)

            @block.scalar
            def _(act):
                def body(i, first, us):
                    for u in us:
                        act.wait_ge(mm_done[u], i + 1)
                        if not first:
                            act.wait_ge(stored[u], 16 * i)
                        act.activation(stage[:, u, :].rearrange("p (c n) -> p c n", c=n_chunks), acc(u),
                                       func).then_inc(evac_done[u], 1)

                seq(act, n_tiles, body)
        else:
            @block.scalar
            def _(act):
                seq(act, n_tiles, split_hi(act, act.copy))

            @block.gpsimd
            def _(pool):
                def body(i, first, us):
                    for u in us:
                        split_lo(pool, i, u, first)

                seq(pool, n_tiles, body)

            @block.vector
            def _(dve):
                def body(i, first, us):
                    for u in us:
                        dve.wait_ge(mm_done[u], i + 1)
                        x = resid[:, bass.ds(2 * i + u, 1), :].rearrange("p o (c n) -> p (o c) n", c=n_chunks)
                        dve.tensor_tensor(x, acc(u), x, ALU.add).then_inc(evac_done[u], 1)

                seq(dve, n_tiles, body)

        @block.tensor
        def _(pe):
            def body(i, first, us):
                for u in us:
                    pe.wait_ge(lo_done[u], i + 1)
                    if not first:
                        pe.wait_ge(evac_done[u], i)
                    for c in range(n_chunks):
                        o = ps[:, 3 * u + c, 0:ch]
                        for kt in range(KT):
                            a, b = kt * 128, kt * 128 + 128
                            h, l = hi[:, kt, c * ch:c * ch + ch], lo[:, kt, c * ch:c * ch + ch]
                            pe.matmul(o, w_hi[:, u, a:b], h, start=(kt == 0), stop=False)
                            pe.matmul(o, w_hi[:, u, a:b], l, start=False, stop=False)
                            last = pe.matmul(o, w_lo[:, u, a:b], h, start=False, stop=(kt == KT - 1))
                    last.then_inc(mm_done[u], 1)

            seq(pe, n_tiles, body)


def norm(k, g, g_col, hi, lo, final_out=None):
    k.recycle()
    nc, ALU, AF, f32 = k.nc, k.ALU, k.AF, k.f32
    with ExitStack() as ctx:
        def sb(name, shape):
            return ctx.enter_context(nc.sbuf_tensor(k.name(name), shape, f32))

        def sem(name):
            return k.semaphore(k.name(name))

        sq = sb("sq", [128, 2, NT])
        rstd = sb("rstd", [128, NT])
        y = sb("y", [128, 2, NT])
        sq_done, ss_done, std_done, rstd_done = sem("sq_done"), sem("ss_done"), sem("std_done"), sem("rstd_done")
        y_done, hi_done, lo_done, stored = sem("y_done"), sem("hi_done"), sem("lo_done"), [sem("st0"), sem("st1")]
        x, ps, ones = k.x, k.ps, k.c("ones")
        block = ctx.enter_context(nc.Block())

        @block.scalar
        def _(act):
            for kt in range(KT):
                if kt >= 2:
                    act.wait_ge(ss_done, kt - 1)
                act.activation(sq[:, kt % 2, :], x[:, kt, :], AF.Square).then_inc(sq_done, 1)
            act.wait_ge(ss_done, KT)
            act.activation(rstd[:, :].rearrange("p (c n) -> p c n", c=NCH), ps[:, 0:NCH, 0:CH], AF.Sqrt,
                           bias=k.c("eps"), scale=1.0 / D).then_inc(std_done, 1)
            if final_out is None:
                for kt in range(KT):
                    act.wait_ge(y_done, kt + 1)
                    act.copy(hi[:, kt, :], y[:, kt % 2, :]).then_inc(hi_done, 1)

        @block.tensor
        def _(pe):
            for kt in range(KT):
                pe.wait_ge(sq_done, kt + 1)
                for c in range(NCH):
                    last = pe.matmul(ps[:, c, 0:CH], ones, sq[:, kt % 2, c * CH:c * CH + CH],
                                     start=(kt == 0), stop=(kt == KT - 1))
                last.then_inc(ss_done, 1)

        @block.vector
        def _(dve):
            dve.wait_ge(std_done, 1)
            dve.reciprocal(rstd[:, :], rstd[:, :]).then_inc(rstd_done, 1)
            dve.wait_ge(rstd_done, 1)
            for kt in range(KT):
                if kt >= 2:
                    if final_out is None:
                        dve.wait_ge(lo_done, kt - 1)
                    else:
                        dve.wait_ge(stored[kt % 2], 16 * (kt // 2))
                dve.scalar_tensor_tensor(y[:, kt % 2, :], x[:, kt, :], g[:, g_col + kt:g_col + kt + 1], rstd[:, :],
                                         ALU.mult, ALU.mult).then_inc(y_done, 1)
                if final_out is None:
                    dve.wait_ge(hi_done, kt + 1)
                    dve.tensor_tensor(lo[:, kt, :], y[:, kt % 2, :], hi[:, kt, :].bitcast(f32),
                                      ALU.subtract).then_inc(lo_done, 1)

        if final_out is not None:
            @block.sync
            def _(sp):
                for kt in range(KT):
                    sp.wait_ge(y_done, kt + 1)
                    sp.dma_start(final_out[kt], y[:, kt % 2, :]).then_inc(stored[kt % 2], 16)
                for u in range(2):
                    sp.wait_ge(stored[u], 16 * (KT // 2))


def load_split(k, src, src0, hi, lo, tokens):
    k.recycle()
    nc, ALU, f32 = k.nc, k.ALU, k.f32
    with ExitStack() as ctx:
        y = ctx.enter_context(nc.sbuf_tensor(k.name("in_raw"), [128, 2, tokens], f32))
        loaded = [k.semaphore(k.name(f"loaded{u}")) for u in range(2)]
        hi_done = k.semaphore(k.name("hi_done"))
        lo_done = k.semaphore(k.name("lo_done"))
        block = ctx.enter_context(nc.Block())

        @block.sync
        def _(sp):
            for kt in range(KT):
                if kt >= 2:
                    sp.wait_ge(lo_done, kt - 1)
                sp.dma_start(y[:, kt % 2, :], src[src0 + kt]).then_inc(loaded[kt % 2], 16)

        @block.scalar
        def _(act):
            for kt in range(KT):
                act.wait_ge(loaded[kt % 2], 16 * (kt // 2 + 1))
                act.copy(hi[:, kt, :], y[:, kt % 2, :]).then_inc(hi_done, 1)

        @block.vector
        def _(dve):
            for kt in range(KT):
                dve.wait_ge(hi_done, kt + 1)
                dve.tensor_tensor(lo[:, kt, :], y[:, kt % 2, :], hi[:, kt, :].bitcast(f32),
                                  ALU.subtract).then_inc(lo_done, 1)


SB_STEPS = [(u, c, i) for u in range(2) for c in range(2) for i in range(4 * c + 3, -1, -1)]


def sb_prompt(k, ab, og, bias):
    k.recycle()
    nc, ALU, AF, f32, ps = k.nc, k.ALU, k.AF, k.f32, k.ps
    NS = len(SB_STEPS)
    group = [2 * u + c for u, c, _ in SB_STEPS]
    ends = [s for s in range(NS) if s == NS - 1 or group[s + 1] != group[s]]
    top = [s == 0 or group[s - 1] != group[s] for s in range(NS)]

    def n0_of(s):
        _, c, i = SB_STEPS[s]
        return max(0, 128 * i - 512 * c)

    with ExitStack() as ctx:
        def sb(name, shape):
            return ctx.enter_context(nc.sbuf_tensor(k.name(name), shape, f32))

        def sem(name):
            return k.semaphore(k.name(name))

        inp = sb("sb_in", [128, 4, T])
        q, kt_, vt, gate = (inp[:, j, :] for j in range(4))
        bias_pair = sb("bias_pair", [128, 2])
        vtok = sb("vtok", [128, T // 128, 128])
        zc = sb("zc", [128, 2, 512])
        sp_ = sb("softplus", [128, 2, 512])
        acc = sb("later_blocks", [128, 512])
        a = sb("a", [128, 2, 512])
        gated = sb("gated", [128, T])
        loaded, q_scaled, vt_done, vtok_done = sem("loaded"), sem("q_scaled"), sem("vt_done"), sem("vtok_done")
        z_done, zc_done, e_done, l_done, sp_done = (sem(x) for x in ("z", "zc", "e", "l", "sp"))
        acc_done, sum_done, a_done, av_done, og_done, stored = (
            sem(x) for x in ("acc", "sum", "a", "av", "og", "stored"))
        VB = 5
        block = ctx.enter_context(nc.Block())

        @block.sync
        def _(sp):
            def body(i, first):
                if not first:
                    sp.wait_ge(og_done, 4 * i)
                for j, t0 in enumerate((AB_Q, AB_K, AB_V, AB_Z)):
                    sp.dma_start(inp[:, j, :], dram_tile(ab, t0 + i)[:, 0:T]).then_inc(loaded, 16)
                sp.dma_start(bias_pair[:, :], bias[:, bass.ds(2 * i, 2)].broadcast_to((128, 2))).then_inc(loaded, 16)
                sp.wait_ge(og_done, 4 * i + 4)
                sp.dma_start(dram_tile(og, i)[:, 0:T], gated[:, :]).then_inc(stored, 16)

            loop(sp, 4, body)
            sp.wait_ge(stored, 64)

        @block.tensor
        def _(pe):
            def body(p, first):
                pe.wait_ge(loaded, 80 * (p + 1))
                for t in range(T // 128):
                    last = pe.transpose(ps[:, VB + t // 4, t % 4 * 128:t % 4 * 128 + 128],
                                        vt[:, t * 128:t * 128 + 128], k.c("ident"))
                last.then_inc(vt_done, 1)

                def z(s):
                    u, c, i = SB_STEPS[s]
                    n0, h = n0_of(s), slice(64 * u, 64 * u + 64)
                    if s >= 3:
                        pe.wait_ge(a_done, NS * p + s - 2)
                    o = ps[:, s % 3, n0:512]
                    last = pe.matmul(o, kt_[h, 128 * i:128 * i + 128], q[h, 512 * c + n0:512 * c + 512],
                                     start=True, stop=(i < 4 * c))
                    if i >= 4 * c:
                        last = pe.matmul(ps[:, s % 3, n0:n0 + 128], k.c("ident"), k.sb_mask[:, :],
                                         start=False, stop=True)
                    last.then_inc(z_done, 1)

                def sums(s):
                    n0 = n0_of(s)
                    pe.wait_ge(sp_done, NS * p + s + 1)
                    last = pe.matmul(ps[:, s % 3, n0:512], k.c("neg_tri"), sp_[:, s % 2, n0:512],
                                     start=False, stop=top[s], skip_group_check=True)
                    if not top[s]:
                        pe.wait_ge(acc_done, NS * p + s + 1)
                        last = pe.matmul(ps[:, s % 3, n0:512], k.c("neg_ones"), acc[:, n0:512],
                                         start=False, stop=True, skip_group_check=True)
                    last.then_inc(sum_done, 1)

                def av(s):
                    u, c, i = SB_STEPS[s]
                    n0, g = n0_of(s), group[s]
                    if s == 0:
                        pe.wait_ge(vtok_done, p + 1)
                    pe.wait_ge(a_done, NS * p + s + 1)
                    if top[s] and g >= 2:
                        pe.wait_ge(og_done, 4 * p + g - 1)
                    pe.matmul(ps[64 * u:64 * u + 64, 3 + g % 2, n0:512], vtok[:, i, 64 * u:64 * u + 64],
                              a[:, s % 2, n0:512], start=top[s], stop=(s in ends),
                              skip_group_check=True).then_inc(av_done, 1)

                pe.wait_ge(q_scaled, p + 1)
                z(0)
                for s in range(NS):
                    if s + 1 < NS:
                        z(s + 1)
                    sums(s)
                    if s >= 1:
                        av(s - 1)
                av(NS - 1)

            loop(pe, 4, body)

        @block.vector
        def _(dve):
            def body(p, first):
                dve.wait_ge(loaded, 80 * (p + 1))
                dve.tensor_scalar(q, q, 0.125, None, ALU.mult).then_inc(q_scaled, 1)

                def clip(s):
                    n0, b = n0_of(s), bias_pair[:, SB_STEPS[s][0]:SB_STEPS[s][0] + 1]
                    dve.wait_ge(z_done, NS * p + s + 1)
                    if s >= 2 or not first:
                        dve.wait_ge(sp_done, NS * p + s - 1)
                    dve.tensor_scalar(zc[:, s % 2, n0:512], ps[:, s % 3, n0:512], b, CLIP, ALU.add,
                                      ALU.min).then_inc(zc_done, 1)

                clip(0)
                for s in range(NS):
                    if s + 1 < NS:
                        clip(s + 1)
                    n0, b = n0_of(s), bias_pair[:, SB_STEPS[s][0]:SB_STEPS[s][0] + 1]
                    dve.wait_ge(l_done, NS * p + s + 1)
                    if s >= 2 or not first:
                        dve.wait_ge(acc_done, NS * p + s)
                    dve.scalar_tensor_tensor(sp_[:, s % 2, n0:512], ps[:, s % 3, n0:512], b, zc[:, s % 2, n0:512],
                                             ALU.add, ALU.max).then_inc(sp_done, 1)
                    done = [g for g, e in enumerate(ends) if e == s - 2 or (s == NS - 1 and e == s)]
                    for g in done:
                        u, c = g // 2, g % 2
                        dve.wait_ge(av_done, NS * p + ends[g] + 1)
                        if g == 0 and not first:
                            dve.wait_ge(stored, 16 * p)
                        h = slice(64 * u, 64 * u + 64)
                        dve.tensor_tensor(gated[h, 512 * c:512 * c + 512], ps[h, 3 + g % 2, :],
                                          gate[h, 512 * c:512 * c + 512], ALU.mult).then_inc(og_done, 1)

            loop(dve, 4, body)

        @block.scalar
        def _(act):
            act.preload_act_table_set("natural_log_exp_and_others")

            def body(p, first):
                act.wait_ge(vt_done, p + 1)
                act.copy(vtok[:, :, :].rearrange("p (b t) n -> p b (t n)", b=2),
                         ps[:, VB:VB + 2, :]).then_inc(vtok_done, 1)

                def weight(s):
                    n0, b = n0_of(s), bias_pair[:, SB_STEPS[s][0]:SB_STEPS[s][0] + 1]
                    act.wait_ge(sum_done, NS * p + s + 1)
                    if s >= 2:
                        act.wait_ge(av_done, NS * p + s - 1)
                    act.activation(a[:, s % 2, n0:512], ps[:, s % 3, n0:512], AF.Exp, bias=b).then_inc(a_done, 1)

                for s in range(NS):
                    z = zc[:, s % 2, n0_of(s):512]
                    act.wait_ge(zc_done, NS * p + s + 1)
                    act.activation(z, z, AF.Exp).then_inc(e_done, 1)
                    act.wait_ge(e_done, NS * p + s + 1)
                    act.activation(z, z, AF.Ln, bias=k.c("ones")[:, 0:1]).then_inc(l_done, 1)
                    if s >= 1:
                        weight(s - 1)
                weight(NS - 1)

            loop(act, 4, body)

        @block.gpsimd
        def _(pool):
            pool.memset(acc[:, :], 0.0).then_inc(acc_done, 1)

            def body(p, first):
                for s in range(NS):
                    n0 = n0_of(s)
                    pool.wait_ge(sum_done, NS * p + s + 1)
                    pool.wait_ge(acc_done, NS * p + s + 1)
                    if s in ends:
                        pool.tensor_tensor(acc[:, :], acc[:, :], acc[:, :], ALU.subtract).then_inc(acc_done, 1)
                    else:
                        pool.tensor_tensor(acc[:, n0:512], acc[:, n0:512], sp_[:, s % 2, n0:512],
                                           ALU.add).then_inc(acc_done, 1)

            loop(pool, 4, body)


W_PLAIN, W_SILU, W_MEM = 2, 1, 4
W_ORDER = (("plain", 0, 0), ("mem", 0, 1), ("plain", 1, 2), ("mem", 1, 0), ("silu", 0, 1), ("mem", 2, 2),
           ("mem", 3, 1))


def weave(k, w_ab, hi, lo, ab, w_mem, m_hi, m_lo, mem_kv, og, cache_k, cache_v, page_table, bias):
    k.recycle(0)
    nc, ALU, AF, f32, f32r, ps = k.nc, k.ALU, k.AF, k.f32, k.f32r, k.ps
    NP, G = PAST_PAGES, 4
    NJ = NP // G
    W = NP * SBH
    SUF = 10
    NPOS = len(W_ORDER)
    A_BANK, M_BANK, SUMB, OB, CB = 0, 3, 5, 6, 7
    with ExitStack() as ctx:
        def sb(name, shape, dt=f32):
            return ctx.enter_context(nc.sbuf_tensor(k.name(name), shape, dt))

        def sem(name):
            return k.semaphore(k.name(name))

        raw = sb("wv_raw", [128, 2, KT * 128])
        w_hi, w_lo = sb("wv_hi", [128, 3, KT * 128], f32r), sb("wv_lo", [128, 3, KT * 128], f32r)
        stage = sb("wv_stage", [128, 3, NT])
        m_stage = sb("wv_mem_stage", [128, 2, MEM])
        pt = sb("page_table", [1, S * NP], mybir.dt.int32)
        qs, gate = sb("qs", [128, 4, S]), sb("gate", [128, 4, S])
        bias_all = sb("bias_all", [128, SBH])
        qbc = sb("q_rows", [128, S, 512])
        kp, vp = sb("k_pages", [128, 2, G * 512]), sb("v_pages", [128, 2, G * 512])
        prod = sb("prod", [128, G * 512])
        z, zc, sp_ = sb("z", [128, W]), sb("zc", [128, W]), sb("softplus", [128, W])
        suf = sb("suffix", [128, 2, W])
        a = sb("a", [128, W])
        om = sb("masked", [128, 512])
        osT, gated = sb("osT", [128, 4, S]), sb("gated", [128, 4, S])

        loaded = [sem(f"w_loaded{n}") for n in range(NPOS)]
        hi_done, lo_done, mm_done, evac_done = sem("w_hi"), sem("w_lo"), sem("mm"), sem("evac")
        stored = [sem(f"w_stored{n}") for n in range(5)]
        (setup, q_rows, q_copied, prod_done, red_done, zb_done, zc_done, e_done, l_done, sp_done, suf_done,
         sum_done, t_done, a_done, pv_done, om_done, col_done, os_done, gate_in, gated_done, og_stored) = (
            sem(x) for x in ("setup", "q_rows", "q_copied", "prod", "red", "zb", "zc", "e", "l", "sp", "suf", "sum",
                             "t", "a", "pv", "om", "col", "os", "gate_in", "gated", "og_stored"))
        k_in, v_in = [sem("k_in0"), sem("k_in1")], [sem("v_in0"), sem("v_in1")]
        block = ctx.enter_context(nc.Block())

        RAW = [pos % 2 for pos in range(NPOS)]
        SLOT = [x[2] for x in W_ORDER]
        BANK = [M_BANK + n % 2 if kind == "mem" else A_BANK for kind, n, _ in W_ORDER]

        def back(of, pos):
            return next(d for d in range(1, NPOS + 1) if of[(pos - d) % NPOS] == of[pos])

        def store_slot(kind, n):
            return {"plain": n, "silu": 2, "mem": 3 + n % 2}[kind]

        def at(step, first, pos, d):
            v = NPOS * step + pos + 1 - d
            return v if not first or v > 0 else None

        def pages(eng, cache, dst, sem_, s, j):
            for g in range(G):
                page = eng.value_load(pt[0:1, bass.ds(s * NP + j * G + g, 1)], min_val=0, max_val=N_PHYS - 1)
                eng.dma_start(dst[:, j % 2, g * 512:(g + 1) * 512], dram_tile(cache, page)).then_inc(sem_[j % 2], 16)

        @block.gpsimd
        def _(pool):
            pool.wait_ge(setup, 48)

            def step(s, first):
                for j in range(NJ):
                    if not (first and j < 2):
                        pool.wait_ge(pv_done, NJ * s + j - 1)
                    pages(pool, cache_v, vp, v_in, s, j)

            loop(pool, S, step)

        @block.sync
        def _(sp):
            sp.dma_start(pt[:, :], page_table).then_inc(setup, 16)
            sp.dma_start(bias_all[:, :], bias.broadcast_to((128, SBH))).then_inc(setup, 16)
            sp.dma_start(qs[:, :, :], ab[AB_Q:AB_Q + 4, :, T:NT].rearrange("t p n -> p t n")).then_inc(setup, 16)
            sp.wait_ge(setup, 48)

            def weights(s, first, pos):
                kind, n, _ = W_ORDER[pos]
                v = at(s, first, pos, back(RAW, pos))
                if v is not None:
                    sp.wait_ge(lo_done, v)
                t = {"plain": AB_V + W_PLAIN * s + n, "silu": AB_Z + s, "mem": W_MEM * s + n}[kind]
                sp.dma_start(raw[:, RAW[pos], :], dram_tile(w_mem if kind == "mem" else w_ab, t)).then_inc(loaded[pos], 16)

            def k_pages(s, j, first):
                if not (first and j < 2):
                    sp.wait_ge(prod_done, NJ * s + j - 1)
                pages(sp, cache_k, kp, k_in, s, j)

            def step(s, first, last=False):
                for j in range(NJ):
                    if j < NPOS:
                        weights(s, first, j)
                    if not last:
                        k_pages(s + 1, j, False)

            for j in range(NJ):
                k_pages(0, j, True)
            loop(sp, S - 1, step)
            step(S - 1, False, last=True)
            sp.wait_ge(os_done, S)
            sp.wait_ge(stored[2], 16 * S)
            sp.dma_start(gate[:, :, :], ab[AB_Z:AB_Z + 4, :, T:NT].rearrange("t p n -> p t n")).then_inc(gate_in, 16)
            sp.wait_ge(gated_done, 1)
            sp.dma_start(og[0:4, :, T:NT].rearrange("t p n -> p t n"), gated[:, :, :]).then_inc(og_stored, 16)
            sp.wait_ge(og_stored, 16)

        @block.vector
        def _(dve):
            v3 = lambda x: x.rearrange("p (n h) -> p n h", h=SBH)
            v4 = lambda x: x.rearrange("p (g n) -> p g n", g=G)

            def split(s, first, pos):
                _, _, slot = W_ORDER[pos]
                dve.wait_ge(loaded[pos], 16 * (s + 1))
                v = at(s, first, pos, back(SLOT, pos))
                if v is not None:
                    dve.wait_ge(mm_done, v)
                dve.tensor_copy(w_hi[:, slot, :], raw[:, RAW[pos], :]).then_inc(hi_done, 1)
                dve.wait_ge(hi_done, NPOS * s + pos + 1)
                dve.tensor_tensor(w_lo[:, slot, :], raw[:, RAW[pos], :], w_hi[:, slot, :].bitcast(f32),
                                  ALU.subtract).then_inc(lo_done, 1)

            def scores(s, j, first):
                dve.wait_ge(k_in[j % 2], 64 * (NJ // 2 * s + j // 2 + 1))
                if not (first and j == 0):
                    dve.wait_ge(red_done, NJ * s + j)
                dve.tensor_tensor(v4(prod[:, :]), v4(kp[:, j % 2, :]),
                                  qbc[:, bass.ds(s, 1), :].broadcast_to((128, G, 512)), ALU.mult).then_inc(prod_done, 1)
                dve.wait_ge(prod_done, NJ * s + j + 1)
                if j == 0 and not first:
                    dve.wait_ge(t_done, s)
                dve.tensor_reduce(z[:, j * G * SBH:(j + 1) * G * SBH], prod[:, :].rearrange("p (n d) -> p n d", d=SBD),
                                  k.AX.X, ALU.add).then_inc(red_done, 1)

            def sums(s, first):
                dve.wait_ge(red_done, NJ * s + NJ)
                dve.scalar_tensor_tensor(v3(z[:, :]), v3(z[:, :]), SBD ** -0.5,
                                         bias_all[:, None, :].broadcast_to((128, NP, SBH)),
                                         ALU.mult, ALU.add).then_inc(zb_done, 1)
                dve.wait_ge(zb_done, s + 1)
                if not first:
                    dve.wait_ge(a_done, s)
                dve.tensor_scalar(zc[:, :], z[:, :], CLIP, None, ALU.min).then_inc(zc_done, 1)
                dve.wait_ge(l_done, s + 1)
                if not first:
                    dve.wait_ge(sum_done, s)
                dve.tensor_tensor(sp_[:, :], z[:, :], zc[:, :], ALU.max).then_inc(sp_done, 1)
                dve.wait_ge(sp_done, s + 1)
                src = sp_[:, :]
                for n in range(5):
                    sh = SBH << n
                    dst = suf[:, n % 2, :]
                    if n >= 1:
                        dve.wait_ge(suf_done, SUF * s + 2 * n)
                    dve.tensor_tensor(dst[:, 0:W - sh], src[:, 0:W - sh], src[:, sh:W], ALU.add).then_inc(suf_done, 1)
                    dve.tensor_copy(dst[:, W - sh:W], src[:, W - sh:W]).then_inc(suf_done, 1)
                    src = dst

            def exponent(s):
                dve.wait_ge(sum_done, s + 1)
                dve.tensor_tensor(zc[:, :], z[:, :], ps[:, SUMB, 0:W], ALU.add).then_inc(t_done, 1)

            def mask(s, first):
                dve.wait_ge(pv_done, NJ * s + NJ)
                if not first:
                    dve.wait_ge(col_done, s)
                dve.tensor_tensor(om[:, :], ps[:, OB, :], k.c("sb_diag"), ALU.mult).then_inc(om_done, 1)

            dve.wait_ge(setup, 48)
            dve.wait_ge(q_copied, S)
            for j in range(NJ):
                scores(0, j, True)
            sums(0, True)
            exponent(0)

            def step(s, first, last=False):
                for j in range(NJ):
                    if j < NPOS:
                        split(s, first, j)
                    if not last:
                        scores(s + 1, j, False)
                if not last:
                    sums(s + 1, False)
                    exponent(s + 1)
                mask(s, first)

            loop(dve, S - 1, step)
            step(S - 1, False, last=True)
            dve.wait_ge(gate_in, 16)
            dve.wait_ge(os_done, S)
            dve.tensor_tensor(gated[:, :, :], osT[:, :, :], gate[:, :, :], ALU.mult).then_inc(gated_done, 1)

        @block.scalar
        def _(act):
            for s in range(S):
                act.wait_ge(q_rows, s + 1)
                act.copy(qbc[:, s, :], ps[:, s % 4, :]).then_inc(q_copied, 1)

            def softplus(s):
                act.wait_ge(zc_done, s + 1)
                act.activation(zc[:, :], zc[:, :], AF.Exp).then_inc(e_done, 1)
                act.wait_ge(e_done, s + 1)
                act.activation(zc[:, :], zc[:, :], AF.Ln, bias=k.c("ones")[:, 0:1]).then_inc(l_done, 1)

            def weights(s, first):
                act.wait_ge(t_done, s + 1)
                if not first:
                    act.wait_ge(pv_done, NJ * s)
                act.activation(a[:, :], zc[:, :], AF.Exp).then_inc(a_done, 1)

            def column(s):
                act.wait_ge(col_done, s + 1)
                act.copy(osT[:, :, bass.ds(s, 1)], ps[:, CB, 0:4].rearrange("p (f o) -> p f o", o=1)).then_inc(os_done, 1)

            def evacuate(s, first, pos):
                kind, n, _ = W_ORDER[pos]
                st = store_slot(kind, n)
                act.wait_ge(mm_done, NPOS * s + pos + 1)
                if kind == "mem":
                    if not first or n >= 2:
                        act.wait_ge(stored[st], 16 * (2 * s + n // 2))
                    act.copy(m_stage[:, n % 2, :], ps[:, M_BANK + n % 2, 0:MEM]).then_inc(evac_done, 1)
                    act.wait_ge(evac_done, NPOS * s + pos + 1)
                    act.dma_start(dram_tile(mem_kv, W_MEM * s + n), m_stage[:, n % 2, :]).then_inc(stored[st], 16)
                else:
                    if not first:
                        act.wait_ge(stored[st], 16 * s)
                    act.activation(stage[:, st, :].rearrange("p (c n) -> p c n", c=NCH), ps[:, A_BANK:A_BANK + 3, 0:CH],
                                   AF.Silu if kind == "silu" else AF.Copy).then_inc(evac_done, 1)
                    act.wait_ge(evac_done, NPOS * s + pos + 1)
                    t = AB_Z + s if kind == "silu" else AB_V + W_PLAIN * s + n
                    act.dma_start(dram_tile(ab, t), stage[:, st, :]).then_inc(stored[st], 16)

            softplus(0)
            weights(0, True)

            def step(s, first, last=False):
                for pos in range(NPOS):
                    evacuate(s, first, pos)
                if not last:
                    softplus(s + 1)
                    weights(s + 1, False)
                column(s)

            loop(act, S - 1, step)
            step(S - 1, False, last=True)
            for n in range(3):
                act.wait_ge(stored[n], 16 * S)
            for n in range(3, 5):
                act.wait_ge(stored[n], 32 * S)

        @block.tensor
        def _(pe):
            pe.wait_ge(setup, 48)
            for s in range(S):
                if s >= 4:
                    pe.wait_ge(q_copied, s - 3)
                for f in range(4):
                    last = pe.matmul(ps[:, s % 4, f * 128:f * 128 + 128],
                                     qs[:, f, s:s + 1].broadcast_to((128, 128)), k.c("ident"), start=True, stop=True)
                last.then_inc(q_rows, 1)

            def sums(s, first):
                pe.wait_ge(sp_done, s + 1)
                if not first:
                    pe.wait_ge(t_done, s)
                pe.matmul(ps[:, SUMB, 0:W], k.c("neg_tri"), sp_[:, :], start=True, stop=False)
                pe.wait_ge(suf_done, SUF * s + SUF)
                pe.matmul(ps[:, SUMB, 0:W - SBH], k.c("neg_ones"), suf[:, 0, SBH:W], start=False,
                          stop=True).then_inc(sum_done, 1)

            def tile(s, first, pos):
                kind, _, slot = W_ORDER[pos]
                pe.wait_ge(lo_done, NPOS * s + pos + 1)
                v = at(s, first, pos, back(BANK, pos))
                if v is not None:
                    pe.wait_ge(evac_done, v)
                if kind == "mem":
                    mov, chunks, width = (m_hi, m_lo), 1, MEM
                else:
                    mov, chunks, width = (hi, lo), NCH, CH
                for c in range(chunks):
                    o = ps[:, BANK[pos] + c, 0:width]
                    for kt in range(KT):
                        x, y = kt * 128, kt * 128 + 128
                        h, l = mov[0][:, kt, c * width:c * width + width], mov[1][:, kt, c * width:c * width + width]
                        pe.matmul(o, w_hi[:, slot, x:y], h, start=(kt == 0), stop=False)
                        pe.matmul(o, w_hi[:, slot, x:y], l, start=False, stop=False)
                        last = pe.matmul(o, w_lo[:, slot, x:y], h, start=False, stop=(kt == KT - 1))
                last.then_inc(mm_done, 1)

            def values(s, j, first):
                if j == 0:
                    pe.wait_ge(a_done, s + 1)
                    if not first:
                        pe.wait_ge(om_done, s)
                pe.wait_ge(v_in[j % 2], 64 * (NJ // 2 * s + j // 2 + 1))
                for g in range(G):
                    last = pe.matmul(ps[32 * g:32 * g + 32, OB, :], a[:, j * 32:j * 32 + 32],
                                     vp[:, j % 2, g * 512:(g + 1) * 512], start=(j == 0), stop=(j == NJ - 1))
                last.then_inc(pv_done, 1)

            def columns(s, first):
                pe.wait_ge(om_done, s + 1)
                for f in range(4):
                    last = pe.matmul(ps[:, CB, f:f + 1], om[:, f * 128:f * 128 + 128], k.c("ones")[:, 0:1],
                                     start=True, stop=True)
                last.then_inc(col_done, 1)

            pe.wait_ge(q_copied, S)
            sums(0, True)

            def step(s, first, last=False):
                for j in range(NJ):
                    if j < NPOS:
                        tile(s, first, j)
                    values(s, j, first)
                if not last:
                    sums(s + 1, False)
                if not first:
                    pe.wait_ge(os_done, s)
                columns(s, first)

            loop(pe, S - 1, step)
            step(S - 1, False, last=True)


def gdn_conv(k, ab, conv, conv_w, conv_buf, conv_s):
    k.recycle()
    nc, ALU, AF, f32 = k.nc, k.ALU, k.AF, k.f32
    N = 12
    with ExitStack() as ctx:
        def sb(name, shape):
            return ctx.enter_context(nc.sbuf_tensor(k.name(name), shape, f32))

        def sem(name):
            return [k.semaphore(k.name(f"{name}{u}")) for u in range(2)]

        x = sb("conv_x", [128, 2, 3 + T])
        new = sb("conv_new", [128, 2, S])
        buf = sb("conv_buf", [128, 2, S, 3])
        w = sb("conv_w", [128, 2, 4])
        y = sb("conv_y", [128, 2, NT])
        o = sb("conv_out", [128, 2, NT])
        tail = sb("conv_tail", [128, 2, S, 3])
        loaded, chain, y_done, act_done, tail_done, stored = (
            sem(n) for n in ("loaded", "chain", "y", "silu", "tail", "stored"))
        zeroed = k.semaphore(k.name("zeroed"))
        block = ctx.enter_context(nc.Block())

        @block.sync
        def _(sp):
            def store(i, u):
                sp.wait_ge(act_done[u], i + 1)
                sp.dma_start(dram_tile(conv, 2 * i + u), o[:, u, :]).then_inc(stored[u], 16)
                sp.wait_ge(tail_done[u], i + 1)
                sp.dma_start(conv_s[bass.ds(2 * i + u, 1)].rearrange("o p s j -> (o p) s j"),
                             tail[:, u]).then_inc(stored[u], 16)

            def body(i, first, us):
                for u in us:
                    if not first:
                        sp.wait_ge(y_done[u], i)
                        sp.wait_ge(tail_done[u], i)
                    t = 2 * i + u
                    src = dram_tile(ab, AB_QKV + t)
                    sp.dma_start(x[:, u, 3:3 + T], src[:, 0:T]).then_inc(loaded[u], 16)
                    sp.dma_start(new[:, u, :], src[:, T:NT]).then_inc(loaded[u], 16)
                    sp.dma_start(buf[:, u], conv_buf[bass.ds(t, 1)].rearrange("o p s j -> (o p) s j")).then_inc(loaded[u], 16)
                    sp.dma_start(w[:, u, :], conv_w[:, bass.ds(t, 1), :].rearrange("p o j -> p (o j)")).then_inc(loaded[u], 16)
                if not first:
                    for u in (0, 1):
                        store(i - 1, u)

            seq(sp, N, body)
            for u in (0, 1):
                store(N // 2 - 1, u)
            for u in (0, 1):
                sp.wait_ge(stored[u], 16 * N)

        @block.gpsimd
        def _(pool):
            pool.memset(x[:, :, 0:3], 0.0).then_inc(zeroed, 1)

        @block.vector
        def _(dve):
            dve.wait_ge(zeroed, 1)

            def body(i, first, us):
                for u in us:
                    dve.wait_ge(loaded[u], 64 * (i + 1))
                    if not first:
                        dve.wait_ge(act_done[u], i)
                        dve.wait_ge(stored[u], 32 * i)
                    ws = [w[:, u, j:j + 1] for j in range(4)]
                    terms = [(x[:, u, j:j + T], buf[:, u, :, j] if j < 3 else new[:, u, :]) for j in range(4)]
                    a, b = y[:, u, 0:T], y[:, u, T:NT]
                    for j, (p, q) in enumerate(terms):
                        if j == 0:
                            dve.tensor_scalar(a, p, ws[0], None, ALU.mult).then_inc(chain[u], 1)
                            dve.tensor_scalar(b, q, ws[0], None, ALU.mult).then_inc(chain[u], 1)
                            continue
                        dve.wait_ge(chain[u], 7 * i + 2 * j)
                        done = chain[u] if j < 3 else y_done[u]
                        dve.scalar_tensor_tensor(a, p, ws[j], a, ALU.mult, ALU.add).then_inc(chain[u], 1)
                        dve.scalar_tensor_tensor(b, q, ws[j], b, ALU.mult, ALU.add).then_inc(done, 1)
                    dve.tensor_copy(tail[:, u, :, 0:2], buf[:, u, :, 1:3])
                    dve.tensor_copy(tail[:, u, :, 2], new[:, u, :]).then_inc(tail_done[u], 1)

            seq(dve, N, body)

        @block.scalar
        def _(act):
            def body(i, first, us):
                for u in us:
                    act.wait_ge(chain[u], 7 * i + 7)
                    act.wait_ge(y_done[u], i + 1)
                    if not first:
                        act.wait_ge(stored[u], 32 * i)
                    act.activation(o[:, u, :], y[:, u, :], AF.Silu).then_inc(act_done[u], 1)

            seq(act, N, body)


def gdn_norms(k, conv, tile0, scale):
    k.recycle()
    nc, ALU, AF, f32, ps = k.nc, k.ALU, k.AF, k.f32, k.ps
    N = GH
    with ExitStack() as ctx:
        def sb(name, shape):
            return ctx.enter_context(nc.sbuf_tensor(k.name(name), shape, f32))

        def sem(name):
            return [k.semaphore(k.name(f"{name}{u}")) for u in range(2)]

        x, sq, r, y = (sb(n, [128, 2, NT]) for n in ("l2_x", "l2_sq", "l2_r", "l2_y"))
        loaded, sq_done, ss_done, std_done, r_done, y_done, stored = (
            sem(n) for n in ("loaded", "sq", "ss", "std", "r", "y", "stored"))
        block = ctx.enter_context(nc.Block())

        @block.sync
        def _(sp):
            for t in range(N):
                u, i = t % 2, t // 2
                if t >= 2:
                    sp.wait_ge(y_done[u], i)
                sp.dma_start(x[:, u, :], conv[tile0 + t]).then_inc(loaded[u], 16)
            for t in range(N):
                u, i = t % 2, t // 2
                sp.wait_ge(y_done[u], i + 1)
                sp.dma_start(conv[tile0 + t], y[:, u, :]).then_inc(stored[u], 16)
            for u in range(2):
                sp.wait_ge(stored[u], 16 * (N // 2))

        @block.scalar
        def _(act):
            def square(t):
                u, i = t % 2, t // 2
                act.wait_ge(loaded[u], 16 * (i + 1))
                if t >= 2:
                    act.wait_ge(ss_done[u], i)
                act.activation(sq[:, u, :], x[:, u, :], AF.Square).then_inc(sq_done[u], 1)

            square(0)
            for t in range(N):
                u, i = t % 2, t // 2
                if t + 1 < N:
                    square(t + 1)
                act.wait_ge(ss_done[u], i + 1)
                if t >= 2:
                    act.wait_ge(y_done[u], i)
                act.activation(r[:, u, :].rearrange("p (c n) -> p c n", c=NCH), ps[:, 3 * u:3 * u + 3, 0:CH], AF.Sqrt,
                               bias=k.c("eps")).then_inc(std_done[u], 1)

        @block.tensor
        def _(pe):
            for t in range(N):
                u, i = t % 2, t // 2
                pe.wait_ge(sq_done[u], i + 1)
                if t >= 2:
                    pe.wait_ge(std_done[u], i)
                for c in range(NCH):
                    last = pe.matmul(ps[:, 3 * u + c, 0:CH], k.c("ones"), sq[:, u, c * CH:c * CH + CH], start=True,
                                     stop=True)
                last.then_inc(ss_done[u], 1)

        @block.vector
        def _(dve):
            for t in range(N):
                u, i = t % 2, t // 2
                dve.wait_ge(std_done[u], i + 1)
                dve.reciprocal(r[:, u, :], r[:, u, :]).then_inc(r_done[u], 1)
                dve.wait_ge(r_done[u], i + 1)
                if t >= 2:
                    dve.wait_ge(stored[u], 16 * i)
                dve.scalar_tensor_tensor(y[:, u, :], x[:, u, :], scale, r[:, u, :], ALU.mult,
                                         ALU.mult).then_inc(y_done[u], 1)


def gdn(k, ab, conv, og, gains, a_log, dt_bias, state_in, state_p, state_s):
    nc, ALU, AF, f32, ps = k.nc, k.ALU, k.AF, k.f32, k.ps
    NG = NCK * GH
    NP = 2 * GH
    with ExitStack() as ctx:
        def sb(name, shape):
            return ctx.enter_context(nc.sbuf_tensor(k.name(name), shape, f32))

        beta = sb("beta", [128, NCK + 1, GH])
        cols = sb("cols", [128, 4, NG])
        gs = sb("gs", [128, 2, GH * S])
        w_all, u_all, attn_all, qe_all, kd_all = (sb(n, [128, NG, 128]) for n in ("w", "u", "attn", "qe", "kd"))
        gc_rows = sb("gc_rows", [128, NG, 128])
        gdn_gates(k, ab, a_log, dt_bias, beta, cols, gs, gc_rows)
        gdn_inverse(k, conv, beta, cols, gc_rows, w_all, u_all, attn_all, qe_all, kd_all)
        gdn_states(k, conv, og, gains, ab, cols, gs, state_in, state_p, state_s, w_all, u_all, attn_all, qe_all,
                   kd_all)


def gdn_gates(k, ab, a_log, dt_bias, beta, cols, gs, gc_rows):
    k.recycle()
    nc, ALU, AF, f32, ps = k.nc, k.ALU, k.AF, k.f32, k.ps
    NG, NTT = NCK * GH, NCK + 1
    with ExitStack() as ctx:
        def sb(name, shape):
            return ctx.enter_context(nc.sbuf_tensor(k.name(name), shape, f32))

        def sem(name):
            return k.semaphore(k.name(name))

        raw = sb("gates_raw", [8, NT])
        al, db = sb("a_log_rows", [128, GH]), sb("dt_rows", [128, GH])
        gt = sb("gates", [128, NTT, 8])
        x, e, u, ln_u, rest, ru, g = (sb(n, [128, NTT, GH]) for n in ("sx", "se", "su", "sl", "sd", "sr", "sg"))
        eg_s = sb("eg_s", [S, GH])
        last_less = sb("last_less", [128, NG])
        sel = sb("sel", [S, 2, GH, S])
        (loaded, zeroed, transposed, gt_done, x_done, clip_done, e_done, u_done, ru_done, rest_done, rest2_done,
         ln_done, log1p_done, sp_done, al_done, g_done, sums_done, row_done, row_copied, c0_done, c1_done, c2_done,
         c3_done, c1b_done, beta_done, eg_done, sel_done, sel_sum, gs_done) = (
            sem(n) for n in ("loaded", "zeroed", "transposed", "gt", "x", "clip", "e", "u", "ru", "rest", "rest2",
                             "ln", "log1p", "sp", "al", "g", "sums", "row", "row_copied", "c0", "c1", "c2", "c3",
                             "c1b", "beta", "eg", "sel", "sel_sum", "gs"))
        block = ctx.enter_context(nc.Block())
        rows = lambda v: v[:, None, :].broadcast_to((128, NTT, GH))
        flat = lambda v: v[:, 0:NCK, :].rearrange("p t h -> p (t h)")

        @block.sync
        def _(sp):
            sp.dma_start(raw[:, :], ab[AB_GATES][0:8, :]).then_inc(loaded, 16)
            sp.dma_start(al[:, :], a_log.broadcast_to((128, GH))).then_inc(loaded, 16)
            sp.dma_start(db[:, :], dt_bias.broadcast_to((128, GH))).then_inc(loaded, 16)

        @block.gpsimd
        def _(pool):
            pool.memset(gt[:, NCK, :], 0.0).then_inc(zeroed, 1)

        @block.tensor
        def _(pe):
            pe.wait_ge(loaded, 48)
            for t in range(NTT):
                n = min(128, NT - 128 * t)
                last = pe.transpose(ps[0:n, 0, 8 * t:8 * t + 8], raw[:, 128 * t:128 * t + n], k.c("ident")[0:8, 0:8])
            last.then_inc(transposed, 1)
            pe.wait_ge(g_done, 1)
            pe.matmul(ps[:, 1, 0:NG], k.c("tri"), flat(g), start=True, stop=True)
            pe.matmul(ps[:, 2, 0:NG], k.c("ones"), flat(g), start=True, stop=True).then_inc(sums_done, 1)
            for n in range(NG):
                if n >= 16 and n % 4 == 0:
                    pe.wait_ge(row_copied, n // 4 - 3)
                last = pe.matmul(ps[:, 4 + n // 4 % 4, n % 4 * 128:n % 4 * 128 + 128],
                                 g[:, n // GH, n % GH:n % GH + 1].broadcast_to((128, 128)), k.c("tri"),
                                 start=True, stop=True)
                if n % 4 == 3:
                    last.then_inc(row_done, 1)
            pe.wait_ge(sel_done, 2)
            pe.matmul(ps[:, 3, 0:2 * GH * S], k.c("ones")[0:S, :], sel[:, :, :, :].rearrange("s a h t -> s (a h t)"),
                      start=True, stop=True).then_inc(sel_sum, 1)

        @block.vector
        def _(dve):
            dve.wait_ge(transposed, 1)
            dve.wait_ge(zeroed, 1)
            dve.tensor_copy(gt[:, 0:NCK, :], ps[:, 0, 0:8 * NCK].rearrange("p (t h) -> p t h", h=8)).then_inc(gt_done, 1)
            dve.tensor_copy(gt[0:S, NCK, :], ps[0:S, 0, 8 * NCK:8 * NCK + 8]).then_inc(gt_done, 1)
            dve.wait_ge(gt_done, 2)
            dve.tensor_tensor(x[:, :, :], gt[:, :, 0:GH], rows(db), ALU.add).then_inc(x_done, 1)
            dve.wait_ge(x_done, 1)
            dve.tensor_scalar(e[:, :, :], x[:, :, :], CLIP, None, ALU.min).then_inc(clip_done, 1)
            dve.wait_ge(e_done, 1)
            dve.tensor_scalar(u[:, :, :], e[:, :, :], 1.0, None, ALU.add).then_inc(u_done, 1)
            dve.wait_ge(u_done, 1)
            dve.scalar_tensor_tensor(rest[:, :, :], u[:, :, :], -1.0, e[:, :, :], ALU.add, ALU.subtract).then_inc(rest_done, 1)
            dve.reciprocal(ru[:, :, :], u[:, :, :]).then_inc(ru_done, 1)
            dve.wait_ge(rest_done, 1)
            dve.wait_ge(ru_done, 1)
            dve.tensor_tensor(rest[:, :, :], rest[:, :, :], ru[:, :, :], ALU.mult).then_inc(rest2_done, 1)
            dve.wait_ge(rest2_done, 1)
            dve.wait_ge(ln_done, 1)
            dve.tensor_tensor(ln_u[:, :, :], ln_u[:, :, :], rest[:, :, :], ALU.subtract).then_inc(log1p_done, 1)
            dve.wait_ge(log1p_done, 1)
            dve.tensor_tensor(x[:, :, :], x[:, :, :], ln_u[:, :, :], ALU.max).then_inc(sp_done, 1)
            dve.wait_ge(sp_done, 1)
            dve.wait_ge(al_done, 1)
            dve.scalar_tensor_tensor(g[:, :, :], x[:, :, :], -1.0, rows(al), ALU.mult, ALU.mult).then_inc(g_done, 1)
            dve.wait_ge(sums_done, 1)
            dve.tensor_copy(cols[:, 0, :], ps[:, 1, 0:NG]).then_inc(c0_done, 1)
            dve.wait_ge(c0_done, 1)
            dve.tensor_tensor(last_less[:, :], ps[:, 2, 0:NG], cols[:, 0, :], ALU.subtract).then_inc(c2_done, 1)
            dve.wait_ge(eg_done, 1)
            dve.wait_ge(beta_done, 1)
            eye = k.c("ident")[0:S, None, 0:S].broadcast_to((S, GH, S))
            dve.tensor_tensor(sel[:, 0], eye, eg_s[:, :, None].broadcast_to((S, GH, S)), ALU.mult).then_inc(sel_done, 1)
            dve.tensor_tensor(sel[:, 1], eye, beta[0:S, NCK, :, None].broadcast_to((S, GH, S)),
                              ALU.mult).then_inc(sel_done, 1)
            dve.wait_ge(c1_done, 1)
            dve.tensor_tensor(cols[:, 1, :], cols[:, 1, :], flat(beta), ALU.mult).then_inc(c1b_done, 1)
            dve.wait_ge(sel_sum, 1)
            dve.tensor_copy(gs[:, :, :], ps[:, 3, 0:2 * GH * S].rearrange("p (a n) -> p a n", a=2)).then_inc(gs_done, 1)

        @block.scalar
        def _(act):
            act.wait_ge(loaded, 48)
            act.activation(al[:, :], al[:, :], AF.Exp).then_inc(al_done, 1)
            act.wait_ge(clip_done, 1)
            act.activation(e[:, :, :], e[:, :, :], AF.Exp).then_inc(e_done, 1)
            act.wait_ge(u_done, 1)
            act.activation(ln_u[:, :, :], u[:, :, :], AF.Ln).then_inc(ln_done, 1)
            act.wait_ge(gt_done, 2)
            act.activation(beta[:, :, :], gt[:, :, GH:8], AF.Sigmoid).then_inc(beta_done, 1)
            act.wait_ge(g_done, 1)
            act.activation(eg_s[:, :], g[0:S, NCK, :], AF.Exp).then_inc(eg_done, 1)
            act.wait_ge(c0_done, 1)
            act.activation(cols[:, 1, :], cols[:, 0, :], AF.Exp).then_inc(c1_done, 1)
            act.wait_ge(c2_done, 1)
            act.activation(cols[:, 2, :], last_less[:, :], AF.Exp).then_inc(c3_done, 1)
            act.activation(cols[:, 3, :], ps[:, 2, 0:NG], AF.Exp).then_inc(c3_done, 1)
            for n in range(NG // 4):
                act.wait_ge(row_done, n + 1)
                act.copy(gc_rows[:, 4 * n:4 * n + 4, :].rearrange("p a n -> p (a n)"),
                         ps[:, 4 + n % 4, :]).then_inc(row_copied, 1)


def gdn_inverse(k, conv, beta, cols, gc_rows, w_all, u_all, attn_all, qe_all, kd_all):
    k.recycle()
    nc, ALU, AF, f32, ps = k.nc, k.ALU, k.AF, k.f32, k.ps
    NP = 2 * GH
    LEVELS = 7
    with ExitStack() as ctx:
        def sb(name, shape):
            return ctx.enter_context(nc.sbuf_tensor(k.name(name), shape, f32))

        def sem(name):
            return k.semaphore(k.name(name))

        q, kk, v = (sb(n, [128, GH, 2 * CHUNK]) for n in ("gq", "gk", "gv"))
        col = sb("gcol", [128, 4, NP])
        dec = sb("decay", [128, NP, 128])
        a0, t_, tt, m1 = (sb(n, [128, NP, 128]) for n in ("a0", "t", "tt", "m1"))
        bm = sb("beta_mask", [128, 2, NP, 128])
        kbe, vb = sb("kbe", [128, NP, 128]), sb("vb", [128, NP, 128])
        loaded, col_done, diff_done, clip_done, exp_done, dec_done = (
            sem(n) for n in ("loaded", "col", "diff", "clip", "exp", "dec"))
        kk_done, qk_done, a0_done, attn_done = sem("kk"), sem("qk"), sem("a0d"), sem("attn")
        bm_done, p1_done, m1_done, p2_done, p3_done, t_done, tt_done = (
            sem(n) for n in ("bm", "p1", "m1d", "p2", "p3", "td", "ttd"))
        kt_done, vt_done, kbe_done, kd_done, vb_done, w_done, u_done, wc_done, uc_done, er_done, qe_done = (
            sem(n) for n in ("kt", "vt", "kbed", "kd", "vbd", "w", "u", "wc", "uc", "er", "qe"))

        def prob(x, j):
            return x[:, j % GH, (j // GH) * CHUNK:(j // GH + 1) * CHUNK]

        def pairs(x):
            return x[:, :, :].rearrange("p h (c n) -> p c h n", c=2)

        def four(x):
            return x.rearrange("p (c h) n -> p c h n", c=2)

        def bank(b, j):
            return ps[:, 2 * b + j // 4, j % 4 * 128:j % 4 * 128 + 128]

        def banks(b):
            return ps[:, 2 * b:2 * b + 2, :].rearrange("p b (h n) -> p (b h) n", n=128)

        def bc(c):
            return c[:, :, None].broadcast_to((128, NP, 128))

        def mask(m):
            return m[:, None, :].broadcast_to((128, NP, 128))

        level = [k.c("levels")[:, 128 * n:128 * n + 128] for n in range(LEVELS)]
        block = ctx.enter_context(nc.Block())

        @block.sync
        def _(sp):
            def body(i, first):
                tokens = bass.ds(2 * CHUNK * i if first else sp.snap(2 * CHUNK * i), 2 * CHUNK)
                if not first:
                    sp.wait_ge(vb_done, i)
                    sp.wait_ge(qe_done, i)
                    sp.wait_ge(kd_done, i)
                for j, dst in enumerate((q, kk, v)):
                    sp.dma_start(dst[:, :, :], conv[GH * j:GH * j + GH, :, tokens]
                                 .rearrange("h p n -> p h n")).then_inc(loaded, 16)

            loop(sp, NCK // 2, body)

        @block.vector
        def _(dve):
            def body(i, first):
                span = bass.ds(NP * i, NP)
                if not first:
                    dve.wait_ge(wc_done, i)
                    dve.wait_ge(uc_done, i)
                dve.tensor_copy(col[:, 0:3, :], cols[:, 0:3, span]).then_inc(col_done, 1)
                dve.tensor_copy(col[:, 3, :], beta[:, bass.ds(2 * i, 2), :].rearrange("p c h -> p (c h)")).then_inc(col_done, 1)
                dve.wait_ge(col_done, 2 * i + 2)
                dve.tensor_tensor(dec[:, :, :], gc_rows[:, span, :], bc(col[:, 0, :]), ALU.subtract).then_inc(diff_done, 1)
                dve.wait_ge(diff_done, i + 1)
                dve.tensor_scalar(dec[:, :, :], dec[:, :, :], 0.0, None, ALU.min).then_inc(clip_done, 1)
                dve.wait_ge(exp_done, i + 1)
                dve.tensor_tensor(dec[:, :, :], dec[:, :, :], mask(k.c("tri")), ALU.mult).then_inc(dec_done, 1)
                dve.wait_ge(dec_done, i + 1)
                dve.wait_ge(kk_done, i + 1)
                dve.tensor_tensor(a0[:, :, :], banks(0), dec[:, :, :], ALU.mult).then_inc(a0_done, 1)
                dve.wait_ge(qk_done, i + 1)
                dve.tensor_tensor(attn_all[:, span, :], banks(1), dec[:, :, :], ALU.mult).then_inc(attn_done, 1)
                dve.wait_ge(er_done, i + 1)
                dve.tensor_tensor(four(qe_all[:, span, :]), pairs(q), four(m1[:, :, :]), ALU.mult).then_inc(qe_done, 1)
                dve.wait_ge(kt_done, i + 1)
                dve.tensor_tensor(kbe[:, :, :], banks(2), bc(col[:, 1, :]), ALU.mult).then_inc(kbe_done, 1)
                dve.tensor_tensor(kd_all[:, span, :], banks(2), bc(col[:, 2, :]), ALU.mult).then_inc(kd_done, 1)
                dve.wait_ge(vt_done, i + 1)
                dve.tensor_tensor(vb[:, :, :], banks(3), bc(col[:, 3, :]), ALU.mult).then_inc(vb_done, 1)
                dve.wait_ge(qe_done, i + 1)
                for n in range(LEVELS):
                    dve.wait_ge(p1_done, LEVELS * i + n + 1)
                    dve.wait_ge(bm_done, LEVELS * i + n + 1)
                    dve.tensor_tensor(m1[:, :, :], banks(0), bm[:, n % 2], ALU.mult).then_inc(m1_done, 1)
                    if n < LEVELS - 1:
                        if n == 0:
                            dve.wait_ge(m1_done, LEVELS * i + 1)
                            dve.tensor_tensor(t_[:, :, :], mask(k.c("ident")), m1[:, :, :], ALU.subtract).then_inc(t_done, 1)
                        else:
                            dve.wait_ge(p2_done, (LEVELS - 2) * i + n)
                            dve.wait_ge(t_done, (LEVELS - 1) * i + n)
                            dve.tensor_tensor(t_[:, :, :], t_[:, :, :], banks(1), ALU.subtract).then_inc(t_done, 1)
                    dve.wait_ge(p3_done, LEVELS * i + n + 1)
                    if n == 0:
                        dve.tensor_tensor(tt[:, :, :], mask(k.c("ident")), banks(2), ALU.subtract).then_inc(tt_done, 1)
                    else:
                        dve.wait_ge(tt_done, LEVELS * i + n)
                        dve.tensor_tensor(tt[:, :, :], tt[:, :, :], banks(2), ALU.subtract).then_inc(tt_done, 1)

            loop(dve, NCK // 2, body)

        @block.gpsimd
        def _(pool):
            def body(i, first):
                pool.wait_ge(col_done, 2 * i + 2)
                for n in range(LEVELS):
                    if n >= 2 or not first:
                        pool.wait_ge(m1_done, LEVELS * i + n - 1)
                    pool.tensor_tensor(bm[:, n % 2], mask(level[n]), bc(col[:, 3, :]), ALU.mult).then_inc(bm_done, 1)

            loop(pool, NCK // 2, body)

        @block.scalar
        def _(act):
            def body(i, first):
                span = bass.ds(NP * i, NP)
                act.wait_ge(clip_done, i + 1)
                act.activation(dec[:, :, :], dec[:, :, :], AF.Exp).then_inc(exp_done, 1)
                act.activation(m1[:, :, :], gc_rows[:, span, :], AF.Exp).then_inc(er_done, 1)
                act.wait_ge(w_done, i + 1)
                act.copy(w_all[:, span, :], banks(3)).then_inc(wc_done, 1)
                act.wait_ge(u_done, i + 1)
                act.copy(u_all[:, span, :], banks(0)).then_inc(uc_done, 1)

            loop(act, NCK // 2, body)

        @block.tensor
        def _(pe):
            def eight(b, lhs, rhs, done, transpose=False):
                for j in range(NP):
                    if transpose:
                        last = pe.transpose(bank(b, j), lhs(j), k.c("ident"))
                    else:
                        last = pe.matmul(bank(b, j), lhs(j), rhs(j), start=True, stop=True)
                last.then_inc(done, 1)

            def body(i, first):
                of = lambda x: (lambda j: x[:, j, :])
                inp = lambda x: (lambda j: prob(x, j))
                eye = lambda j: k.c("ident")
                pe.wait_ge(loaded, 48 * (i + 1))
                if not first:
                    pe.wait_ge(uc_done, i)
                    pe.wait_ge(wc_done, i)
                eight(0, inp(kk), inp(kk), kk_done)
                eight(1, inp(kk), inp(q), qk_done)
                eight(2, inp(kk), None, kt_done, True)
                eight(3, inp(v), None, vt_done, True)
                pe.wait_ge(a0_done, i + 1)
                for n in range(LEVELS):
                    if n >= 1:
                        pe.wait_ge(t_done, (LEVELS - 1) * i + n)
                    eight(0, of(a0), eye if n == 0 else of(t_), p1_done)
                    pe.wait_ge(m1_done, LEVELS * i + n + 1)
                    if n >= 1:
                        pe.wait_ge(tt_done, LEVELS * i + n)
                        if n < LEVELS - 1:
                            if n == 1:
                                pe.wait_ge(attn_done, i + 1)
                            eight(1, of(tt), of(m1), p2_done)
                    if n == 0:
                        pe.wait_ge(kd_done, i + 1)
                        pe.wait_ge(kbe_done, i + 1)
                    eight(2, of(m1), eye if n == 0 else of(tt), p3_done)
                pe.wait_ge(tt_done, LEVELS * (i + 1))
                pe.wait_ge(vb_done, i + 1)
                eight(3, of(kbe), of(tt), w_done)
                eight(0, of(tt), of(vb), u_done)

            loop(pe, NCK // 2, body)


def gdn_states(k, conv, og, gains, ab, cols, gs, state_in, state_p, state_s, w_all, u_all, attn_all, qe_all, kd_all):
    k.recycle()
    nc, ALU, AF, f32, ps = k.nc, k.ALU, k.AF, k.f32, k.ps
    NS = GH * S
    with ExitStack() as outer:
        o_all = outer.enter_context(nc.sbuf_tensor(k.name("gdn_o"), [128, GH, NT], f32))
        with ExitStack() as ctx:
            def sb(name, shape):
                return ctx.enter_context(nc.sbuf_tensor(k.name(name), shape, f32))

            def sem(name):
                return k.semaphore(k.name(name))

            s = sb("state", [128, 2, GH, 128])
            se = sb("state_decayed", [128, GH, 128])
            vn = sb("v_new", [128, 2, GH, 128])
            s_done, ws_done, vn_done, ds_done, se_done, o_done, o_copied, stored = (
                sem(n) for n in ("s", "ws", "vn", "ds", "se", "o", "oc", "stored"))
            block = ctx.enter_context(nc.Block())

            @block.tensor
            def _(pe):
                for c in range(NCK):
                    pe.wait_ge(s_done, c + 1)
                    for h in range(GH):
                        last = pe.matmul(ps[:, 0, 128 * h:128 * h + 128], w_all[:, GH * c + h, :], s[:, c % 2, h, :],
                                         start=True, stop=True)
                    last.then_inc(ws_done, 1)
                    pe.wait_ge(vn_done, c + 1)
                    for h in range(GH):
                        last = pe.matmul(ps[:, 3, 128 * h:128 * h + 128], kd_all[:, GH * c + h, :], vn[:, c % 2, h, :],
                                         start=True, stop=True)
                    last.then_inc(ds_done, 1)
                    if c >= 2:
                        pe.wait_ge(o_copied, c - 1)
                    for h in range(GH):
                        o = ps[:, 1 + c % 2, 128 * h:128 * h + 128]
                        pe.matmul(o, s[:, c % 2, h, :], qe_all[:, GH * c + h, :], start=True, stop=False)
                        last = pe.matmul(o, vn[:, c % 2, h, :], attn_all[:, GH * c + h, :], start=False, stop=True)
                    last.then_inc(o_done, 1)

            @block.vector
            def _(dve):
                dve.memset(s[:, 0], 0.0).then_inc(s_done, 1)
                for c in range(NCK):
                    dve.wait_ge(ws_done, c + 1)
                    if c >= 2:
                        dve.wait_ge(o_done, c - 1)
                    dve.tensor_tensor(vn[:, c % 2], u_all[:, GH * c:GH * c + GH, :],
                                      ps[:, 0, :].rearrange("p (h n) -> p h n", h=GH), ALU.subtract).then_inc(vn_done, 1)
                    dve.wait_ge(ds_done, c + 1)
                    dve.wait_ge(se_done, c + 1)
                    if c >= 1:
                        dve.wait_ge(o_done, c)
                    dve.tensor_tensor(s[:, (c + 1) % 2], se[:, :, :], ps[:, 3, :].rearrange("p (h n) -> p h n", h=GH),
                                      ALU.add).then_inc(s_done, 1)

            @block.gpsimd
            def _(pool):
                for c in range(NCK):
                    pool.wait_ge(s_done, c + 1)
                    pool.tensor_tensor(se[:, :, :], s[:, c % 2],
                                       cols[:, 3, GH * c:GH * c + GH, None].broadcast_to((128, GH, 128)),
                                       ALU.mult).then_inc(se_done, 1)

            @block.scalar
            def _(act):
                for c in range(NCK):
                    act.wait_ge(o_done, c + 1)
                    act.copy(o_all[:, :, 128 * c:128 * c + 128],
                             ps[:, 1 + c % 2, :].rearrange("p (h n) -> p h n", h=GH)).then_inc(o_copied, 1)

            @block.sync
            def _(sp):
                sp.wait_ge(s_done, NCK + 1)
                sp.dma_start(state_p, s[:, NCK % 2]).then_inc(stored, 16)
                sp.wait_ge(stored, 16)

        with ExitStack() as ctx:
            def sb(name, shape):
                return ctx.enter_context(nc.sbuf_tensor(k.name(name), shape, f32))

            def sem(name):
                return k.semaphore(k.name(name))

            st = sb("sample_states", [128, NS, 128])
            qkv = sb("sample_qkv", [128, 12, S])
            vn = sb("sample_v_new", [128, NS])
            loaded, ks_done, dec_done, m_done, d_done, vn_done, rows_done, st_done, o_done, oc_done, stored = (
                sem(n) for n in ("loaded", "ks", "dec", "m", "d", "vn", "rows", "st", "o", "oc", "stored"))
            block = ctx.enter_context(nc.Block())

            @block.sync
            def _(sp):
                for h in range(GH):
                    sp.dma_start(st[:, h * S:h * S + S, :], state_in[:, h].rearrange("s p n -> p s n")).then_inc(loaded, 16)
                sp.dma_start(qkv[:, :, :], conv[:, :, T:NT].rearrange("t p n -> p t n")).then_inc(loaded, 16)
                for h in range(GH):
                    sp.wait_ge(st_done, S * h + S)
                    sp.dma_start(state_s[:, h].rearrange("s p n -> p s n"), st[:, h * S:h * S + S, :]).then_inc(stored, 16)
                sp.wait_ge(stored, 16 * GH)

            @block.tensor
            def _(pe):
                pe.wait_ge(loaded, 80)
                for n in range(NS):
                    last = pe.matmul(ps[:, 0, n:n + 1], st[:, n, :], qkv[:, GH + n // S, n % S:n % S + 1],
                                     start=True, stop=True)
                last.then_inc(ks_done, 1)
                pe.wait_ge(vn_done, 1)
                for n in range(NS):
                    b = 2 + n // 4 % 4
                    if n >= 16 and n % 4 == 0:
                        pe.wait_ge(st_done, n - 12)
                    last = pe.matmul(ps[:, b, n % 4 * 128:n % 4 * 128 + 128], vn[:, n:n + 1].broadcast_to((128, 128)),
                                     k.c("ident"), start=True, stop=True)
                    if n % 4 == 3:
                        last.then_inc(rows_done, 1)
                pe.wait_ge(st_done, NS)
                for n in range(NS):
                    last = pe.matmul(ps[:, 1, n:n + 1], st[:, n, :], qkv[:, n // S, n % S:n % S + 1],
                                     start=True, stop=True)
                last.then_inc(o_done, 1)

            @block.vector
            def _(dve):
                dve.wait_ge(ks_done, 1)
                dve.tensor_tensor(vn[:, :], ps[:, 0, 0:NS], gs[:, 0, :], ALU.mult).then_inc(m_done, 1)
                dve.wait_ge(m_done, 1)
                dve.tensor_tensor(vn[:, :], qkv[:, 2 * GH:3 * GH, :].rearrange("p h s -> p (h s)"), vn[:, :],
                                  ALU.subtract).then_inc(d_done, 1)
                dve.wait_ge(d_done, 1)
                dve.tensor_tensor(vn[:, :], vn[:, :], gs[:, 1, :], ALU.mult).then_inc(vn_done, 1)
                dve.tensor_tensor(st[:, :, :], st[:, :, :], gs[:, 0, :, None].broadcast_to((128, NS, 128)),
                                  ALU.mult).then_inc(dec_done, 1)
                dve.wait_ge(dec_done, 1)
                for n in range(NS):
                    dve.wait_ge(rows_done, n // 4 + 1)
                    dve.scalar_tensor_tensor(st[:, n, :], ps[:, 2 + n // 4 % 4, n % 4 * 128:n % 4 * 128 + 128],
                                             qkv[:, GH + n // S, n % S:n % S + 1], st[:, n, :], ALU.mult,
                                             ALU.add).then_inc(st_done, 1)

            @block.scalar
            def _(act):
                act.wait_ge(o_done, 1)
                act.copy(o_all[:, :, T:NT], ps[:, 1, 0:NS].rearrange("p (h s) -> p h s", h=GH)).then_inc(oc_done, 1)

        head_norms(k, o_all, GH, 1, gains, G_GDN, ab, AB_GZ, og, GH)


def head_norms(k, o, groups, subs, gains, g_col, gate, gate0, og, og0):
    k.recycle()
    nc, ALU, AF, f32, ps = k.nc, k.ALU, k.AF, k.f32, k.ps
    N = groups * subs
    with ExitStack() as ctx:
        def sb(name, shape):
            return ctx.enter_context(nc.sbuf_tensor(k.name(name), shape, f32))

        def sem(name):
            return k.semaphore(k.name(name))

        sq, y, z = sb("hn_sq", [128, 2, NT]), sb("hn_y", [128, 2, NT]), sb("hn_gate", [128, 2, NT])
        r = sb("hn_r", [128, 2, NT])
        sq_done, ss_done, std_done, r_done, n_done, y_done = (sem(n) for n in ("sq", "ss", "std", "r", "n", "y"))
        loaded, stored = [sem("ld0"), sem("ld1")], [sem("st0"), sem("st1")]
        block = ctx.enter_context(nc.Block())

        @block.sync
        def _(sp):
            def store(t):
                sp.wait_ge(y_done, t + 1)
                sp.dma_start(og[og0 + t], y[:, t % 2, :]).then_inc(stored[t % 2], 16)

            for t in range(N):
                if t >= 2:
                    sp.wait_ge(y_done, t - 1)
                sp.dma_start(z[:, t % 2, :], gate[gate0 + t]).then_inc(loaded[t % 2], 16)
                if t >= 2:
                    store(t - 2)
            store(N - 2)
            store(N - 1)
            for u in range(2):
                sp.wait_ge(stored[u], 16 * (N // 2))

        @block.scalar
        def _(act):
            def squares(g):
                for t in range(g * subs, (g + 1) * subs):
                    if t >= 2:
                        act.wait_ge(ss_done, t - 1)
                    act.activation(sq[:, t % 2, :], o[:, t, :], AF.Square).then_inc(sq_done, 1)

            squares(0)
            for g in range(groups):
                if g + 1 < groups:
                    squares(g + 1)
                act.wait_ge(ss_done, (g + 1) * subs)
                if g >= 2:
                    act.wait_ge(n_done, (g - 1) * subs)
                act.activation(r[:, g % 2, :].rearrange("p (c n) -> p c n", c=NCH), ps[:, 3 * (g % 2):3 * (g % 2) + 3, 0:CH],
                               AF.Sqrt, bias=k.c("eps"), scale=1.0 / (128 * subs)).then_inc(std_done, 1)

        @block.tensor
        def _(pe):
            for t in range(N):
                g, j = t // subs, t % subs
                pe.wait_ge(sq_done, t + 1)
                if g >= 2 and j == 0:
                    pe.wait_ge(std_done, g - 1)
                for c in range(NCH):
                    last = pe.matmul(ps[:, 3 * (g % 2) + c, 0:CH], k.c("ones"), sq[:, t % 2, c * CH:c * CH + CH],
                                     start=(j == 0), stop=(j == subs - 1))
                last.then_inc(ss_done, 1)

        @block.vector
        def _(dve):
            for t in range(N):
                g, j = t // subs, t % subs
                if j == 0:
                    dve.wait_ge(std_done, g + 1)
                    dve.reciprocal(r[:, g % 2, :], r[:, g % 2, :]).then_inc(r_done, 1)
                    dve.wait_ge(r_done, g + 1)
                if t >= 2:
                    dve.wait_ge(stored[t % 2], 16 * (t // 2))
                gc = g_col + j
                dve.scalar_tensor_tensor(y[:, t % 2, :], o[:, t, :], gains[:, gc:gc + 1], r[:, g % 2, :], ALU.mult,
                                         ALU.mult).then_inc(n_done, 1)
                dve.wait_ge(n_done, t + 1)
                dve.wait_ge(loaded[t % 2], 16 * (t // 2 + 1))
                dve.tensor_tensor(y[:, t % 2, :], y[:, t % 2, :], z[:, t % 2, :], ALU.mult).then_inc(y_done, 1)


def xa_prompt(k, xq, kv, kv0, og):
    k.recycle()
    nc, ALU, AF, f32, ps = k.nc, k.ALU, k.AF, k.f32, k.ps
    NB = T // 128
    MB = MEM // 128
    with ExitStack() as ctx:
        def sb(name, shape):
            return ctx.enter_context(nc.sbuf_tensor(k.name(name), shape, f32))

        def sem(name):
            return k.semaphore(k.name(name))

        q = sb("xa_q", [128, 2, T])
        kk, vt = sb("xa_k", [128, 2, MEM]), sb("xa_vt", [128, 2, MEM])
        v = sb("xa_v", [128, MB, XD])
        p = sb("xa_p", [128, NB, MEM])
        pt = sb("xa_pt", [128, MB, T])
        mx, nmx, sm, rs = (sb(n, [128, NB]) for n in ("xa_mx", "xa_nmx", "xa_sum", "xa_rs"))
        o = sb("xa_o", [128, 2, T])
        (loaded, vt_done, v_done, s_done, mx_done, nmx_done, e_done, rs_done, p_done, t_done, pt_done, o_done,
         oc_done, stored) = (sem(n) for n in ("loaded", "vt", "v", "s", "mx", "nmx", "e", "rs", "p", "t", "pt", "o",
                                              "oc", "stored"))
        block = ctx.enter_context(nc.Block())

        @block.sync
        def _(sp):
            def body(h, first):
                if not first:
                    sp.wait_ge(oc_done, 4 * h)
                for j in range(2):
                    sp.dma_start(q[:, j, :], dram_tile(xq, 2 * h + j)[:, 0:T]).then_inc(loaded, 16)
                    sp.dma_start(kk[:, j, :], dram_tile(kv, kv0 + 2 * h + j)).then_inc(loaded, 16)
                    sp.dma_start(vt[:, j, :], dram_tile(kv, kv0 + 8 + 2 * h + j)).then_inc(loaded, 16)
                sp.wait_ge(oc_done, 4 * h + 4)
                for j in range(2):
                    sp.dma_start(dram_tile(og, 2 * h + j)[:, 0:T], o[:, j, :]).then_inc(stored, 16)

            loop(sp, XH, body)
            sp.wait_ge(stored, 32 * XH)

        @block.tensor
        def _(pe):
            def body(h, first):
                pe.wait_ge(loaded, 96 * (h + 1))
                for m in range(MB):
                    for j in range(2):
                        last = pe.transpose(ps[:, 4, (2 * m + j) * 128:(2 * m + j) * 128 + 128],
                                            vt[:, j, 128 * m:128 * m + 128], k.c("ident"))
                last.then_inc(vt_done, 1)

                def scores(b):
                    if b >= 2:
                        pe.wait_ge(e_done, NB * h + b - 1)
                    for j in range(2):
                        last = pe.matmul(ps[:, b % 2, 0:MEM], q[:, j, 128 * b:128 * b + 128], kk[:, j, :],
                                         start=(j == 0), stop=(j == 1))
                    last.then_inc(s_done, 1)

                def transposes(b):
                    pe.wait_ge(p_done, NB * h + b + 1)
                    if b >= 2:
                        pe.wait_ge(pt_done, NB * h + b - 1)
                    for m in range(MB):
                        last = pe.transpose(ps[:, 2 + b % 2, 128 * m:128 * m + 128], p[:, b, 128 * m:128 * m + 128],
                                            k.c("ident"))
                    last.then_inc(t_done, 1)

                def outputs(c):
                    pe.wait_ge(pt_done, NB * h + 4 * c + 4)
                    for j in range(2):
                        for m in range(MB):
                            last = pe.matmul(ps[:, 4 + 2 * c + j, :], v[:, m, 128 * j:128 * j + 128],
                                             pt[:, m, 512 * c:512 * c + 512], start=(m == 0), stop=(m == MB - 1))
                        last.then_inc(o_done, 1)

                scores(0)
                scores(1)
                pe.wait_ge(v_done, h + 1)
                for b in range(NB):
                    transposes(b)
                    if b + 2 < NB:
                        scores(b + 2)
                    if b == 5:
                        outputs(0)
                outputs(1)

            loop(pe, XH, body)

        @block.vector
        def _(dve):
            def body(h, first):
                if not first:
                    dve.wait_ge(pt_done, NB * h)

                def maximum(b):
                    dve.wait_ge(s_done, NB * h + b + 1)
                    dve.tensor_reduce(mx[:, b:b + 1], ps[:, b % 2, 0:MEM], k.AX.X, ALU.max).then_inc(mx_done, 1)
                    dve.wait_ge(mx_done, NB * h + b + 1)
                    dve.tensor_scalar(nmx[:, b:b + 1], mx[:, b:b + 1], -XD ** -0.5, None, ALU.mult).then_inc(nmx_done, 1)

                maximum(0)
                maximum(1)
                for b in range(NB):
                    dve.wait_ge(e_done, NB * h + b + 1)
                    dve.reciprocal(rs[:, b:b + 1], sm[:, b:b + 1]).then_inc(rs_done, 1)
                    dve.wait_ge(rs_done, NB * h + b + 1)
                    dve.tensor_scalar(p[:, b, :], p[:, b, :], rs[:, b:b + 1], None, ALU.mult).then_inc(p_done, 1)
                    if b + 2 < NB:
                        maximum(b + 2)
                    if b >= 1:
                        copy_pt(h, b - 1)
                copy_pt(h, NB - 1)

            def copy_pt(h, b):
                dve.wait_ge(t_done, NB * h + b + 1)
                dve.tensor_copy(pt[:, :, 128 * b:128 * b + 128],
                                ps[:, 2 + b % 2, 0:MEM].rearrange("p (m n) -> p m n", m=MB)).then_inc(pt_done, 1)

            loop(dve, XH, body)

        @block.scalar
        def _(act):
            def body(h, first):
                act.wait_ge(vt_done, h + 1)
                act.copy(v[:, :, :].rearrange("p m d -> p (m d)"), ps[:, 4, :]).then_inc(v_done, 1)
                for b in range(NB):
                    act.wait_ge(nmx_done, NB * h + b + 1)
                    act.activation(p[:, b, :], ps[:, b % 2, 0:MEM], AF.Exp, bias=nmx[:, b:b + 1], scale=XD ** -0.5,
                                   accum_out=sm[:, b:b + 1]).then_inc(e_done, 1)
                    if b == 7:
                        outputs(h, 0, first)
                outputs(h, 1, first)

            def outputs(h, c, first):
                if c == 0 and not first:
                    act.wait_ge(stored, 32 * h)
                for j in range(2):
                    act.wait_ge(o_done, 4 * h + 2 * c + j + 1)
                    act.copy(o[:, j, 512 * c:512 * c + 512], ps[:, 4 + 2 * c + j, :]).then_inc(oc_done, 1)

            loop(act, XH, body)


def xa_sample(k, xq, mem_k, mem_v, s0, og):
    k.recycle()
    nc, ALU, AF, f32, ps = k.nc, k.ALU, k.AF, k.f32, k.ps
    MB = MEM // 128
    NR = S * XH
    with ExitStack() as ctx:
        def sb(name, shape):
            return ctx.enter_context(nc.sbuf_tensor(k.name(name), shape, f32))

        def sem(name):
            return k.semaphore(k.name(name))

        qs = sb("xs_q", [128, KT, S])
        qr = sb("xs_q_rows", [128, 2, D])
        kc, vc = sb("xs_k", [128, 2, MB, D]), sb("xs_v", [128, 2, MB, D])
        prod = sb("xs_prod", [128, MB, D])
        z = sb("xs_z", [128, MB, NR])
        zt = sb("xs_zt", [NR, MEM])
        mx, nmx, sm, rs = (sb(n, [NR, 1]) for n in ("xs_mx", "xs_nmx", "xs_sum", "xs_rs"))
        pt = sb("xs_pt", [128, MB, NR])
        om = sb("xs_masked", [XH, D])
        o = sb("xs_o", [128, KT, S])
        (q_in, qb_done, qr_done, prod_done, z_done, zt_done, mx_done, nmx_done, e_done, rs_done, p_done, t_done,
         pt_done, pv_done, om_done, col_done, o_done, stored) = (
            sem(n) for n in ("q_in", "qb", "qr", "prod", "z", "ztd", "mx", "nmx", "e", "rs", "p", "t", "ptd", "pv",
                             "om", "col", "o", "stored"))
        k_in, v_in = [sem("k0"), sem("k1")], [sem("v0"), sem("v1")]
        block = ctx.enter_context(nc.Block())

        @block.sync
        def _(sp):
            sp.dma_start(qs[:, :, :], xq[:, :, T:NT].rearrange("t p n -> p t n")).then_inc(q_in, 16)
            for s in range(S):
                if s >= 2:
                    sp.wait_ge(prod_done, s - 1)
                sp.dma_start(kc[:, s % 2], mem_k[s0 + s].rearrange("(b p) n -> p b n", p=128)).then_inc(k_in[s % 2], 16)
            for s in range(S):
                if s >= 2:
                    sp.wait_ge(pv_done, s - 1)
                sp.dma_start(vc[:, s % 2], mem_v[s0 + s].rearrange("(b p) n -> p b n", p=128)).then_inc(v_in[s % 2], 16)
            sp.wait_ge(o_done, S)
            sp.dma_start(og[0:KT, :, T:NT].rearrange("t p n -> p t n"), o[:, :, :]).then_inc(stored, 16)
            sp.wait_ge(stored, 16)

        @block.tensor
        def _(pe):
            pe.wait_ge(q_in, 16)
            for s in range(S):
                if s >= 2:
                    pe.wait_ge(qr_done, s - 1)
                for f in range(KT):
                    last = pe.matmul(ps[:, 2 * (s % 2) + f // 4, f % 4 * 128:f % 4 * 128 + 128],
                                     qs[:, f, s:s + 1].broadcast_to((128, 128)), k.c("ident"), start=True, stop=True)
                last.then_inc(qb_done, 1)
            pe.wait_ge(z_done, S)
            for m in range(MB):
                last = pe.transpose(ps[0:NR, 4, 128 * m:128 * m + 128], z[:, m, :], k.c("ident"))
            last.then_inc(zt_done, 1)
            pe.wait_ge(p_done, 1)
            for m in range(MB):
                last = pe.transpose(ps[:, 5, NR * m:NR * m + NR], zt[:, 128 * m:128 * m + 128],
                                    k.c("ident")[0:NR, 0:NR])
            last.then_inc(t_done, 1)
            pe.wait_ge(pt_done, 1)

            def columns(s):
                pe.wait_ge(om_done, s + 1)
                if s >= 1:
                    pe.wait_ge(o_done, s)
                for f in range(KT):
                    last = pe.matmul(ps[:, 6, f:f + 1], om[:, f * 128:f * 128 + 128], k.c("ones")[0:XH, 0:1],
                                     start=True, stop=True)
                last.then_inc(col_done, 1)

            for s in range(S):
                pe.wait_ge(v_in[s % 2], 16 * (s // 2 + 1))
                if s >= 2:
                    pe.wait_ge(om_done, s - 1)
                for c in range(2):
                    for m in range(MB):
                        last = pe.matmul(ps[0:XH, 2 * (s % 2) + c, :], pt[:, m, XH * s:XH * s + XH],
                                         vc[:, s % 2, m, 512 * c:512 * c + 512], start=(m == 0), stop=(m == MB - 1))
                last.then_inc(pv_done, 1)
                if s >= 1:
                    columns(s - 1)
            columns(S - 1)

        @block.scalar
        def _(act):
            for s in range(S):
                act.wait_ge(qb_done, s + 1)
                if s >= 2:
                    act.wait_ge(prod_done, s - 1)
                act.copy(qr[:, s % 2, :].rearrange("p (b n) -> p b n", b=2),
                         ps[:, 2 * (s % 2):2 * (s % 2) + 2, :]).then_inc(qr_done, 1)
            act.wait_ge(nmx_done, 1)
            act.activation(zt[:, :], ps[0:NR, 4, 0:MEM], AF.Exp, bias=nmx[:, :], scale=XD ** -0.5,
                           accum_out=sm[:, :]).then_inc(e_done, 1)
            act.wait_ge(t_done, 1)
            act.copy(pt[:, :, :].rearrange("p m n -> p (m n)"), ps[:, 5, 0:MB * NR]).then_inc(pt_done, 1)
            for s in range(S):
                act.wait_ge(col_done, s + 1)
                act.copy(o[:, :, s], ps[:, 6, 0:KT]).then_inc(o_done, 1)

        @block.vector
        def _(dve):
            for s in range(S):
                dve.wait_ge(k_in[s % 2], 16 * (s // 2 + 1))
                dve.wait_ge(qr_done, s + 1)
                if s >= 1:
                    dve.wait_ge(z_done, s)
                dve.tensor_tensor(prod[:, :, :], kc[:, s % 2], qr[:, s % 2, None, :].broadcast_to((128, MB, D)),
                                  ALU.mult).then_inc(prod_done, 1)
                dve.wait_ge(prod_done, s + 1)
                dve.tensor_reduce(z[:, :, XH * s:XH * s + XH], prod[:, :, :].rearrange("p m (h d) -> p m h d", h=XH),
                                  k.AX.X, ALU.add).then_inc(z_done, 1)
            dve.wait_ge(zt_done, 1)
            dve.tensor_reduce(mx[:, :], ps[0:NR, 4, 0:MEM], k.AX.X, ALU.max).then_inc(mx_done, 1)
            dve.wait_ge(mx_done, 1)
            dve.tensor_scalar(nmx[:, :], mx[:, :], -XD ** -0.5, None, ALU.mult).then_inc(nmx_done, 1)
            dve.wait_ge(e_done, 1)
            dve.reciprocal(rs[:, :], sm[:, :]).then_inc(rs_done, 1)
            dve.wait_ge(rs_done, 1)
            dve.tensor_scalar(zt[:, :], zt[:, :], rs[:, :], None, ALU.mult).then_inc(p_done, 1)
            for s in range(S):
                dve.wait_ge(pv_done, s + 1)
                if s >= 1:
                    dve.wait_ge(col_done, s)
                dve.tensor_tensor(om[:, :].rearrange("h (c n) -> h c n", c=2), ps[0:XH, 2 * (s % 2):2 * (s % 2) + 2, :],
                                  k.c("xa_diag")[0:XH, :].rearrange("h (c n) -> h c n", c=2), ALU.mult).then_inc(om_done, 1)


def retention(k, cc, og, gains, rope, ret_const, state_in, state_p, state_s):
    nc, f32 = k.nc, k.f32
    with ExitStack() as ctx:
        cs = ctx.enter_context(nc.sbuf_tensor(k.name("rope"), [128, 2, NT], f32))
        o = ctx.enter_context(nc.sbuf_tensor(k.name("ret_o"), [128, 4, NT], f32))
        for h in range(RH):
            with nc.sbuf_tensor(k.name("ret_q"), [128, 2, NT], f32) as q, \
                    nc.sbuf_tensor(k.name("ret_k"), [128, 2, NT], f32) as kk:
                rotary(k, cc, h, rope, cs, q, kk)
                retention_chunks(k, cc, h, ret_const, q, kk, o, state_p)
                retention_samples(k, cc, h, ret_const, q, kk, o, state_in, state_s)
            head_norms(k, o, 1, 4, gains, G_RET, cc, C_Z + 4 * h, og, 4 * h)


def rotary(k, cc, h, rope, cs, q, kk):
    k.recycle()
    nc, ALU, AF, f32 = k.nc, k.ALU, k.AF, k.f32
    with ExitStack() as ctx:
        def sb(name, shape):
            return ctx.enter_context(nc.sbuf_tensor(k.name(name), shape, f32))

        x = sb("rot_x", [128, 2, 2, NT])
        t = sb("rot_t", [128, 2, 4, NT])
        table = k.semaphore(k.name("table"))
        loaded = [k.semaphore(k.name(f"loaded{j}")) for j in range(2)]
        parts, done = k.semaphore(k.name("products")), k.semaphore(k.name("rotated"))
        block = ctx.enter_context(nc.Block())

        @block.sync
        def _(sp):
            if h == 0:
                sp.dma_start(cs[:, :, :], rope).then_inc(table, 16)
            for j, t0 in enumerate((C_Q, C_K)):
                sp.dma_start(x[:, j], cc[t0 + 2 * h:t0 + 2 * h + 2].rearrange("t p n -> p t n")).then_inc(loaded[j], 16)

        @block.vector
        def _(dve):
            if h == 0:
                dve.wait_ge(table, 16)
            for j, dst in enumerate((q, kk)):
                dve.wait_ge(loaded[j], 16)
                for n, (a, b) in enumerate(((0, 0), (1, 1), (1, 0), (0, 1))):
                    dve.tensor_tensor(t[:, j, n], x[:, j, a], cs[:, b, :], ALU.mult).then_inc(parts, 1)
                dve.wait_ge(parts, 4 * j + 4)
                dve.tensor_tensor(dst[:, 0, :], t[:, j, 0], t[:, j, 1], ALU.subtract).then_inc(done, 1)
                dve.tensor_tensor(dst[:, 1, :], t[:, j, 2], t[:, j, 3], ALU.add).then_inc(done, 1)


def retention_chunks(k, cc, h, ret_const, q, kk, o, state_p):
    k.recycle()
    nc, ALU, AF, f32, ps = k.nc, k.ALU, k.AF, k.f32, k.ps
    with ExitStack() as ctx:
        def sb(name, shape):
            return ctx.enter_context(nc.sbuf_tensor(k.name(name), shape, f32))

        def sem(name):
            return k.semaphore(k.name(name))

        rc = sb("ret_c", [128, RETC_W])
        vt = sb("ret_vt", [128, 2, 4, 128])
        v = sb("ret_v", [128, 2, 512])
        kz = sb("ret_kz", [128, 2, 2, 128])
        qx = sb("ret_qx", [128, 2, 2, 128])
        inner = sb("ret_inner", [128, 2, 128])
        s = sb("ret_s", [128, 2, 2, 512])
        c_in, v_in = sem("c_in"), [sem("v0"), sem("v1")]
        (i_done, in_done, kt_done, kz_done, vt_done, v_done, qx_done, o_done, oc_done, ds_done, s_done, stored) = (
            sem(n) for n in ("i", "inner", "kt", "kz", "vt", "v", "qx", "o", "oc", "ds", "s", "stored"))
        block = ctx.enter_context(nc.Block())

        @block.sync
        def _(sp):
            sp.dma_start(rc[:, :], ret_const[h]).then_inc(c_in, 16)
            for c in range(NCK):
                if c >= 2:
                    sp.wait_ge(vt_done, c - 1)
                sp.dma_start(vt[:, c % 2], cc[C_V + 4 * h:C_V + 4 * h + 4, :, CHUNK * c:CHUNK * c + CHUNK]
                             .rearrange("t p n -> p t n")).then_inc(v_in[c % 2], 16)
            sp.wait_ge(s_done, 2 * NCK + 1)
            sp.dma_start(state_p[h].rearrange("t p n -> p t n"), s[:, NCK % 2]).then_inc(stored, 16)
            sp.wait_ge(stored, 16)

        @block.tensor
        def _(pe):
            def prepare(c):
                a, b = CHUNK * c, CHUNK * c + CHUNK
                if c >= 1:
                    pe.wait_ge(in_done, c)
                    pe.wait_ge(kz_done, c)
                    pe.wait_ge(v_done, c)
                for t in range(2):
                    last = pe.matmul(ps[:, 0, 0:128], kk[:, t, a:b], q[:, t, a:b], start=(t == 0), stop=(t == 1))
                last.then_inc(i_done, 1)
                for t in range(2):
                    last = pe.transpose(ps[:, 1, 128 * t:128 * t + 128], kk[:, t, a:b], k.c("ident"))
                last.then_inc(kt_done, 1)
                pe.wait_ge(v_in[c % 2], 16 * (c // 2 + 1))
                for t in range(4):
                    last = pe.transpose(ps[:, 2, 128 * t:128 * t + 128], vt[:, c % 2, t, :], k.c("ident"))
                last.then_inc(vt_done, 1)

            prepare(0)
            for c in range(NCK):
                if c + 1 < NCK:
                    prepare(c + 1)
                pe.wait_ge(kz_done, c + 1)
                pe.wait_ge(v_done, c + 1)
                pe.wait_ge(s_done, 2 * c + 1)
                for t in range(2):
                    last = pe.matmul(ps[:, 5 + t, :], kz[:, c % 2, t, :], v[:, c % 2, :], start=True, stop=True)
                last.then_inc(ds_done, 1)
                pe.wait_ge(in_done, c + 1)
                pe.wait_ge(qx_done, c + 1)
                if c >= 2:
                    pe.wait_ge(oc_done, c - 1)
                for d in range(4):
                    out = ps[:, 3 + c % 2, 128 * d:128 * d + 128]
                    pe.matmul(out, v[:, c % 2, 128 * d:128 * d + 128], inner[:, c % 2, :], start=True, stop=False)
                    for t in range(2):
                        last = pe.matmul(out, s[:, c % 2, t, 128 * d:128 * d + 128], qx[:, c % 2, t, :], start=False,
                                         stop=(t == 1))
                last.then_inc(o_done, 1)

        @block.vector
        def _(dve):
            dve.memset(s[:, 0], 0.0).then_inc(s_done, 1)
            dve.wait_ge(c_in, 16)

            def prepare(c):
                a, b = CHUNK * c, CHUNK * c + CHUNK
                if c >= 2:
                    dve.wait_ge(o_done, c - 1)
                dve.tensor_tensor(qx[:, c % 2], q[:, :, a:b], rc[:, None, 128:256].broadcast_to((128, 2, 128)),
                                  ALU.mult).then_inc(qx_done, 1)
                dve.wait_ge(i_done, c + 1)
                dve.tensor_tensor(inner[:, c % 2], ps[:, 0, 0:128], rc[:, 0:128], ALU.mult).then_inc(in_done, 1)

            prepare(0)
            for c in range(NCK):
                if c + 1 < NCK:
                    prepare(c + 1)
                dve.wait_ge(ds_done, c + 1)
                if c >= 1:
                    dve.wait_ge(o_done, c)
                dve.wait_ge(s_done, 2 * c + 1)
                for t in range(2):
                    dve.scalar_tensor_tensor(s[:, (c + 1) % 2, t, :], s[:, c % 2, t, :], rc[:, 257:258],
                                             ps[:, 5 + t, :], ALU.mult, ALU.add).then_inc(s_done, 1)

        @block.scalar
        def _(act):
            act.wait_ge(c_in, 16)

            def prepare(c):
                if c >= 2:
                    act.wait_ge(o_done, c - 1)
                act.wait_ge(kt_done, c + 1)
                act.activation(kz[:, c % 2].rearrange("p t n -> p (t n)"), ps[:, 1, 0:256], AF.Copy,
                               scale=rc[:, 256:257]).then_inc(kz_done, 1)
                act.wait_ge(vt_done, c + 1)
                act.copy(v[:, c % 2, :], ps[:, 2, :]).then_inc(v_done, 1)

            prepare(0)
            for c in range(NCK):
                if c + 1 < NCK:
                    prepare(c + 1)
                act.wait_ge(o_done, c + 1)
                act.copy(o[:, :, CHUNK * c:CHUNK * c + CHUNK],
                         ps[:, 3 + c % 2, :].rearrange("p (d n) -> p d n", d=4)).then_inc(oc_done, 1)


def retention_samples(k, cc, h, ret_const, q, kk, o, state_in, state_s):
    k.recycle()
    nc, ALU, AF, f32, ps = k.nc, k.ALU, k.AF, k.f32, k.ps
    NSL = 4
    with ExitStack() as ctx:
        def sb(name, shape):
            return ctx.enter_context(nc.sbuf_tensor(k.name(name), shape, f32))

        def sem(name):
            return k.semaphore(k.name(name))

        rc = sb("rs_c", [128, 3])
        vs = sb("rs_v", [128, 4, S])
        ks = sb("rs_k", [128, 2, S])
        s = sb("rs_s", [128, NSL, 2, 512])
        g = sb("rs_g", [128, 2, 2, 512])
        c_in, ks_done, rows_done, g_done, s_done, o_done, oc_done = (
            sem(n) for n in ("c_in", "ks", "rows", "g", "s", "o", "oc"))
        s_in = [sem(f"s_in{j}") for j in range(NSL)]
        stored = [sem(f"st{j}") for j in range(NSL)]
        block = ctx.enter_context(nc.Block())

        @block.sync
        def _(sp):
            sp.dma_start(rc[:, :], ret_const[h][:, 256:259]).then_inc(c_in, 16)
            sp.dma_start(vs[:, :, :], cc[C_V + 4 * h:C_V + 4 * h + 4, :, T:NT].rearrange("t p n -> p t n")).then_inc(c_in, 16)

            def store(n):
                sp.wait_ge(s_done, 2 * n + 2)
                sp.dma_start(state_s[n, h].rearrange("t p n -> p t n"), g[:, n % 2]).then_inc(stored[n % 2], 16)

            for n in range(S):
                if n >= NSL:
                    sp.wait_ge(g_done, n - NSL + 1)
                sp.dma_start(s[:, n % NSL], state_in[n, h].rearrange("t p n -> p t n")).then_inc(s_in[n % NSL], 16)
                if n >= NSL:
                    store(n - NSL)
            for n in range(S - NSL, S):
                store(n)
            for j in range(2):
                sp.wait_ge(stored[j], 16 * (S // 2))

        @block.scalar
        def _(act):
            act.wait_ge(c_in, 32)
            for n in range(S):
                act.wait_ge(s_in[n % NSL], 16 * (n // NSL + 1))
                if n >= 2:
                    act.wait_ge(stored[n % 2], 16 * (n // 2))
                    act.wait_ge(o_done, n - 1)
                act.activation(g[:, n % 2], s[:, n % NSL], AF.Copy, scale=rc[:, 2:3]).then_inc(g_done, 1)
            act.wait_ge(o_done, S)
            act.copy(o[:, :, T:NT], ps[:, 2, 0:4 * S].rearrange("p (s d) -> p d s", d=4)).then_inc(oc_done, 1)

        @block.tensor
        def _(pe):
            pe.wait_ge(c_in, 32)

            def rows(n):
                if n >= 2:
                    pe.wait_ge(s_done, 2 * n - 2)
                for d in range(4):
                    last = pe.matmul(ps[:, n % 2, 128 * d:128 * d + 128], vs[:, d, n:n + 1].broadcast_to((128, 128)),
                                     k.c("ident"), start=True, stop=True)
                last.then_inc(rows_done, 1)

            rows(0)
            for n in range(S):
                if n + 1 < S:
                    rows(n + 1)
                pe.wait_ge(s_done, 2 * n + 2)
                for d in range(4):
                    for t in range(2):
                        last = pe.matmul(ps[:, 2, 4 * n + d:4 * n + d + 1], g[:, n % 2, t, 128 * d:128 * d + 128],
                                         q[:, t, T + n:T + n + 1], start=(t == 0), stop=(t == 1))
                last.then_inc(o_done, 1)

        @block.vector
        def _(dve):
            dve.tensor_scalar(ks[:, :, :], kk[:, :, T:NT], XD ** -0.5, None, ALU.mult).then_inc(ks_done, 1)
            dve.wait_ge(ks_done, 1)
            for n in range(S):
                dve.wait_ge(rows_done, n + 1)
                dve.wait_ge(g_done, n + 1)
                for t in range(2):
                    dve.scalar_tensor_tensor(g[:, n % 2, t, :], ps[:, n % 2, :], ks[:, t, n:n + 1], g[:, n % 2, t, :],
                                             ALU.mult, ALU.add).then_inc(s_done, 1)


INPUTS = ["x_t", "mem_t", "consts", "sb_mask", "rope", "ret_const", "w_ab", "w_oab", "w_c", "w_oc", "w_xq", "w_xo",
          "w_mem", "gains", "conv_w", "sb_bias", "a_log", "dt_bias", "page_table", "cache_k", "cache_v", "gdn_state",
          "gdn_conv", "ret_state", "mem_k", "mem_v"]
OUTPUTS = {
    "y_t": (KT, 128, NT), "sb_k_t": (4, 128, NT), "sb_v_t": (4, 128, NT),
    "gdn_p": (128, GH, 128), "gdn_s": (S, GH, 128, 128),
    "conv_p": (12, 128, 3), "conv_s": (12, 128, S, 3),
    "ret_p": (RH, 2, 128, 512), "ret_s": (S, RH, 2, 128, 512),
    "mem_kv_t": (32, 128, MEM),
}
G_MIX, G_XA, G_FINAL, G_GDN, G_RET, G_W = 0, 16, 32, 40, 41, 45


def trunk_program(nc, ins, outs, upto=99):
    k = Kit()
    k.nc, k.ALU, k.AF, k.AX = nc, mybir.AluOpType, mybir.ActivationFunctionType, mybir.AxisListType
    k.f32, k.f32r = mybir.dt.float32, mybir.dt.float32r
    f32 = k.f32
    count = [0]

    def name(x):
        count[0] += 1
        return f"{x}_{count[0]}"

    k.name = name
    with ExitStack() as ctx:
        def scratch(n, shape):
            return nc.dram_tensor(n, shape, f32, kind="Internal").ap()

        ab = scratch("ab", (AB_TILES, 128, NT))
        cc = scratch("cc", (C_TILES, 128, NT))
        og = scratch("og", (16, 128, NT))
        xq = scratch("xq", (KT, 128, NT))
        conv = scratch("conv", (12, 128, NT))
        k.ps = ctx.enter_context(nc.psum_tensor("ps", [128, 8, 512], f32))
        consts = ctx.enter_context(nc.sbuf_tensor("consts_sb", [128, CONST_W], f32))
        sb_mask = ctx.enter_context(nc.sbuf_tensor("sb_mask_sb", [128, 128], f32))
        gains = ctx.enter_context(nc.sbuf_tensor("gains_sb", [128, G_W], f32))
        k.sb_mask = sb_mask
        k.c = lambda n: consts[:, CONST[n][0]:CONST[n][1]]

        def load_residual(x, *more):
            with ExitStack() as stack:
                got = k.semaphore(name("residual_loaded"))
                block = stack.enter_context(nc.Block())

                @block.sync
                def _(sp):
                    for dst, src in ((x[:, :, :], ins["x_t"].rearrange("t p n -> p t n")), *more):
                        sp.dma_start(dst, src).then_inc(got, 16)
                    sp.wait_ge(got, 16 * (1 + len(more)))

        def halves(tokens):
            hi = nc.sbuf_tensor(name("in_hi"), [128, KT, tokens], k.f32r)
            lo = nc.sbuf_tensor(name("in_lo"), [128, KT, tokens], k.f32r)
            return hi, lo

        AF = k.AF
        (a, b), (c, d) = halves(NT), halves(MEM)
        with a as hi, b as lo, c as m_hi, d as m_lo:
            with nc.sbuf_tensor("layer0_in", [128, KT, NT], f32) as x:
                k.x = x
                load_residual(x, (consts[:, :], ins["consts"]), (sb_mask[:, :], ins["sb_mask"]),
                              (gains[:, :], ins["gains"]))
                norm(k, gains, G_MIX, hi, lo)
            load_split(k, ins["mem_t"], 0, m_hi, m_lo, MEM)
            linear(k, ins["w_ab"], 0, AB_V, hi, lo, NT, NCH, func=AF.Copy, out=ab)
            weave(k, ins["w_ab"], hi, lo, ab, ins["w_mem"], m_hi, m_lo, outs["mem_kv_t"], og, ins["cache_k"],
                  ins["cache_v"], ins["page_table"], ins["sb_bias"])
        x = ctx.enter_context(nc.sbuf_tensor("residual", [128, KT, NT], f32))
        k.x = x
        load_residual(x)
        copy_out(k, [(outs["sb_k_t"], ab[AB_K:AB_K + 4]), (outs["sb_v_t"], ab[AB_V:AB_V + 4]),
                     (outs["conv_p"], ab[AB_QKV:AB_QKV + 12, :, T - 3:T])])
        if upto < 2:
            return
        sb_prompt(k, ab, og, ins["sb_bias"])
        if upto < 4:
            return
        gdn_conv(k, ab, conv, ins["conv_w"], ins["gdn_conv"], outs["conv_s"])
        gdn_norms(k, conv, 0, GDN_SCALE)
        gdn_norms(k, conv, GH, 1.0)
        gdn(k, ab, conv, og, gains, ins["a_log"], ins["dt_bias"], ins["gdn_state"], outs["gdn_p"], outs["gdn_s"])
        if upto < 5:
            return

        def project_out(w, w0, tile0):
            a, b = halves(NT)
            with a as hi, b as lo:
                load_split(k, og, tile0, hi, lo, NT)
                linear(k, w, w0, KT, hi, lo, NT, NCH, resid=x)

        def cross_attention(layer):
            a, b = halves(NT)
            with a as hi, b as lo:
                norm(k, gains, G_XA + KT * layer, hi, lo)
                linear(k, ins["w_xq"], KT * layer, KT, hi, lo, NT, NCH, func=AF.Copy, out=xq)
            xa_prompt(k, xq, outs["mem_kv_t"], 16 * layer, og)
            xa_sample(k, xq, ins["mem_k"], ins["mem_v"], S * layer, og)
            project_out(ins["w_xo"], KT * layer, 0)

        project_out(ins["w_oab"], 0, 0)
        cross_attention(0)
        if upto < 6:
            return
        a, b = halves(NT)
        with a as hi, b as lo:
            norm(k, gains, G_MIX + KT, hi, lo)
            linear(k, ins["w_c"], 0, C_PLAIN, hi, lo, NT, NCH, func=AF.Copy, out=cc)
            linear(k, ins["w_c"], C_Z, C_TILES - C_Z, hi, lo, NT, NCH, func=AF.Silu, out=cc, out0=C_Z)
        retention(k, cc, og, gains, ins["rope"], ins["ret_const"], ins["ret_state"], outs["ret_p"], outs["ret_s"])
        if upto < 7:
            return
        for half in range(2):
            project_out(ins["w_oc"], KT * half, KT * half)
        cross_attention(1)
        norm(k, gains, G_FINAL, None, None, final_out=outs["y_t"])


def copy_out(k, pairs):
    nc = k.nc
    with ExitStack() as ctx:
        done = ctx.enter_context(nc.semaphore(k.name("copied")))
        block = ctx.enter_context(nc.Block())

        @block.sync
        def _(sp):
            for dst, src in pairs:
                sp.dma_start(dst, src).then_inc(done, 16)
            sp.wait_ge(done, 16 * len(pairs))


def weight_tiles(w):
    kk, f = w.shape
    pad = -f % 128
    if pad:
        w = np.concatenate([w, np.zeros((kk, pad), w.dtype)], axis=1)
        f += pad
    return np.ascontiguousarray(w.reshape(kk // 128, 128, f // 128, 128).transpose(2, 1, 0, 3).reshape(f // 128, 128, kk))


def to_tiles(rows):
    n, f = rows.shape
    return np.ascontiguousarray(rows.T.reshape(f // 128, 128, n))


def from_tiles(t):
    return np.ascontiguousarray(t.reshape(-1, t.shape[-1]).T)


def kernel(**inputs):
    import concourse.bacc as bacc
    from concourse.bass_utils import run_bass_kernel_spmd

    arrays = layout(inputs)
    nc = bacc.Bacc("TRN2", target_bir_lowering=False, num_devices=1)
    ins = {n: nc.dram_tensor(f"in_{n}", arrays[n].shape, mybir.dt.from_np(arrays[n].dtype), kind="ExternalInput").ap()
           for n in INPUTS}
    outs = {n: nc.dram_tensor(f"out_{n}", shape, mybir.dt.float32, kind="ExternalOutput").ap()
            for n, shape in OUTPUTS.items()}
    trunk_program(nc, ins, outs)
    r = run_bass_kernel_spmd(nc, [{f"in_{n}": arrays[n] for n in INPUTS}], core_ids=[0])
    got = {n: np.asarray(r.results[0][f"out_{n}"]) for n in OUTPUTS}
    return unpack(got)


def layout(inputs):
    i = {n: np.asarray(v) for n, v in inputs.items()}
    w = i["w_in_ab"][0]
    cuts = np.cumsum([0, 512, 512, 512, 512, 1536, 512, 4, 4])
    q, kk, v, z, qkv, gz, ga, gb = (w[:, cuts[j]:cuts[j + 1]] for j in range(8))
    gates = np.concatenate([ga, gb, np.zeros((D, 120), w.dtype)], axis=1)
    a = {}
    a["x_t"] = to_tiles(np.concatenate([i["x_prompt"][0], i["x_sample"][:, 0]], axis=0))
    a["mem_t"] = to_tiles(i["mem_prompt"][0])
    a["consts"] = constants()
    m = np.where(np.arange(128)[:, None] < np.arange(128)[None, :], 0.0, -1e30).astype(np.float32)
    a["sb_mask"] = m
    a["rope"] = rope_tables()
    a["ret_const"] = retention_tables()
    a["w_ab"] = weight_tiles(np.concatenate([q, kk, gates, v, qkv, z, gz], axis=1))
    a["w_oab"] = weight_tiles(i["w_out_ab"][0])
    a["w_c"] = weight_tiles(i["w_in_c"][0])
    a["w_oc"] = np.concatenate([weight_tiles(i["w_out_c"][0][:D]), weight_tiles(i["w_out_c"][0][D:])], axis=0)
    a["w_xq"] = np.concatenate([weight_tiles(x) for x in i["xa_wq"]], axis=0)
    a["w_xo"] = np.concatenate([weight_tiles(x) for x in i["xa_wo"]], axis=0)
    a["w_mem"] = np.concatenate([weight_tiles(x) for l in range(2) for x in (i["xa_wk"][l], i["xa_wv"][l])], axis=0)
    cols = [i["norm_mix_g"].reshape(16, 128), i["norm_xa_g"].reshape(16, 128), i["norm_final_g"].reshape(8, 128),
            i["gdn_norm_g"].reshape(1, 128), i["ret_norm_g"].reshape(4, 128)]
    a["gains"] = np.ascontiguousarray(np.concatenate(cols, axis=0).T)
    a["conv_w"] = np.ascontiguousarray(i["conv_w_gdn"][0].T.reshape(12, 128, 4).transpose(1, 0, 2))
    a["sb_bias"] = i["sb_logit_bias"]
    a["a_log"] = i["gdn_a_log"]
    a["dt_bias"] = i["gdn_dt_bias"]
    a["page_table"] = i["page_table"].reshape(1, -1).astype(np.int32)
    a["cache_k"] = i["cache_sb_k"].reshape(N_PHYS, PAGE, SBH * SBD)
    a["cache_v"] = i["cache_sb_v"].reshape(N_PHYS, PAGE, SBH * SBD)
    a["gdn_state"] = i["state_gdn"][0]
    a["gdn_conv"] = np.ascontiguousarray(i["state_gdn_conv"][0].transpose(2, 0, 1).reshape(12, 128, S, 3))
    a["ret_state"] = i["state_ret"][0].reshape(S, RH, 2, 128, 512)
    a["mem_k"] = i["cache_mem_k"].reshape(2 * S, MEM, XH * XD)
    a["mem_v"] = i["cache_mem_v"].reshape(2 * S, MEM, XH * XD)
    return {n: np.ascontiguousarray(v) for n, v in a.items()}


def unpack(got):
    y = from_tiles(got["y_t"])
    kv, vv = from_tiles(got["sb_k_t"]), from_tiles(got["sb_v_t"])
    mem = [from_tiles(got["mem_kv_t"][8 * j:8 * j + 8]) for j in range(4)]
    conv_p = got["conv_p"].reshape(1536, 3).T[None, None]
    conv_s = got["conv_s"].reshape(1536, S, 3).transpose(1, 2, 0)[None]
    return (y[:T].reshape(1, T, D), y[T:].reshape(S, 1, D),
            kv[:T].reshape(1, 1, T, SBH, SBD), vv[:T].reshape(1, 1, T, SBH, SBD),
            np.ascontiguousarray(got["gdn_p"].transpose(1, 0, 2)).reshape(1, 1, GH, 128, 128), np.ascontiguousarray(conv_p),
            got["ret_p"].reshape(1, 1, RH, 256, 512),
            np.stack([mem[0], mem[2]]).reshape(2, 1, MEM, XH, XD), np.stack([mem[1], mem[3]]).reshape(2, 1, MEM, XH, XD),
            kv[T:].reshape(1, S, 1, SBH, SBD), vv[T:].reshape(1, S, 1, SBH, SBD),
            got["gdn_s"].reshape(1, S, GH, 128, 128), np.ascontiguousarray(conv_s),
            got["ret_s"].reshape(1, S, RH, 256, 512))
```

```python
import concourse.bass as bass
import numpy as np
from concourse import mybir
from contextlib import ExitStack

D = 1024
T = 1024
S = 8
NT = T + S
MEM = 256
PAST_PAGES = 32
PAGE = 128
N_PHYS = 320
SBH, SBD = 8, 64
GH = 4
XH, XD = 4, 256
RH = 4
KT = D // 128
NCH = 3
CH = NT // NCH
CHUNK = 128
NCK = T // CHUNK
EPS = 1e-6
CLIP = 40.0
GDN_SCALE = 128 ** -0.5

AB_Q, AB_K, AB_GATES, AB_V, AB_QKV = 0, 4, 8, 9, 13
AB_Z = 25
AB_GZ = 29
AB_TILES = 33
C_Q, C_K, C_V, C_PLAIN, C_Z, C_TILES = 0, 8, 16, 32, 32, 48

CONST = {}
_at = 0
for _name, _n in (("ident", 128), ("ones", 128), ("neg_ones", 128), ("neg_tri", 128), ("tri", 128),
                  ("strict_up", 128), ("levels", 7 * 128), ("sb_diag", 512), ("xs_diag", 512), ("xs_pick", 2 * S), ("eps", 1),
                  ("gq_scale", 2)):
    CONST[_name] = (_at, _at + _n)
    _at += _n
CONST_W = _at


def constants():
    c = np.zeros((128, CONST_W), np.float32)
    p = np.arange(128)[:, None]
    f = np.arange(128)[None, :]

    def put(name, value):
        a, b = CONST[name]
        c[:value.shape[0], a:b] = value

    put("ident", (p == f).astype(np.float32))
    put("ones", np.ones((128, 128), np.float32))
    put("neg_ones", -np.ones((128, 128), np.float32))
    put("neg_tri", -(p >= f).astype(np.float32))
    put("tri", (p <= f).astype(np.float32))
    put("strict_up", (p < f).astype(np.float32))
    lv = []
    for n in range(7):
        b = 1 << n
        lv.append(((p // (2 * b) == f // (2 * b)) & (p // b % 2 == 1) & (f // b % 2 == 0)).astype(np.float32))
    put("levels", np.concatenate(lv, axis=1))
    on = (p // 32 == p % 32 // 8) & (np.arange(512)[None, :] // 64 == p % 8)
    put("sb_diag", on.astype(np.float32))
    put("xs_diag", (p < 64) * (p // 32 * 2 + np.arange(512)[None, :] // 256 == p % 4).astype(np.float32))
    j = np.arange(2 * S)[None, :]
    put("xs_pick", ((p // 32 == j // S) & (p % 32 // XH == j % S)).astype(np.float32))
    put("eps", np.full((128, 1), EPS, np.float32))
    put("gq_scale", np.broadcast_to(np.array([128 ** -0.5, 1.0], np.float32), (128, 2)))
    return c


def rope_tables():
    inv = np.float32(10000.0) ** (-np.arange(128, dtype=np.float32) / np.float32(128))
    pos = np.concatenate([np.arange(T), np.full(S, PAST_PAGES * PAGE)]).astype(np.float32)
    ang = inv.astype(np.float32)[:, None] * pos[None, :]
    return np.stack([np.cos(ang), np.sin(ang)], axis=1).astype(np.float32)


RETC_W = 128 + 128 + 3


def retention_tables():
    out = np.zeros((RH, 128, RETC_W), np.float32)
    lg = np.log1p(-np.exp2(-5.0 - np.arange(RH))).astype(np.float32)
    i = np.arange(128, dtype=np.float32)
    scale = np.float32(XD ** -0.5)
    for h in range(RH):
        diff = i[None, :] - i[:, None]
        out[h, :, 0:128] = np.where(diff >= 0, np.exp(lg[h] * np.maximum(diff, 0)), 0) * scale
        out[h, :, 128:256] = np.exp(lg[h] * (i + 1))[None, :]
        out[h, :, 256] = np.exp(lg[h] * (127 - i)) * scale
        out[h, :, 257] = np.exp(lg[h] * 128)
        out[h, :, 258] = np.exp(lg[h])
    return out


class Kit:

    used = ()

    def semaphore(self, name):
        s = self.nc.alloc_semaphore(name)
        self.used = (*self.used, s)
        return s

    def recycle(self, most=100):
        if len(self.used) > most:
            self.nc.all_engine_barrier()
            self.nc.clear_and_free_semaphores(list(self.used))
            self.nc.all_engine_barrier()
            self.used = ()


def seq(eng, n_tiles, body, after_first=None):
    n = n_tiles // 2
    body(0, True, (0, 1))
    if after_first:
        after_first()
    if n > 1:
        with eng.Fori(1, n) as i:
            body(i, False, (0, 1))
    if n_tiles % 2:
        body(n, False, (0,))


def loop(eng, n, body):
    body(0, True)
    if n > 1:
        with eng.Fori(1, n) as i:
            body(i, False)


def dram_tile(ap, t):
    return ap[bass.ds(t, 1)].rearrange("o p n -> (o p) n")


def inverse_root_mean(act, k, r, sum_banks, sum_done, log_done, r_done):
    act.wait_ge(sum_done, 1)
    act.activation(r[:, :].rearrange("p (c n) -> p c n", c=NCH), sum_banks, k.AF.Ln, bias=k.c("eps"),
                   scale=1.0 / D).then_inc(log_done, 1)
    act.wait_ge(log_done, 1)
    act.activation(r[:, :], r[:, :], k.AF.Exp, scale=-0.5).then_inc(r_done, 1)


def linear(k, w, w0, n_tiles, hi, lo, load=None, norm=None, fresh=None, funcs=(), out=None, resid=None, sumsq=False,
           beside=None):
    k.recycle()
    nc, ALU, AF, f32, f32r, ps = k.nc, k.ALU, k.AF, k.f32, k.f32r, k.ps
    SLOTS = 4
    SUM_BANK = 3
    with ExitStack() as ctx:
        def sb(name, shape, dt=f32):
            return ctx.enter_context(nc.sbuf_tensor(k.name(name), shape, dt))

        def one(name):
            return k.semaphore(k.name(name))

        def sem(name, n=2):
            return [one(f"{name}{u}") for u in range(n)]

        raw = sb("w_raw", [128, 2, KT * 128])
        w_hi = sb("w_hi", [128, 2, KT * 128], f32r)
        w_lo = sb("w_lo", [128, 2, KT * 128], f32r)
        stage = sb("stage", [128, 2, NT]) if resid is None else None
        loaded, hi_done, lo_done = sem("w_loaded"), sem("w_hi_done"), sem("w_lo_done")
        mm_done, evac_done, stored = sem("mm_done"), sem("evac_done"), sem("stored")
        n_y = SLOTS if load else 2
        y = sb("in_raw", [128, n_y, NT])
        y_in = sem("y_in", SLOTS)
        y_done, x_hi_done, x_lo_done = one("y_done"), one("x_hi_done"), one("x_lo_done")
        if norm:
            rstd = sb("rstd", [128, NT])
            sum_done, log_done, r_done = one("sum_done"), one("log_done"), one("rstd_done")
        if sumsq or fresh:
            sq = sb("sq", [128, 2, NT])
            sq_done, add_done = sem("sq_done"), one("add_done")
        if fresh:
            resid_in, tables_in = sem("resid_in", KT), one("tables_in")

        def acc(u):
            return ps[:, 3 * u:3 * u + NCH, 0:CH]

        def add_squares(dve, u, count, i):
            dve.wait_ge(sq_done[u], i + 1)
            dve.wait_ge(add_done, count)
            dve.tensor_tensor(k.sumsq[:, :], k.sumsq[:, :], sq[:, u, :], ALU.add).then_inc(add_done, 1)

        block = ctx.enter_context(nc.Block())

        @block.sync
        def _(sp):
            def store(i, u):
                sp.wait_ge(evac_done[u], i + 1)
                sp.dma_start(dram_tile(out, 2 * i + u), stage[:, u, :]).then_inc(stored[u], 16)

            def body(i, first, us):
                for u in us:
                    if not first:
                        sp.wait_ge(lo_done[u], i)
                    sp.dma_start(raw[:, u, :], dram_tile(w, w0 + 2 * i + u)).then_inc(loaded[u], 16)
                if first and load:
                    load_x()
                if out is not None and not first:
                    for u in (0, 1):
                        store(i - 1, u)

            def load_x():
                for kt in range(KT):
                    if kt >= SLOTS:
                        sp.wait_ge(x_lo_done, kt - SLOTS + 1)
                    sp.dma_start(y[:, kt % SLOTS, :], load[0][load[1] + kt]).then_inc(y_in[kt % SLOTS], 16)

            if fresh:
                for kt in range(KT):
                    sp.dma_start(k.x[:, kt, :], fresh[0][kt]).then_inc(resid_in[kt], 16)
                for dst, src in fresh[1]:
                    sp.dma_start(dst, src).then_inc(tables_in, 16)
            seq(sp, n_tiles, body)
            if out is not None:
                last = (n_tiles - 1) // 2
                for u in range(2 if n_tiles % 2 == 0 else 1):
                    store(last, u)
                sp.wait_ge(stored[0], 16 * ((n_tiles + 1) // 2))
                sp.wait_ge(stored[1], 16 * (n_tiles // 2))

        def split_hi(eng, copy, i, u, first):
            eng.wait_ge(loaded[u], 16 * (i + 1))
            if not first:
                eng.wait_ge(mm_done[u], i)
            copy(w_hi[:, u, :], raw[:, u, :]).then_inc(hi_done[u], 1)

        def split_lo(eng, i, u):
            eng.wait_ge(hi_done[u], i + 1)
            eng.tensor_tensor(w_lo[:, u, :], raw[:, u, :], w_hi[:, u, :].bitcast(f32),
                              ALU.subtract).then_inc(lo_done[u], 1)

        def input_high(act):
            if fresh:
                for kt in range(KT):
                    act.wait_ge(resid_in[kt], 16)
                    if kt >= 2:
                        act.wait_ge(add_done, kt)
                    act.activation(sq[:, kt % 2, :], k.x[:, kt, :], AF.Square).then_inc(sq_done[kt % 2], 1)
            if norm:
                inverse_root_mean(act, k, rstd, ps[:, SUM_BANK:SUM_BANK + NCH, 0:CH], sum_done, log_done, r_done)
            for kt in range(KT):
                if norm:
                    act.wait_ge(y_done, kt + 1)
                else:
                    act.wait_ge(y_in[kt % SLOTS], 16 * (kt // SLOTS + 1))
                act.copy(hi[:, kt, :], y[:, kt % n_y, :]).then_inc(x_hi_done, 1)

        def input_low(dve):
            def scaled(kt):
                if kt >= 2:
                    dve.wait_ge(x_lo_done, kt - 1)
                g = norm[0][:, norm[1] + kt:norm[1] + kt + 1]
                dve.scalar_tensor_tensor(y[:, kt % 2, :], k.x[:, kt, :], g, rstd[:, :], ALU.mult,
                                         ALU.mult).then_inc(y_done, 1)

            if fresh:
                dve.memset(k.sumsq[:, :], 0.0).then_inc(add_done, 1)
                for kt in range(KT):
                    add_squares(dve, kt % 2, kt + 1, kt // 2)
            if norm:
                dve.wait_ge(r_done, 1)
                scaled(0)
            for kt in range(KT):
                if norm and kt + 1 < KT:
                    scaled(kt + 1)
                dve.wait_ge(x_hi_done, kt + 1)
                dve.tensor_tensor(lo[:, kt, :], y[:, kt % n_y, :], hi[:, kt, :].bitcast(f32),
                                  ALU.subtract).then_inc(x_lo_done, 1)

        if beside:
            @block.gpsimd
            def _(pool):
                beside(pool, stored)

        if resid is None:
            @block.vector
            def _(dve):
                def body(i, first, us):
                    for u in us:
                        split_hi(dve, dve.tensor_copy, i, u, first)
                        split_lo(dve, i, u)

                seq(dve, n_tiles, body, lambda: input_low(dve))

            @block.scalar
            def _(act):
                def evacuate(i, u, first, func):
                    act.wait_ge(mm_done[u], i + 1)
                    if not first:
                        act.wait_ge(stored[u], 16 * i)
                    act.activation(stage[:, u, :].rearrange("p (c n) -> p c n", c=NCH), acc(u),
                                   func).then_inc(evac_done[u], 1)

                if norm:
                    act.preload_act_table_set("natural_log_exp_and_others")
                input_high(act)
                done = 0
                for tiles, func in funcs:
                    pairs = (done + tiles) // 2
                    if done == 0:
                        for u in range(2):
                            evacuate(0, u, True, func)
                    if pairs > max(done // 2, 1):
                        with act.Fori(max(done // 2, 1), pairs) as i:
                            for u in range(2):
                                evacuate(i, u, False, func)
                    done += tiles
                if done % 2:
                    evacuate(done // 2, 0, False, func)
        else:
            @block.scalar
            def _(act):
                def square(i, u):
                    act.wait_ge(evac_done[u], i + 1)
                    t = 2 * i + u
                    act.activation(sq[:, u, :], resid[:, bass.ds(t, 1), :].rearrange("p o n -> p (o n)"),
                                   AF.Square).then_inc(sq_done[u], 1)

                def body(i, first, us):
                    for u in us:
                        split_hi(act, act.copy, i, u, first)
                    if sumsq and not first:
                        for u in us:
                            act.wait_ge(add_done, 2 * i + u - 1)
                            square(i - 1, u)

                seq(act, n_tiles, body, lambda: input_high(act))
                if sumsq:
                    for u in range(2):
                        act.wait_ge(add_done, n_tiles + u - 1)
                        square(n_tiles // 2 - 1, u)

            @block.gpsimd
            def _(pool):
                def body(i, first, us):
                    for u in us:
                        split_lo(pool, i, u)

                seq(pool, n_tiles, body)

            @block.vector
            def _(dve):
                def body(i, first, us):
                    for u in us:
                        if sumsq and not first:
                            add_squares(dve, u, 2 * i + u - 1, i - 1)
                        dve.wait_ge(mm_done[u], i + 1)
                        x = resid[:, bass.ds(2 * i + u, 1), :].rearrange("p o (c n) -> p (o c) n", c=NCH)
                        dve.tensor_tensor(x, acc(u), x, ALU.add).then_inc(evac_done[u], 1)

                if sumsq:
                    dve.memset(k.sumsq[:, :], 0.0).then_inc(add_done, 1)
                input_low(dve)
                seq(dve, n_tiles, body)
                if sumsq:
                    for u in range(2):
                        add_squares(dve, u, n_tiles + u - 1, n_tiles // 2 - 1)

        @block.tensor
        def _(pe):
            def product(u, kt, c):
                o, a, b = ps[:, 3 * u + c, 0:CH], kt * 128, kt * 128 + 128
                h, l = hi[:, kt, c * CH:c * CH + CH], lo[:, kt, c * CH:c * CH + CH]
                pe.matmul(o, w_hi[:, u, a:b], h, start=(kt == 0), stop=False)
                pe.matmul(o, w_hi[:, u, a:b], l, start=False, stop=False)
                return pe.matmul(o, w_lo[:, u, a:b], h, start=False, stop=(kt == KT - 1))

            def body(i, first, us):
                if first:
                    order = [(kt, u) for kt in range(KT) for u in us if u == 0 or kt < KT // 2]
                    order += [(kt, 1) for kt in range(KT // 2, KT)]
                    for kt, u in order:
                        pe.wait_ge(x_lo_done, kt + 1)
                        if kt == 0:
                            pe.wait_ge(lo_done[u], 1)
                        for c in range(NCH):
                            last = product(u, kt, c)
                        if kt == KT - 1:
                            last.then_inc(mm_done[u], 1)
                    return
                for u in us:
                    pe.wait_ge(lo_done[u], i + 1)
                    pe.wait_ge(evac_done[u], i)
                    for c in range(NCH):
                        for kt in range(KT):
                            last = product(u, kt, c)
                    last.then_inc(mm_done[u], 1)

            if norm:
                if fresh:
                    pe.wait_ge(tables_in, 16 * len(fresh[1]))
                    pe.wait_ge(add_done, KT + 1)
                for c in range(NCH):
                    last = pe.matmul(ps[:, SUM_BANK + c, 0:CH], k.c("ones"), k.sumsq[:, c * CH:c * CH + CH], start=True,
                                     stop=True)
                last.then_inc(sum_done, 1)
            seq(pe, n_tiles, body)


def final_norm(k, g, g_col, out):
    k.recycle()
    nc, ALU, f32, ps = k.nc, k.ALU, k.f32, k.ps
    SLOTS = 4
    with ExitStack() as ctx:
        def sb(name, shape):
            return ctx.enter_context(nc.sbuf_tensor(k.name(name), shape, f32))

        rstd = sb("rstd", [128, NT])
        y = sb("y", [128, SLOTS, NT])
        sum_done, log_done, r_done, y_done = (k.semaphore(k.name(n)) for n in ("sum_done", "log_done", "r_done", "y_done"))
        stored = [k.semaphore(k.name(f"stored{u}")) for u in range(SLOTS)]
        block = ctx.enter_context(nc.Block())

        @block.scalar
        def _(act):
            act.preload_act_table_set("natural_log_exp_and_others")
            inverse_root_mean(act, k, rstd, ps[:, 0:NCH, 0:CH], sum_done, log_done, r_done)

        @block.tensor
        def _(pe):
            for c in range(NCH):
                last = pe.matmul(ps[:, c, 0:CH], k.c("ones"), k.sumsq[:, c * CH:c * CH + CH], start=True, stop=True)
            last.then_inc(sum_done, 1)

        @block.vector
        def _(dve):
            dve.wait_ge(r_done, 1)
            for kt in range(KT):
                if kt >= SLOTS:
                    dve.wait_ge(stored[kt % SLOTS], 16 * (kt // SLOTS))
                dve.scalar_tensor_tensor(y[:, kt % SLOTS, :], k.x[:, kt, :], g[:, g_col + kt:g_col + kt + 1], rstd[:, :],
                                         ALU.mult, ALU.mult).then_inc(y_done, 1)

        @block.sync
        def _(sp):
            for kt in range(KT):
                sp.wait_ge(y_done, kt + 1)
                sp.dma_start(out[kt], y[:, kt % SLOTS, :]).then_inc(stored[kt % SLOTS], 16)
            for u in range(SLOTS):
                sp.wait_ge(stored[u], 16 * (KT // SLOTS))


def load_split(k, src, src0, hi, lo, tokens):
    k.recycle()
    nc, ALU, f32 = k.nc, k.ALU, k.f32
    SLOTS = 4
    with ExitStack() as ctx:
        y = ctx.enter_context(nc.sbuf_tensor(k.name("in_raw"), [128, SLOTS, tokens], f32))
        loaded = [k.semaphore(k.name(f"loaded{u}")) for u in range(SLOTS)]
        hi_done = k.semaphore(k.name("hi_done"))
        lo_done = k.semaphore(k.name("lo_done"))
        block = ctx.enter_context(nc.Block())

        @block.sync
        def _(sp):
            for kt in range(KT):
                if kt >= SLOTS:
                    sp.wait_ge(lo_done, kt - SLOTS + 1)
                sp.dma_start(y[:, kt % SLOTS, :], src[src0 + kt]).then_inc(loaded[kt % SLOTS], 16)

        @block.scalar
        def _(act):
            for kt in range(KT):
                act.wait_ge(loaded[kt % SLOTS], 16 * (kt // SLOTS + 1))
                act.copy(hi[:, kt, :], y[:, kt % SLOTS, :]).then_inc(hi_done, 1)

        @block.vector
        def _(dve):
            for kt in range(KT):
                dve.wait_ge(hi_done, kt + 1)
                dve.tensor_tensor(lo[:, kt, :], y[:, kt % SLOTS, :], hi[:, kt, :].bitcast(f32),
                                  ALU.subtract).then_inc(lo_done, 1)


SB_STEPS = [(u, c, i) for u in range(2) for c in range(2) for i in range(4 * c + 3, -1, -1)]


def sb_prompt(k, ab, og, bias, copies):
    k.recycle()
    nc, ALU, AF, f32, f32r, ps = k.nc, k.ALU, k.AF, k.f32, k.f32r, k.ps
    NS = len(SB_STEPS)
    PAIRS = SBH // 2
    group = [2 * u + c for u, c, _ in SB_STEPS]
    ends = [s for s in range(NS) if s == NS - 1 or group[s + 1] != group[s]]
    top = [s == 0 or group[s - 1] != group[s] for s in range(NS)]
    NZ = 6
    ZB, OB = 0, NZ
    PREP_1, PREP_0 = 2, 14
    TRANSPOSES = ((14, 0, OB + 1), (18, 1, OB))

    NA = NS - len(ends)

    def n0_of(t):
        _, c, i = SB_STEPS[t % NS]
        return max(0, 128 * i - 512 * c)

    def accs(t):
        return t // NS * NA + t % NS - sum(e < t % NS for e in ends)

    with ExitStack() as ctx:
        def sb(name, shape, dt=f32):
            return ctx.enter_context(nc.sbuf_tensor(k.name(name), shape, dt))

        def sem(name):
            return k.semaphore(k.name(name))

        raw = sb("kq_raw", [128, 2, 2, T])
        ks = sb("k_stack", [128, 2, T], f32r)
        qh = sb("q_hi", [128, 2, T], f32r)
        ql = sb("q_lo", [64, 2, T], f32r)
        vt, gate, gated = sb("v_t", [128, T]), sb("gate", [128, T]), sb("gated", [128, T])
        bias_all, bias_u = sb("bias_all", [128, SBH]), sb("bias_u", [128, 2])
        vtok, vnext = sb("vtok", [128, T // 128, 128]), sb("vtok_next", [128, T // 128, 128])
        ident_r, mask_r, tri_r = (sb(n, [128, 128], f32r) for n in ("ident_r", "mask_r", "neg_tri_r"))
        zc = sb("zc", [128, 3, 512])
        sp_ = sb("softplus", [128, 3, 512])
        sp_hi = sb("softplus_hi", [128, 3, 512], f32r)
        sp_lo = sb("softplus_lo", [128, 3, 512], f32r)
        acc = sb("later_blocks", [128, 2, 512])
        zeros = sb("zeros", [128, 128])
        a = sb("a", [128, 2, 512])
        raw_in, kh_done, qh_done, prepared = ([sem(f"{n}{u}") for u in range(2)] for n in ("raw_in", "kh", "qh", "prep"))
        bias_in, v_in, gate_in, tables_done, vt_done, vnext_done, vtok_done = (
            sem(x) for x in ("bias_in", "v_in", "gate_in", "tables", "vt_done", "vnext", "vtok_done"))
        z_done, zc_done, e_done, l_done, sp_done, hi_done, lo_done = (
            sem(x) for x in ("z", "zc", "e", "l", "sp", "sp_hi", "sp_lo"))
        acc_done, sum_done, a_done, av_done, og_done, stored, zeroed, copied = (
            sem(x) for x in ("acc", "sum", "a", "av", "og", "stored", "zeroed", "copied"))
        block = ctx.enter_context(nc.Block())

        def pairs(eng, body):
            body(0, True, False)
            with eng.Fori(1, PAIRS - 1) as p:
                body(p, False, False)
            body(PAIRS - 1, False, True)

        @block.sync
        def _(sp):
            def load_head(p, u):
                for j, t0 in enumerate((AB_K, AB_Q)):
                    for half in range(2):
                        sp.dma_start(raw[64 * half:64 * half + 64, u, j, :],
                                     dram_tile(ab, t0 + p)[64 * u:64 * u + 64, 0:T]).then_inc(raw_in[u], 16)

            def store(p):
                sp.dma_start(dram_tile(og, p)[:, 0:T], gated[:, :]).then_inc(stored, 16)

            def body(p, first, last):
                if first:
                    load_head(0, 0)
                    sp.dma_start(bias_all[:, :], bias.broadcast_to((128, SBH))).then_inc(bias_in, 16)
                    sp.dma_start(vt[:, :], ab[AB_V][:, 0:T]).then_inc(v_in, 16)
                    load_head(0, 1)
                else:
                    sp.wait_ge(og_done, 4 * p)
                sp.dma_start(gate[:, :], dram_tile(ab, AB_Z + p)[:, 0:T]).then_inc(gate_in, 16)
                if first:
                    for dst, src in copies:
                        sp.dma_start(dst, src).then_inc(copied, 16)
                if not first:
                    store(p - 1)
                if not last:
                    for u in range(2):
                        sp.wait_ge(prepared[u], 3 * p + 3)
                        load_head(p + 1, u)
                    sp.wait_ge(vt_done, 2 * p + 2)
                    sp.dma_start(vt[:, :], dram_tile(ab, AB_V + 1 + p)[:, 0:T]).then_inc(v_in, 16)

            pairs(sp, body)
            sp.wait_ge(og_done, 4 * PAIRS)
            store(PAIRS - 1)
            sp.wait_ge(stored, 16 * PAIRS)
            sp.wait_ge(copied, 16 * len(copies))

        @block.tensor
        def _(pe):
            def transpose_values(p, half, bank):
                pe.wait_ge(v_in, 16 * p + 16)
                for j in range(4):
                    t = 4 * half + j
                    last = pe.transpose(ps[:, bank, 128 * j:128 * j + 128], vt[:, t * 128:t * 128 + 128], k.c("ident"))
                last.then_inc(vt_done, 1)

            def z(p, t, first):
                u, c, i = SB_STEPS[t % NS]
                n0, cols = n0_of(t), slice(512 * c + n0_of(t), 512 * c + 512)
                if t % (NS // 2) == 0:
                    pe.wait_ge(prepared[u], 3 * (p + t // NS) + 3)
                if t >= NZ or not first:
                    pe.wait_ge(a_done, NS * p + t - NZ + 1)
                o = ps[:, ZB + t % NZ, n0:512]
                pe.matmul(o, ks[:, u, 128 * i:128 * i + 128], qh[:, u, cols], start=True, stop=False)
                last = pe.matmul(o, ks[0:64, u, 128 * i:128 * i + 128], ql[:, u, cols], start=False, stop=(i < 4 * c))
                if i >= 4 * c:
                    last = pe.matmul(ps[:, ZB + t % NZ, n0:n0 + 128], ident_r[:, :], mask_r[:, :],
                                     start=False, stop=True)
                last.then_inc(z_done, 1)

            def sums(p, s):
                n0 = n0_of(s)
                o = ps[:, ZB + s % NZ, n0:512]
                pe.wait_ge(lo_done, NS * p + s + 1)
                pe.matmul(o, tri_r[:, :], sp_hi[:, s % 3, n0:512], start=False, stop=False, skip_group_check=True)
                last = pe.matmul(o, tri_r[:, :], sp_lo[:, s % 3, n0:512], start=False, stop=top[s],
                                 skip_group_check=True)
                if not top[s]:
                    n1 = n0_of(s - 1)
                    pe.wait_ge(acc_done, NA * p + accs(s))
                    last = pe.matmul(ps[:, ZB + s % NZ, n1:512], k.c("neg_ones"), acc[:, s % 2, n1:512], start=False,
                                     stop=True, skip_group_check=True)
                last.then_inc(sum_done, 1)

            def av(p, t, first, last):
                u, c, i = SB_STEPS[t % NS]
                n0, g = n0_of(t), group[t % NS]
                if t == 0:
                    if first:
                        pe.wait_ge(vnext_done, 2)
                    else:
                        pe.wait_ge(vtok_done, p)
                pe.wait_ge(a_done, NS * p + t + 1)
                if top[t % NS] and (g >= 2 or not first):
                    pe.wait_ge(og_done, 4 * p + g - 1)
                if top[t % NS] and g in (0, 3):
                    pe.wait_ge(vnext_done, 2 * p + (2 if g == 0 or g == 3 and last else 3))
                pe.matmul(ps[64 * u:64 * u + 64, OB + g % 2, n0:512], vtok[:, i, 64 * u:64 * u + 64],
                          a[:, t % 2, n0:512], start=top[t % NS], stop=(t % NS in ends),
                          skip_group_check=True).then_inc(av_done, 1)

            def body(p, first, last):
                if first:
                    for _, half, bank in TRANSPOSES:
                        transpose_values(0, half, bank)
                    pe.wait_ge(tables_done, 3)
                    for t in range(3):
                        z(p, t, first)
                for s in range(NS):
                    if s + 3 < NS or not last:
                        z(p, s + 3, first)
                    sums(p, s)
                    if s >= 1 or not first:
                        av(p, s - 1, first, last)
                    for step, half, bank in TRANSPOSES:
                        if s == step and not last:
                            pe.wait_ge(og_done, 4 * p + 2 + half)
                            transpose_values(p + 1, half, bank)

            pairs(pe, body)
            av(PAIRS - 1, NS - 1, False, True)

        @block.vector
        def _(dve):
            def prepare(p, u, first):
                dve.wait_ge(kh_done[u], p + 1)
                dve.tensor_tensor(ks[64:128, u, :], raw[64:128, u, 0, :], ks[64:128, u, :].bitcast(f32),
                                  ALU.subtract).then_inc(prepared[u], 1)
                dve.wait_ge(qh_done[u], p + 1)
                dve.scalar_tensor_tensor(ql[:, u, :], raw[0:64, u, 1, :], SBD ** -0.5, qh[0:64, u, :].bitcast(f32),
                                         ALU.mult, ALU.subtract).then_inc(prepared[u], 1)
                if first:
                    dve.wait_ge(bias_in, 16)
                else:
                    dve.wait_ge(a_done, NS * (p - 1) + NS // 2 * (u + 1))
                dve.tensor_copy(bias_u[:, u:u + 1], bias_all[:, bass.ds(2 * p + u, 1)]).then_inc(prepared[u], 1)

            def clip(p, t, first):
                n0, u = n0_of(t), SB_STEPS[t % NS][0]
                if t % (NS // 2) == 0:
                    dve.wait_ge(prepared[u], 3 * (p + t // NS) + 3)
                dve.wait_ge(z_done, NS * p + t + 1)
                if t >= 3 or not first:
                    dve.wait_ge(sp_done, NS * p + t - 2)
                dve.tensor_scalar(zc[:, t % 3, n0:512], ps[:, ZB + t % NZ, n0:512], bias_u[:, u:u + 1], CLIP, ALU.add,
                                  ALU.min).then_inc(zc_done, 1)

            def softplus(p, t, first):
                n0, u = n0_of(t), SB_STEPS[t % NS][0]
                dve.wait_ge(l_done, NS * p + t + 1)
                if t >= 3 or not first:
                    dve.wait_ge(acc_done, NA * p + accs(t - 2))
                    dve.wait_ge(hi_done, NS * p + t - 2)
                dve.scalar_tensor_tensor(sp_[:, t % 3, n0:512], ps[:, ZB + t % NZ, n0:512], bias_u[:, u:u + 1],
                                         zc[:, t % 3, n0:512], ALU.add, ALU.max).then_inc(sp_done, 1)

            def low(p, t):
                n0 = n0_of(t)
                dve.wait_ge(hi_done, NS * p + t + 1)
                dve.tensor_tensor(sp_lo[:, t % 3, n0:512], sp_[:, t % 3, n0:512], sp_hi[:, t % 3, n0:512].bitcast(f32),
                                  ALU.subtract).then_inc(lo_done, 1)

            def gated_out(p, g):
                u, c = g // 2, g % 2
                dve.wait_ge(av_done, NS * p + ends[g] + 1)
                if g == 0:
                    dve.wait_ge(gate_in, 16 * p + 16)
                h = slice(64 * u, 64 * u + 64)
                dve.tensor_tensor(gated[h, 512 * c:512 * c + 512], ps[h, OB + c, :], gate[h, 512 * c:512 * c + 512],
                                  ALU.mult).then_inc(og_done, 1)

            def values(p):
                dve.wait_ge(vnext_done, 2 * p + 2)
                dve.wait_ge(av_done, NS * p)
                dve.tensor_copy(vtok[:, :, :], vnext[:, :, :]).then_inc(vtok_done, 1)

            def body(p, first, last):
                if first:
                    prepare(0, 0, True)
                    for t in range(3):
                        clip(p, t, first)
                    softplus(p, 0, first)
                    low(p, 0)
                for s in range(NS):
                    if s + 1 < NS or not last:
                        softplus(p, s + 1, first)
                    if s + 3 < NS or not last:
                        clip(p, s + 3, first)
                    if s + 1 < NS or not last:
                        low(p, s + 1)
                    if s == PREP_1:
                        prepare(p, 1, first)
                    if s == PREP_0 and not last:
                        prepare(p + 1, 0, False)
                    if s == 1 and not first:
                        values(p)
                        gated_out(p - 1, 3)
                    for g in range(3):
                        if s == ends[g] + 2:
                            if g == 0 and not first:
                                dve.wait_ge(stored, 16 * p)
                            gated_out(p, g)

            pairs(dve, body)
            gated_out(PAIRS - 1, 3)

        @block.scalar
        def _(act):
            def prepare(p, u, first):
                act.wait_ge(raw_in[u], 64 * p + 64)
                if not first:
                    act.wait_ge(z_done, NS * (p - 1) + NS // 2 * (u + 1))
                act.copy(ks[:, u, :], raw[:, u, 0, :]).then_inc(kh_done[u], 1)
                act.activation(qh[:, u, :], raw[:, u, 1, :], AF.Copy, scale=SBD ** -0.5).then_inc(qh_done[u], 1)

            def values(p, half, bank, dst):
                act.wait_ge(vt_done, 2 * p + half + 1)
                act.copy(dst[:, 4 * half:4 * half + 4].rearrange("p t n -> p (t n)"), ps[:, bank, :]).then_inc(vnext_done, 1)

            def logarithm(p, t):
                z = zc[:, t % 3, n0_of(t):512]
                act.wait_ge(zc_done, NS * p + t + 1)
                act.activation(z, z, AF.Exp).then_inc(e_done, 1)
                act.wait_ge(e_done, NS * p + t + 1)
                act.activation(z, z, AF.Ln, bias=k.c("ones")[:, 0:1]).then_inc(l_done, 1)

            def high(p, t, first):
                n0 = n0_of(t)
                act.wait_ge(sp_done, NS * p + t + 1)
                if t >= 3 or not first:
                    act.wait_ge(sum_done, NS * p + t - 2)
                act.copy(sp_hi[:, t % 3, n0:512], sp_[:, t % 3, n0:512]).then_inc(hi_done, 1)

            def weight(p, t, first):
                n0, u = n0_of(t), SB_STEPS[t % NS][0]
                act.wait_ge(sum_done, NS * p + t + 1)
                if t >= 2 or not first:
                    act.wait_ge(av_done, NS * p + t - 1)
                act.activation(a[:, t % 2, n0:512], ps[:, ZB + t % NZ, n0:512], AF.Exp,
                               bias=bias_u[:, u:u + 1]).then_inc(a_done, 1)

            def body(p, first, last):
                if first:
                    prepare(0, 0, True)
                    for _, half, bank in TRANSPOSES:
                        values(0, half, bank, vtok)
                    for t in range(3):
                        logarithm(p, t)
                    high(p, 0, first)
                for s in range(NS):
                    if s >= 1 or not first:
                        weight(p, s - 1, first)
                    if s + 1 < NS or not last:
                        high(p, s + 1, first)
                    if s + 3 < NS or not last:
                        logarithm(p, s + 3)
                    if s == PREP_1:
                        prepare(p, 1, first)
                    if s == PREP_0 and not last:
                        prepare(p + 1, 0, False)
                    for step, half, bank in TRANSPOSES:
                        if s == step and not last:
                            if half == 0 and not first:
                                act.wait_ge(vtok_done, p)
                            values(p + 1, half, bank, vnext)

            act.preload_act_table_set("natural_log_exp_and_others")
            for dst, src in ((ident_r, k.c("ident")), (mask_r, k.sb_mask[:, :]), (tri_r, k.c("neg_tri"))):
                act.copy(dst[:, :], src).then_inc(tables_done, 1)
            pairs(act, body)
            weight(PAIRS - 1, NS - 1, False)

        @block.gpsimd
        def _(pool):
            pool.memset(zeros[:, :], 0.0).then_inc(zeroed, 1)
            pool.wait_ge(zeroed, 1)

            def body(p, first, last):
                for s in range(NS):
                    if s in ends:
                        continue
                    n0 = n0_of(s)
                    pool.wait_ge(sp_done, NS * p + s + 1)
                    if s >= 1 or not first:
                        pool.wait_ge(sum_done, NS * p + s)
                    sp_new, acc_new, acc_old = sp_[:, s % 3], acc[:, (s + 1) % 2], acc[:, s % 2]
                    n1 = 512 if top[s] else n0_of(s - 1)
                    if n0 < n1:
                        last_op = pool.tensor_tensor(acc_new[:, n0:n0 + 128], sp_new[:, n0:n0 + 128], zeros[:, :], ALU.add)
                    if not top[s]:
                        pool.wait_ge(acc_done, NA * p + accs(s))
                        last_op = pool.tensor_tensor(acc_new[:, n1:512], acc_old[:, n1:512], sp_new[:, n1:512], ALU.add)
                    last_op.then_inc(acc_done, 1)

            pairs(pool, body)


W_PLAIN, W_SILU, W_MEM = 2, 1, 4
W_ORDER = (("plain", 0, 0), ("mem", 0, 1), ("plain", 1, 2), ("mem", 1, 0), ("silu", 0, 1), ("mem", 2, 2),
           ("mem", 3, 1))


def weave(k, early0, w_ab, hi, lo, ab, w_mem, m_hi, m_lo, mem_kv, og, cache_k, cache_v, page_table, bias):
    k.recycle(0)
    nc, ALU, AF, f32, f32r, ps = k.nc, k.ALU, k.AF, k.f32, k.f32r, k.ps
    NP, G = PAST_PAGES, 4
    NJ = NP // G
    W = NP * SBH
    SUF = 10
    NPOS = len(W_ORDER)
    A_BANK, M_BANK, SUMB, OB, CB = 0, 3, 5, 6, 7
    with ExitStack() as ctx:
        def sb(name, shape, dt=f32):
            return ctx.enter_context(nc.sbuf_tensor(k.name(name), shape, dt))

        def sem(name):
            return k.semaphore(k.name(name))

        raw = sb("wv_raw", [128, 2, KT * 128])
        w_hi, w_lo = sb("wv_hi", [128, 3, KT * 128], f32r), sb("wv_lo", [128, 3, KT * 128], f32r)
        stage = sb("wv_stage", [128, 3, NT])
        m_stage = sb("wv_mem_stage", [128, 2, MEM])
        pt = sb("page_table", [1, S * NP], mybir.dt.int32)
        qs, gate = sb("qs", [128, 4, S]), sb("gate", [128, 4, S])
        bias_all = sb("bias_all", [128, SBH])
        qbc = sb("q_rows", [128, S, 512])
        kp, vp = sb("k_pages", [128, 2, G * 512]), sb("v_pages", [128, 2, G * 512])
        prod = sb("prod", [128, G * 512])
        z, zc, sp_ = sb("z", [128, W]), sb("zc", [128, W]), sb("softplus", [128, W])
        suf = sb("suffix", [128, 2, W])
        a = sb("a", [128, W])
        om = sb("masked", [128, 512])
        osT, gated = sb("osT", [128, 4, S]), sb("gated", [128, 4, S])

        loaded = [sem(f"w_loaded{n}") for n in range(NPOS)]
        hi_done, lo_done, mm_done, evac_done = sem("w_hi"), sem("w_lo"), sem("mm"), sem("evac")
        stored = [sem(f"w_stored{n}") for n in range(5)]
        (setup, q_rows, q_copied, prod_done, red_done, zb_done, zc_done, e_done, l_done, sp_done, suf_done,
         sum_done, t_done, a_done, pv_done, om_done, col_done, os_done, gate_in, gated_done, og_stored) = (
            sem(x) for x in ("setup", "q_rows", "q_copied", "prod", "red", "zb", "zc", "e", "l", "sp", "suf", "sum",
                             "t", "a", "pv", "om", "col", "os", "gate_in", "gated", "og_stored"))
        NE = AB_V - early0
        early_in = [sem(f"early_in{n}") for n in range(2)]
        early_stored = [sem(f"early_st{n}") for n in range(3)]
        early_hi, early_lo, early_mm, early_evac = sem("early_hi"), sem("early_lo"), sem("early_mm"), sem("early_evac")
        k_in, v_in = [sem("k_in0"), sem("k_in1")], [sem("v_in0"), sem("v_in1")]
        block = ctx.enter_context(nc.Block())

        RAW = [pos % 2 for pos in range(NPOS)]
        SLOT = [x[2] for x in W_ORDER]
        BANK = [M_BANK + n % 2 if kind == "mem" else A_BANK for kind, n, _ in W_ORDER]

        def back(of, pos):
            return next(d for d in range(1, NPOS + 1) if of[(pos - d) % NPOS] == of[pos])

        def store_slot(kind, n):
            return {"plain": n, "silu": 2, "mem": 3 + n % 2}[kind]

        def at(step, first, pos, d):
            v = NPOS * step + pos + 1 - d
            return v if not first or v > 0 else None

        def pages(eng, cache, dst, sem_, s, j):
            for g in range(G):
                page = eng.value_load(pt[0:1, bass.ds(s * NP + j * G + g, 1)], min_val=0, max_val=N_PHYS - 1)
                eng.dma_start(dst[:, j % 2, g * 512:(g + 1) * 512], dram_tile(cache, page)).then_inc(sem_[j % 2], 16)

        @block.gpsimd
        def _(pool):
            pool.wait_ge(setup, 48)

            def step(s, first):
                for j in range(NJ):
                    if not (first and j < 2):
                        pool.wait_ge(pv_done, NJ * s + j - 1)
                    pages(pool, cache_v, vp, v_in, s, j)

            loop(pool, S, step)

        @block.sync
        def _(sp):
            sp.dma_start(pt[:, :], page_table).then_inc(setup, 16)
            sp.dma_start(bias_all[:, :], bias.broadcast_to((128, SBH))).then_inc(setup, 16)
            sp.dma_start(qs[:, :, :], ab[AB_Q:AB_Q + 4, :, T:NT].rearrange("t p n -> p t n")).then_inc(setup, 16)
            sp.wait_ge(setup, 48)

            def weights(s, first, pos):
                kind, n, _ = W_ORDER[pos]
                v = at(s, first, pos, back(RAW, pos))
                if v is not None:
                    sp.wait_ge(lo_done, v)
                else:
                    sp.wait_ge(early_lo, NE)
                t = {"plain": AB_V + W_PLAIN * s + n, "silu": AB_Z + s, "mem": W_MEM * s + n}[kind]
                sp.dma_start(raw[:, RAW[pos], :], dram_tile(w_mem if kind == "mem" else w_ab, t)).then_inc(loaded[pos], 16)

            def k_pages(s, j, first):
                if not (first and j < 2):
                    sp.wait_ge(prod_done, NJ * s + j - 1)
                pages(sp, cache_k, kp, k_in, s, j)

            def step(s, first, last=False):
                for j in range(NJ):
                    if j < NPOS:
                        weights(s, first, j)
                    if not last:
                        k_pages(s + 1, j, False)

            for j in range(NJ):
                if j < NE:
                    if j >= 2:
                        sp.wait_ge(early_lo, j - 1)
                    sp.dma_start(raw[:, j % 2, :], w_ab[early0 + j]).then_inc(early_in[j % 2], 16)
                k_pages(0, j, True)
            loop(sp, S - 1, step)
            step(S - 1, False, last=True)
            sp.wait_ge(os_done, S)
            sp.wait_ge(stored[2], 16 * S)
            sp.dma_start(gate[:, :, :], ab[AB_Z:AB_Z + 4, :, T:NT].rearrange("t p n -> p t n")).then_inc(gate_in, 16)
            sp.wait_ge(gated_done, 1)
            sp.dma_start(og[0:4, :, T:NT].rearrange("t p n -> p t n"), gated[:, :, :]).then_inc(og_stored, 16)
            sp.wait_ge(og_stored, 16)

        @block.vector
        def _(dve):
            v3 = lambda x: x.rearrange("p (n h) -> p n h", h=SBH)
            v4 = lambda x: x.rearrange("p (g n) -> p g n", g=G)

            def split(s, first, pos):
                _, _, slot = W_ORDER[pos]
                dve.wait_ge(loaded[pos], 16 * (s + 1))
                v = at(s, first, pos, back(SLOT, pos))
                if v is not None:
                    dve.wait_ge(mm_done, v)
                else:
                    dve.wait_ge(early_mm, NE)
                dve.tensor_copy(w_hi[:, slot, :], raw[:, RAW[pos], :]).then_inc(hi_done, 1)
                dve.wait_ge(hi_done, NPOS * s + pos + 1)
                dve.tensor_tensor(w_lo[:, slot, :], raw[:, RAW[pos], :], w_hi[:, slot, :].bitcast(f32),
                                  ALU.subtract).then_inc(lo_done, 1)

            def scores(s, j, first):
                dve.wait_ge(k_in[j % 2], 64 * (NJ // 2 * s + j // 2 + 1))
                if not (first and j == 0):
                    dve.wait_ge(red_done, NJ * s + j)
                dve.tensor_tensor(v4(prod[:, :]), v4(kp[:, j % 2, :]),
                                  qbc[:, bass.ds(s, 1), :].broadcast_to((128, G, 512)), ALU.mult).then_inc(prod_done, 1)
                dve.wait_ge(prod_done, NJ * s + j + 1)
                if j == 0 and not first:
                    dve.wait_ge(t_done, s)
                dve.tensor_reduce(z[:, j * G * SBH:(j + 1) * G * SBH], prod[:, :].rearrange("p (n d) -> p n d", d=SBD),
                                  k.AX.X, ALU.add).then_inc(red_done, 1)

            def sums(s, first):
                dve.wait_ge(red_done, NJ * s + NJ)
                dve.scalar_tensor_tensor(v3(z[:, :]), v3(z[:, :]), SBD ** -0.5,
                                         bias_all[:, None, :].broadcast_to((128, NP, SBH)),
                                         ALU.mult, ALU.add).then_inc(zb_done, 1)
                dve.wait_ge(zb_done, s + 1)
                if not first:
                    dve.wait_ge(a_done, s)
                dve.tensor_scalar(zc[:, :], z[:, :], CLIP, None, ALU.min).then_inc(zc_done, 1)
                dve.wait_ge(l_done, s + 1)
                if not first:
                    dve.wait_ge(sum_done, s)
                dve.tensor_tensor(sp_[:, :], z[:, :], zc[:, :], ALU.max).then_inc(sp_done, 1)
                dve.wait_ge(sp_done, s + 1)
                src = sp_[:, :]
                for n in range(5):
                    sh = SBH << n
                    dst = suf[:, n % 2, :]
                    if n >= 1:
                        dve.wait_ge(suf_done, SUF * s + 2 * n)
                    dve.tensor_tensor(dst[:, 0:W - sh], src[:, 0:W - sh], src[:, sh:W], ALU.add).then_inc(suf_done, 1)
                    dve.tensor_copy(dst[:, W - sh:W], src[:, W - sh:W]).then_inc(suf_done, 1)
                    src = dst

            def exponent(s):
                dve.wait_ge(sum_done, s + 1)
                dve.tensor_tensor(zc[:, :], z[:, :], ps[:, SUMB, 0:W], ALU.add).then_inc(t_done, 1)

            def mask(s, first):
                dve.wait_ge(pv_done, NJ * s + NJ)
                if not first:
                    dve.wait_ge(col_done, s)
                dve.tensor_tensor(om[:, :], ps[:, OB, :], k.c("sb_diag"), ALU.mult).then_inc(om_done, 1)

            def early_split(n):
                dve.wait_ge(early_in[n % 2], 16 * (n // 2 + 1))
                if n >= 3:
                    dve.wait_ge(early_mm, n - 2)
                dve.tensor_copy(w_hi[:, n % 3, :], raw[:, n % 2, :]).then_inc(early_hi, 1)
                dve.wait_ge(early_hi, n + 1)
                dve.tensor_tensor(w_lo[:, n % 3, :], raw[:, n % 2, :], w_hi[:, n % 3, :].bitcast(f32),
                                  ALU.subtract).then_inc(early_lo, 1)

            early_split(0)
            early_split(1)
            dve.wait_ge(setup, 48)
            dve.wait_ge(q_copied, S)
            for j in range(NJ):
                scores(0, j, True)
                if j + 2 < NE:
                    early_split(j + 2)
            sums(0, True)
            exponent(0)

            def step(s, first, last=False):
                for j in range(NJ):
                    if j < NPOS:
                        split(s, first, j)
                    if not last:
                        scores(s + 1, j, False)
                if not last:
                    sums(s + 1, False)
                    exponent(s + 1)
                mask(s, first)

            loop(dve, S - 1, step)
            step(S - 1, False, last=True)
            dve.wait_ge(gate_in, 16)
            dve.wait_ge(os_done, S)
            dve.tensor_tensor(gated[:, :, :], osT[:, :, :], gate[:, :, :], ALU.mult).then_inc(gated_done, 1)

        @block.scalar
        def _(act):
            for s in range(S):
                act.wait_ge(q_rows, s + 1)
                act.copy(qbc[:, s, :], ps[:, s % 4, :]).then_inc(q_copied, 1)

            def softplus(s):
                act.wait_ge(zc_done, s + 1)
                act.activation(zc[:, :], zc[:, :], AF.Exp).then_inc(e_done, 1)
                act.wait_ge(e_done, s + 1)
                act.activation(zc[:, :], zc[:, :], AF.Ln, bias=k.c("ones")[:, 0:1]).then_inc(l_done, 1)

            def weights(s, first):
                act.wait_ge(t_done, s + 1)
                if not first:
                    act.wait_ge(pv_done, NJ * s)
                act.activation(a[:, :], zc[:, :], AF.Exp).then_inc(a_done, 1)

            def column(s):
                act.wait_ge(col_done, s + 1)
                act.copy(osT[:, :, bass.ds(s, 1)], ps[:, CB, 0:4].rearrange("p (f o) -> p f o", o=1)).then_inc(os_done, 1)

            def evacuate(s, first, pos):
                kind, n, _ = W_ORDER[pos]
                st = store_slot(kind, n)
                act.wait_ge(mm_done, NPOS * s + pos + 1)
                if first and pos == 0:
                    for e in range(3):
                        act.wait_ge(early_stored[e], 16 * len(range(e, NE, 3)))
                if kind == "mem":
                    if not first or n >= 2:
                        act.wait_ge(stored[st], 16 * (2 * s + n // 2))
                    act.copy(m_stage[:, n % 2, :], ps[:, M_BANK + n % 2, 0:MEM]).then_inc(evac_done, 1)
                    act.wait_ge(evac_done, NPOS * s + pos + 1)
                    act.dma_start(dram_tile(mem_kv, W_MEM * s + n), m_stage[:, n % 2, :]).then_inc(stored[st], 16)
                else:
                    if not first:
                        act.wait_ge(stored[st], 16 * s)
                    act.activation(stage[:, st, :].rearrange("p (c n) -> p c n", c=NCH), ps[:, A_BANK:A_BANK + 3, 0:CH],
                                   AF.Silu if kind == "silu" else AF.Copy).then_inc(evac_done, 1)
                    act.wait_ge(evac_done, NPOS * s + pos + 1)
                    t = AB_Z + s if kind == "silu" else AB_V + W_PLAIN * s + n
                    act.dma_start(dram_tile(ab, t), stage[:, st, :]).then_inc(stored[st], 16)

            for n in range(NE):
                act.wait_ge(early_mm, n + 1)
                if n >= 3:
                    act.wait_ge(early_stored[n % 3], 16 * (n // 3))
                act.copy(stage[:, n % 3, :].rearrange("p (c n) -> p c n", c=NCH),
                         ps[:, 3 * (n % 2):3 * (n % 2) + 3, 0:CH]).then_inc(early_evac, 1)
                act.wait_ge(early_evac, n + 1)
                act.dma_start(ab[early0 + n], stage[:, n % 3, :]).then_inc(early_stored[n % 3], 16)
            softplus(0)
            weights(0, True)

            def step(s, first, last=False):
                for pos in range(NPOS):
                    evacuate(s, first, pos)
                if not last:
                    softplus(s + 1)
                    weights(s + 1, False)
                column(s)

            loop(act, S - 1, step)
            step(S - 1, False, last=True)
            for n in range(3):
                act.wait_ge(stored[n], 16 * S)
            for n in range(3, 5):
                act.wait_ge(stored[n], 32 * S)

        @block.tensor
        def _(pe):
            pe.wait_ge(setup, 48)
            for s in range(S):
                if s >= 4:
                    pe.wait_ge(q_copied, s - 3)
                for f in range(4):
                    last = pe.matmul(ps[:, s % 4, f * 128:f * 128 + 128],
                                     qs[:, f, s:s + 1].broadcast_to((128, 128)), k.c("ident"), start=True, stop=True)
                last.then_inc(q_rows, 1)

            def sums(s, first):
                pe.wait_ge(sp_done, s + 1)
                if not first:
                    pe.wait_ge(t_done, s)
                pe.matmul(ps[:, SUMB, 0:W], k.c("neg_tri"), sp_[:, :], start=True, stop=False)
                pe.wait_ge(suf_done, SUF * s + SUF)
                pe.matmul(ps[:, SUMB, 0:W - SBH], k.c("neg_ones"), suf[:, 0, SBH:W], start=False,
                          stop=True).then_inc(sum_done, 1)

            def product(slot, bank, mov, chunks, width):
                for c in range(chunks):
                    o = ps[:, bank + c, 0:width]
                    for kt in range(KT):
                        x, y = kt * 128, kt * 128 + 128
                        h, l = mov[0][:, kt, c * width:c * width + width], mov[1][:, kt, c * width:c * width + width]
                        pe.matmul(o, w_hi[:, slot, x:y], h, start=(kt == 0), stop=False)
                        pe.matmul(o, w_hi[:, slot, x:y], l, start=False, stop=False)
                        last = pe.matmul(o, w_lo[:, slot, x:y], h, start=False, stop=(kt == KT - 1))
                return last

            def tile(s, first, pos):
                kind, _, slot = W_ORDER[pos]
                pe.wait_ge(lo_done, NPOS * s + pos + 1)
                v = at(s, first, pos, back(BANK, pos))
                if v is not None:
                    pe.wait_ge(evac_done, v)
                else:
                    pe.wait_ge(early_evac, NE)
                if kind == "mem":
                    mov, chunks, width = (m_hi, m_lo), 1, MEM
                else:
                    mov, chunks, width = (hi, lo), NCH, CH
                product(slot, BANK[pos], mov, chunks, width).then_inc(mm_done, 1)

            def values(s, j, first):
                if j == 0:
                    pe.wait_ge(a_done, s + 1)
                    if not first:
                        pe.wait_ge(om_done, s)
                pe.wait_ge(v_in[j % 2], 64 * (NJ // 2 * s + j // 2 + 1))
                for g in range(G):
                    last = pe.matmul(ps[32 * g:32 * g + 32, OB, :], a[:, j * 32:j * 32 + 32],
                                     vp[:, j % 2, g * 512:(g + 1) * 512], start=(j == 0), stop=(j == NJ - 1))
                last.then_inc(pv_done, 1)

            def columns(s, first):
                pe.wait_ge(om_done, s + 1)
                for f in range(4):
                    last = pe.matmul(ps[:, CB, f:f + 1], om[:, f * 128:f * 128 + 128], k.c("ones")[:, 0:1],
                                     start=True, stop=True)
                last.then_inc(col_done, 1)

            pe.wait_ge(q_copied, S)
            for n in range(NE):
                pe.wait_ge(early_lo, n + 1)
                if n >= 2:
                    pe.wait_ge(early_evac, n - 1)
                product(n % 3, 3 * (n % 2), (hi, lo), NCH, CH).then_inc(early_mm, 1)
            pe.wait_ge(early_evac, NE)
            sums(0, True)

            def step(s, first, last=False):
                for j in range(NJ):
                    if j < NPOS:
                        tile(s, first, j)
                    values(s, j, first)
                if not last:
                    sums(s + 1, False)
                if not first:
                    pe.wait_ge(os_done, s)
                columns(s, first)

            loop(pe, S - 1, step)
            step(S - 1, False, last=True)


def gdn_front(k, ab, conv, conv_w, conv_buf, conv_s):
    k.recycle()
    nc, ALU, AF, f32, ps = k.nc, k.ALU, k.AF, k.f32, k.ps
    N, NQK, TAPS, GROUP = 3 * GH, 2 * GH, 4, 2
    OUTS = 4
    HALVES = T // 512
    with ExitStack() as ctx:
        def sb(name, shape):
            return ctx.enter_context(nc.sbuf_tensor(k.name(name), shape, f32))

        def sem(name):
            return k.semaphore(k.name(name))

        x = sb("conv_x", [128, N, TAPS - 1 + NT])
        new, buf = sb("conv_new", [128, N, S]), sb("conv_buf", [128, N, S, TAPS - 1])
        w = sb("conv_w", [128, N, TAPS])
        diag = sb("taps", [128, GH, TAPS, 128])
        acc = sb("conv_acc", [128, 2, T])
        term, acc_s = sb("conv_term", [128, N, S]), sb("conv_acc_s", [128, N, S])
        y = sb("silu", [128, N, NT])
        tail = sb("conv_tail", [128, N, S, TAPS - 1])
        r, out = sb("l2_r", [128, 2, NT]), sb("l2_out", [128, OUTS, NT])
        x_in = [sem(f"x_in{g}") for g in range(N // GROUP)]
        small_in, zeroed, diag_done, chain, conv_done, pe_conv_done, chain_s, tail_done = (
            sem(n) for n in ("small_in", "zeroed", "diag", "chain", "conv", "pe_conv", "chain_s", "tail"))
        silu_done, silu_v_done, silu_s_done, sq_done, ss_done, log_done, r_done, y_done, v_stored, tail_stored = (
            sem(n) for n in ("silu", "silu_v", "silu_s", "sq", "ss", "log", "r", "y", "v_st", "tail_st"))
        stored = [sem(f"st{u}") for u in range(OUTS)]
        block = ctx.enter_context(nc.Block())
        order = [g for pair in zip(range(NQK // GROUP), range(NQK // GROUP, N // GROUP)) for g in pair]
        order += [g for g in range(N // GROUP) if g not in order]

        def sums(t):
            b = 4 if t % 2 == 0 else 0
            return ps[:, b:b + NCH, 0:CH]

        def conv_banks(i):
            return ps[:, 2 * (i % 2):2 * (i % 2) + HALVES, :]

        @block.sync
        def _(sp):
            sp.dma_start(w[:, :, :], conv_w).then_inc(small_in, 16)
            for n, g in enumerate(order):
                a = AB_QKV + GROUP * g
                sp.dma_start(x[:, GROUP * g:GROUP * g + GROUP, TAPS - 1:TAPS - 1 + T],
                             ab[a:a + GROUP, :, 0:T].rearrange("t p n -> p t n")).then_inc(x_in[g], 16)
                if n == 0:
                    sp.dma_start(new[:, :, :], ab[AB_QKV:AB_QKV + N, :, T:NT].rearrange("t p n -> p t n")).then_inc(small_in, 16)
                    sp.dma_start(buf[:, :, :, :], conv_buf.rearrange("t p s j -> p t s j")).then_inc(small_in, 16)
            sp.wait_ge(tail_done, 1)
            sp.dma_start(conv_s.rearrange("t p s j -> p t s j"), tail[:, :, :, :]).then_inc(tail_stored, 16)
            sp.wait_ge(silu_v_done, GH)
            sp.wait_ge(silu_s_done, 1)
            sp.dma_start(conv[NQK:N].rearrange("t p n -> p t n"), y[:, NQK:N, :]).then_inc(v_stored, 16)
            for t in range(NQK):
                sp.wait_ge(y_done, t + 1)
                sp.dma_start(conv[t], out[:, t % OUTS, :]).then_inc(stored[t % OUTS], 16)
            for u in range(OUTS):
                sp.wait_ge(stored[u], 16 * (NQK // OUTS))
            sp.wait_ge(v_stored, 16)
            sp.wait_ge(tail_stored, 16)

        @block.gpsimd
        def _(pool):
            pool.memset(x[:, :, 0:TAPS - 1], 0.0).then_inc(zeroed, 1)
            pool.wait_ge(small_in, 48)
            for i in range(GH):
                for j in range(TAPS):
                    last = pool.tensor_tensor(diag[:, i, j, :], k.c("ident"),
                                              w[:, NQK + i, j:j + 1].broadcast_to((128, 128)), ALU.mult)
                last.then_inc(diag_done, 1)

        @block.tensor
        def _(pe):
            pe.wait_ge(zeroed, 1)
            for i in range(GH):
                t = NQK + i
                pe.wait_ge(x_in[t // GROUP], 16)
                pe.wait_ge(diag_done, i + 1)
                if i >= 2:
                    pe.wait_ge(silu_v_done, i - 1)
                for b in range(HALVES):
                    for j in range(TAPS):
                        last = pe.matmul(ps[:, 2 * (i % 2) + b, :], diag[:, i, j, :], x[:, t, 512 * b + j:512 * b + j + 512],
                                         start=(j == 0), stop=(j == TAPS - 1))
                last.then_inc(pe_conv_done, 1)
            for t in range(NQK):
                pe.wait_ge(sq_done, t + 1)
                if t == 1:
                    pe.wait_ge(silu_v_done, GH)
                if t >= 2:
                    pe.wait_ge(log_done, t - 1)
                for c in range(NCH):
                    last = pe.matmul(sums(t)[:, c], k.c("ones"), x[:, t, c * CH:c * CH + CH], start=True, stop=True)
                last.then_inc(ss_done, 1)

        @block.vector
        def _(dve):
            dve.wait_ge(zeroed, 1)
            dve.wait_ge(small_in, 48)

            def samples():
                for j in range(TAPS):
                    src = buf[:, :, :, j] if j < TAPS - 1 else new[:, :, :]
                    ws = w[:, :, j:j + 1].broadcast_to((128, N, S))
                    if j == 0:
                        dve.tensor_tensor(acc_s[:, :, :], src, ws, ALU.mult).then_inc(chain_s, 1)
                        continue
                    dve.wait_ge(chain_s, 2 * j - 1)
                    dve.tensor_tensor(term[:, :, :], src, ws, ALU.mult).then_inc(chain_s, 1)
                    dve.wait_ge(chain_s, 2 * j)
                    dve.tensor_tensor(acc_s[:, :, :], acc_s[:, :, :], term[:, :, :], ALU.add).then_inc(chain_s, 1)
                dve.tensor_copy(tail[:, :, :, 0:TAPS - 2], buf[:, :, :, 1:TAPS - 1])
                dve.tensor_copy(tail[:, :, :, TAPS - 2], new[:, :, :]).then_inc(tail_done, 1)

            for t in range(NQK):
                dve.wait_ge(x_in[t // GROUP], 16)
                if t >= 2:
                    dve.wait_ge(silu_done, t - 1)
                a = acc[:, t % 2, :]
                dve.tensor_scalar(a, x[:, t, 0:T], w[:, t, 0:1], None, ALU.mult).then_inc(chain, 1)
                for j in range(1, TAPS):
                    dve.wait_ge(chain, (TAPS - 1) * t + j)
                    dve.scalar_tensor_tensor(a, x[:, t, j:j + T], w[:, t, j:j + 1], a, ALU.mult,
                                             ALU.add).then_inc(chain if j < TAPS - 1 else conv_done, 1)
                if t == 0:
                    samples()
            for t in range(NQK):
                dve.wait_ge(r_done, t + 1)
                if t >= OUTS:
                    dve.wait_ge(stored[t % OUTS], 16 * (t // OUTS))
                dve.scalar_tensor_tensor(out[:, t % OUTS, :], y[:, t, :], GDN_SCALE if t < GH else 1.0, r[:, t % 2, :],
                                         ALU.mult, ALU.mult).then_inc(y_done, 1)

        @block.scalar
        def _(act):
            for t in range(NQK):
                act.wait_ge(conv_done, t + 1)
                act.activation(y[:, t, 0:T], acc[:, t % 2, :], AF.Silu).then_inc(silu_done, 1)
                if t == 0:
                    act.wait_ge(chain_s, 2 * TAPS - 1)
                    act.activation(y[:, :, T:NT], acc_s[:, :, :], AF.Silu).then_inc(silu_s_done, 1)
                    act.wait_ge(silu_s_done, 1)
                act.wait_ge(silu_done, t + 1)
                act.activation(x[:, t, 0:NT], y[:, t, :], AF.Square).then_inc(sq_done, 1)
                if t % 2:
                    i = t // 2
                    act.wait_ge(pe_conv_done, i + 1)
                    act.activation(y[:, NQK + i, 0:T].rearrange("p (b n) -> p b n", b=HALVES), conv_banks(i),
                                   AF.Silu).then_inc(silu_v_done, 1)
            act.preload_act_table_set("natural_log_exp_and_others")
            for t in range(NQK):
                rr = r[:, t % 2, :]
                act.wait_ge(ss_done, t + 1)
                if t >= 2:
                    act.wait_ge(y_done, t - 1)
                act.activation(rr.rearrange("p (c n) -> p c n", c=NCH), sums(t), AF.Ln, bias=k.c("eps")).then_inc(log_done, 1)
                act.wait_ge(log_done, t + 1)
                act.activation(rr, rr, AF.Exp, scale=-0.5).then_inc(r_done, 1)


def gdn(k, ab, conv, og, gains, a_log, dt_bias, state_in, state_p, state_s):
    nc, ALU, AF, f32, ps = k.nc, k.ALU, k.AF, k.f32, k.ps
    NG = NCK * GH
    NP = 2 * GH
    with ExitStack() as ctx:
        def sb(name, shape):
            return ctx.enter_context(nc.sbuf_tensor(k.name(name), shape, f32))

        beta = sb("beta", [128, NCK + 1, GH])
        cols = sb("cols", [128, 4, NG])
        gs = sb("gs", [128, 2, GH * S])
        w_all, u_all, attn_all, qe_all, kd_all = (sb(n, [128, NG, 128]) for n in ("w", "u", "attn", "qe", "kd"))
        with nc.sbuf_tensor(k.name("gc_rows"), [128, NG, 128], f32) as gc_rows:
            gdn_gates(k, ab, a_log, dt_bias, beta, cols, gs, gc_rows)
            gdn_inverse(k, conv, beta, cols, gc_rows, w_all, u_all, attn_all, qe_all, kd_all)
        gdn_states(k, conv, og, gains, ab, cols, gs, state_in, state_p, state_s, w_all, u_all, attn_all, qe_all,
                   kd_all)


def gdn_gates(k, ab, a_log, dt_bias, beta, cols, gs, gc_rows):
    k.recycle()
    nc, ALU, AF, f32, ps = k.nc, k.ALU, k.AF, k.f32, k.ps
    NG, NTT = NCK * GH, NCK + 1
    with ExitStack() as ctx:
        def sb(name, shape):
            return ctx.enter_context(nc.sbuf_tensor(k.name(name), shape, f32))

        def sem(name):
            return k.semaphore(k.name(name))

        raw = sb("gates_raw", [8, NT])
        al, db = sb("a_log_rows", [128, GH]), sb("dt_rows", [128, GH])
        gt = sb("gates", [128, NTT, 8])
        x, e, u, ln_u, rest, ru, g = (sb(n, [128, NTT, GH]) for n in ("sx", "se", "su", "sl", "sd", "sr", "sg"))
        eg_s = sb("eg_s", [S, GH])
        last_less = sb("last_less", [128, NG])
        sel = sb("sel", [S, 2, GH, S])
        (loaded, zeroed, transposed, gt_done, x_done, clip_done, e_done, u_done, ru_done, rest_done, rest2_done,
         ln_done, log1p_done, sp_done, al_done, g_done, sums_done, row_done, row_copied, c0_done, c1_done, c2_done,
         c3_done, c1b_done, beta_done, eg_done, sel_done, sel_sum, gs_done) = (
            sem(n) for n in ("loaded", "zeroed", "transposed", "gt", "x", "clip", "e", "u", "ru", "rest", "rest2",
                             "ln", "log1p", "sp", "al", "g", "sums", "row", "row_copied", "c0", "c1", "c2", "c3",
                             "c1b", "beta", "eg", "sel", "sel_sum", "gs"))
        block = ctx.enter_context(nc.Block())
        rows = lambda v: v[:, None, :].broadcast_to((128, NTT, GH))
        flat = lambda v: v[:, 0:NCK, :].rearrange("p t h -> p (t h)")

        @block.sync
        def _(sp):
            sp.dma_start(raw[:, :], ab[AB_GATES][0:8, :]).then_inc(loaded, 16)
            sp.dma_start(al[:, :], a_log.broadcast_to((128, GH))).then_inc(loaded, 16)
            sp.dma_start(db[:, :], dt_bias.broadcast_to((128, GH))).then_inc(loaded, 16)

        @block.gpsimd
        def _(pool):
            pool.memset(gt[:, NCK, :], 0.0).then_inc(zeroed, 1)

        @block.tensor
        def _(pe):
            pe.wait_ge(loaded, 48)
            for t in range(NTT):
                n = min(128, NT - 128 * t)
                last = pe.transpose(ps[0:n, 0, 8 * t:8 * t + 8], raw[:, 128 * t:128 * t + n], k.c("ident")[0:8, 0:8])
            last.then_inc(transposed, 1)
            pe.wait_ge(g_done, 1)
            pe.matmul(ps[:, 1, 0:NG], k.c("tri"), flat(g), start=True, stop=True)
            pe.matmul(ps[:, 2, 0:NG], k.c("ones"), flat(g), start=True, stop=True).then_inc(sums_done, 1)
            for n in range(NG):
                if n >= 16 and n % 4 == 0:
                    pe.wait_ge(row_copied, n // 4 - 3)
                last = pe.matmul(ps[:, 4 + n // 4 % 4, n % 4 * 128:n % 4 * 128 + 128],
                                 g[:, n // GH, n % GH:n % GH + 1].broadcast_to((128, 128)), k.c("tri"),
                                 start=True, stop=True)
                if n % 4 == 3:
                    last.then_inc(row_done, 1)
            pe.wait_ge(sel_done, 2)
            pe.matmul(ps[:, 3, 0:2 * GH * S], k.c("ones")[0:S, :], sel[:, :, :, :].rearrange("s a h t -> s (a h t)"),
                      start=True, stop=True).then_inc(sel_sum, 1)

        @block.vector
        def _(dve):
            dve.wait_ge(transposed, 1)
            dve.wait_ge(zeroed, 1)
            dve.tensor_copy(gt[:, 0:NCK, :], ps[:, 0, 0:8 * NCK].rearrange("p (t h) -> p t h", h=8)).then_inc(gt_done, 1)
            dve.tensor_copy(gt[0:S, NCK, :], ps[0:S, 0, 8 * NCK:8 * NCK + 8]).then_inc(gt_done, 1)
            dve.wait_ge(gt_done, 2)
            dve.tensor_tensor(x[:, :, :], gt[:, :, 0:GH], rows(db), ALU.add).then_inc(x_done, 1)
            dve.wait_ge(x_done, 1)
            dve.tensor_scalar(e[:, :, :], x[:, :, :], CLIP, None, ALU.min).then_inc(clip_done, 1)
            dve.wait_ge(e_done, 1)
            dve.tensor_scalar(u[:, :, :], e[:, :, :], 1.0, None, ALU.add).then_inc(u_done, 1)
            dve.wait_ge(u_done, 1)
            dve.scalar_tensor_tensor(rest[:, :, :], u[:, :, :], -1.0, e[:, :, :], ALU.add, ALU.subtract).then_inc(rest_done, 1)
            dve.reciprocal(ru[:, :, :], u[:, :, :]).then_inc(ru_done, 1)
            dve.wait_ge(rest_done, 1)
            dve.wait_ge(ru_done, 1)
            dve.tensor_tensor(rest[:, :, :], rest[:, :, :], ru[:, :, :], ALU.mult).then_inc(rest2_done, 1)
            dve.wait_ge(rest2_done, 1)
            dve.wait_ge(ln_done, 1)
            dve.tensor_tensor(ln_u[:, :, :], ln_u[:, :, :], rest[:, :, :], ALU.subtract).then_inc(log1p_done, 1)
            dve.wait_ge(log1p_done, 1)
            dve.tensor_tensor(x[:, :, :], x[:, :, :], ln_u[:, :, :], ALU.max).then_inc(sp_done, 1)
            dve.wait_ge(sp_done, 1)
            dve.wait_ge(al_done, 1)
            dve.scalar_tensor_tensor(g[:, :, :], x[:, :, :], -1.0, rows(al), ALU.mult, ALU.mult).then_inc(g_done, 1)
            dve.wait_ge(sums_done, 1)
            dve.tensor_copy(cols[:, 0, :], ps[:, 1, 0:NG]).then_inc(c0_done, 1)
            dve.wait_ge(c0_done, 1)
            dve.tensor_tensor(last_less[:, :], ps[:, 2, 0:NG], cols[:, 0, :], ALU.subtract).then_inc(c2_done, 1)
            dve.wait_ge(eg_done, 1)
            dve.wait_ge(beta_done, 1)
            eye = k.c("ident")[0:S, None, 0:S].broadcast_to((S, GH, S))
            dve.tensor_tensor(sel[:, 0], eye, eg_s[:, :, None].broadcast_to((S, GH, S)), ALU.mult).then_inc(sel_done, 1)
            dve.tensor_tensor(sel[:, 1], eye, beta[0:S, NCK, :, None].broadcast_to((S, GH, S)),
                              ALU.mult).then_inc(sel_done, 1)
            dve.wait_ge(c1_done, 1)
            dve.tensor_tensor(cols[:, 1, :], cols[:, 1, :], flat(beta), ALU.mult).then_inc(c1b_done, 1)
            dve.wait_ge(sel_sum, 1)
            dve.tensor_copy(gs[:, :, :], ps[:, 3, 0:2 * GH * S].rearrange("p (a n) -> p a n", a=2)).then_inc(gs_done, 1)

        @block.scalar
        def _(act):
            act.wait_ge(loaded, 48)
            act.activation(al[:, :], al[:, :], AF.Exp).then_inc(al_done, 1)
            act.wait_ge(clip_done, 1)
            act.activation(e[:, :, :], e[:, :, :], AF.Exp).then_inc(e_done, 1)
            act.wait_ge(u_done, 1)
            act.activation(ln_u[:, :, :], u[:, :, :], AF.Ln).then_inc(ln_done, 1)
            act.wait_ge(gt_done, 2)
            act.activation(beta[:, :, :], gt[:, :, GH:8], AF.Sigmoid).then_inc(beta_done, 1)
            act.wait_ge(g_done, 1)
            act.activation(eg_s[:, :], g[0:S, NCK, :], AF.Exp).then_inc(eg_done, 1)
            act.wait_ge(c0_done, 1)
            act.activation(cols[:, 1, :], cols[:, 0, :], AF.Exp).then_inc(c1_done, 1)
            act.wait_ge(c2_done, 1)
            act.activation(cols[:, 2, :], last_less[:, :], AF.Exp).then_inc(c3_done, 1)
            act.activation(cols[:, 3, :], ps[:, 2, 0:NG], AF.Exp).then_inc(c3_done, 1)
            for n in range(NG // 4):
                act.wait_ge(row_done, n + 1)
                act.copy(gc_rows[:, 4 * n:4 * n + 4, :].rearrange("p a n -> p (a n)"),
                         ps[:, 4 + n % 4, :]).then_inc(row_copied, 1)


def gdn_inverse(k, conv, beta, cols, gc_rows, w_all, u_all, attn_all, qe_all, kd_all):
    k.recycle()
    nc, ALU, AF, f32, ps = k.nc, k.ALU, k.AF, k.f32, k.ps
    NP = 2 * GH
    LEVELS = 7
    with ExitStack() as ctx:
        def sb(name, shape):
            return ctx.enter_context(nc.sbuf_tensor(k.name(name), shape, f32))

        def sem(name):
            return k.semaphore(k.name(name))

        q, kk, v = (sb(n, [128, GH, 2 * CHUNK]) for n in ("gq", "gk", "gv"))
        col = sb("gcol", [128, 4, NP])
        dec, er = sb("decay", [128, NP, 128]), sb("decay_rows", [128, NP, 128])
        a0, t_, tt, m1 = (sb(n, [128, NP, 128]) for n in ("a0", "t", "tt", "m1"))
        bm = sb("beta_mask", [128, 2, NP, 128])
        kbe, vb = sb("kbe", [128, NP, 128]), sb("vb", [128, NP, 128])
        loaded, col_done, diff_done, clip_done, exp_done, dec_done = (
            sem(n) for n in ("loaded", "col", "diff", "clip", "exp", "dec"))
        kk_done, qk_done, a0_done, attn_done = sem("kk"), sem("qk"), sem("a0d"), sem("attn")
        bm_done, p1_done, m1_done, p2_done, p3_done, t_done, tt_done = (
            sem(n) for n in ("bm", "p1", "m1d", "p2", "p3", "td", "ttd"))
        kt_done, vt_done, kbe_done, kd_done, vb_done, w_done, u_done, wc_done, uc_done, er_done, qe_done = (
            sem(n) for n in ("kt", "vt", "kbed", "kd", "vbd", "w", "u", "wc", "uc", "er", "qe"))

        def prob(x, j):
            return x[:, j % GH, (j // GH) * CHUNK:(j // GH + 1) * CHUNK]

        def pairs(x):
            return x[:, :, :].rearrange("p h (c n) -> p c h n", c=2)

        def four(x):
            return x.rearrange("p (c h) n -> p c h n", c=2)

        def bank(b, j):
            return ps[:, 2 * b + j // 4, j % 4 * 128:j % 4 * 128 + 128]

        def banks(b):
            return ps[:, 2 * b:2 * b + 2, :].rearrange("p b (h n) -> p (b h) n", n=128)

        def part(half):
            return slice(NP // 2 * half, NP // 2 * (half + 1))

        def half_bank(b, half):
            return ps[:, 2 * b + half, :].rearrange("p (h n) -> p h n", n=128)

        def half_mask(m):
            return m[:, None, :].broadcast_to((128, NP // 2, 128))

        def nth(level, half):
            return 2 * level + half + 1

        def bc(c):
            return c[:, :, None].broadcast_to((128, NP, 128))

        def mask(m):
            return m[:, None, :].broadcast_to((128, NP, 128))

        level = [k.c("levels")[:, 128 * n:128 * n + 128] for n in range(LEVELS)]
        block = ctx.enter_context(nc.Block())

        @block.sync
        def _(sp):
            def body(i, first):
                tokens = bass.ds(2 * CHUNK * i if first else sp.snap(2 * CHUNK * i), 2 * CHUNK)
                if not first:
                    sp.wait_ge(vb_done, i)
                    sp.wait_ge(qe_done, i)
                    sp.wait_ge(kd_done, i)
                for j, dst in enumerate((q, kk, v)):
                    sp.dma_start(dst[:, :, :], conv[GH * j:GH * j + GH, :, tokens]
                                 .rearrange("h p n -> p h n")).then_inc(loaded, 16)

            loop(sp, NCK // 2, body)

        @block.vector
        def _(dve):
            def body(i, first):
                span = bass.ds(NP * i, NP)
                if not first:
                    dve.wait_ge(wc_done, i)
                    dve.wait_ge(uc_done, i)
                dve.tensor_copy(col[:, 0:3, :], cols[:, 0:3, span]).then_inc(col_done, 1)
                dve.tensor_copy(col[:, 3, :], beta[:, bass.ds(2 * i, 2), :].rearrange("p c h -> p (c h)")).then_inc(col_done, 1)
                dve.wait_ge(col_done, 2 * i + 2)
                dve.tensor_tensor(dec[:, :, :], gc_rows[:, span, :], bc(col[:, 0, :]), ALU.subtract).then_inc(diff_done, 1)
                dve.wait_ge(diff_done, i + 1)
                dve.tensor_scalar(dec[:, :, :], dec[:, :, :], 0.0, None, ALU.min).then_inc(clip_done, 1)
                dve.wait_ge(exp_done, i + 1)
                dve.tensor_tensor(dec[:, :, :], dec[:, :, :], mask(k.c("tri")), ALU.mult).then_inc(dec_done, 1)
                dve.wait_ge(dec_done, i + 1)
                dve.wait_ge(kk_done, i + 1)
                dve.tensor_tensor(a0[:, :, :], banks(0), dec[:, :, :], ALU.mult).then_inc(a0_done, 1)
                dve.wait_ge(kt_done, i + 1)
                dve.tensor_tensor(kbe[:, :, :], banks(2), bc(col[:, 1, :]), ALU.mult).then_inc(kbe_done, 1)
                dve.tensor_tensor(kd_all[:, span, :], banks(2), bc(col[:, 2, :]), ALU.mult).then_inc(kd_done, 1)

                def later():
                    dve.wait_ge(qk_done, i + 1)
                    dve.tensor_tensor(attn_all[:, span, :], banks(1), dec[:, :, :], ALU.mult).then_inc(attn_done, 1)
                    dve.wait_ge(er_done, i + 1)
                    dve.tensor_tensor(four(qe_all[:, span, :]), pairs(q), four(er[:, :, :]), ALU.mult).then_inc(qe_done, 1)

                for n in range(LEVELS):
                    dve.wait_ge(bm_done, LEVELS * i + n + 1)
                    for half in range(2):
                        j = part(half)
                        dve.wait_ge(p1_done, nth(LEVELS * i + n, half))
                        dve.tensor_tensor(m1[:, j, :], half_bank(0, half), bm[:, n % 2, j], ALU.mult).then_inc(m1_done, 1)
                    for half in range(2):
                        j = part(half)
                        if n == 0:
                            dve.wait_ge(m1_done, nth(LEVELS * i, half))
                            dve.tensor_tensor(t_[:, j, :], half_mask(k.c("ident")), m1[:, j, :],
                                              ALU.subtract).then_inc(t_done, 1)
                        elif n < LEVELS - 1:
                            dve.wait_ge(p2_done, nth((LEVELS - 2) * i + n - 1, half))
                            dve.wait_ge(t_done, nth((LEVELS - 1) * i + n - 1, half))
                            dve.tensor_tensor(t_[:, j, :], t_[:, j, :], half_bank(1, half), ALU.subtract).then_inc(t_done, 1)
                    for half in range(2):
                        j = part(half)
                        dve.wait_ge(p3_done, nth(LEVELS * i + n, half))
                        if n == 0:
                            dve.tensor_tensor(tt[:, j, :], half_mask(k.c("ident")), half_bank(2, half),
                                              ALU.subtract).then_inc(tt_done, 1)
                        else:
                            dve.wait_ge(tt_done, nth(LEVELS * i + n - 1, half))
                            dve.tensor_tensor(tt[:, j, :], tt[:, j, :], half_bank(2, half), ALU.subtract).then_inc(tt_done, 1)
                    if n == 0:
                        later()

            loop(dve, NCK // 2, body)

        @block.gpsimd
        def _(pool):
            def body(i, first):
                pool.wait_ge(col_done, 2 * i + 2)
                for n in range(LEVELS):
                    if n >= 2 or not first:
                        pool.wait_ge(m1_done, nth(LEVELS * i + n - 2, 1))
                    pool.tensor_tensor(bm[:, n % 2], mask(level[n]), bc(col[:, 3, :]), ALU.mult).then_inc(bm_done, 1)

            loop(pool, NCK // 2, body)

        @block.scalar
        def _(act):
            def body(i, first):
                span = bass.ds(NP * i, NP)
                act.wait_ge(clip_done, i + 1)
                act.activation(dec[:, :, :], dec[:, :, :], AF.Exp).then_inc(exp_done, 1)
                if not first:
                    act.wait_ge(qe_done, i)
                act.activation(er[:, :, :], gc_rows[:, span, :], AF.Exp).then_inc(er_done, 1)
                act.wait_ge(col_done, 2 * i + 2)
                act.wait_ge(vt_done, i + 1)
                for j in range(NP):
                    last = act.activation(vb[:, j, :], bank(3, j), AF.Copy, scale=col[:, 3, j:j + 1])
                last.then_inc(vb_done, 1)
                act.wait_ge(w_done, i + 1)
                act.copy(w_all[:, span, :], banks(3)).then_inc(wc_done, 1)
                act.wait_ge(u_done, i + 1)
                act.copy(u_all[:, span, :], banks(1)).then_inc(uc_done, 1)

            loop(act, NCK // 2, body)

        @block.tensor
        def _(pe):
            def eight(b, lhs, rhs, done, transpose=False):
                for j in range(NP):
                    if transpose:
                        last = pe.transpose(bank(b, j), lhs(j), k.c("ident"))
                    else:
                        last = pe.matmul(bank(b, j), lhs(j), rhs(j), start=True, stop=True)
                last.then_inc(done, 1)

            def four_of(half, b, lhs, rhs, done):
                for j in range(4 * half, 4 * half + 4):
                    last = pe.matmul(bank(b, j), lhs(j), rhs(j), start=True, stop=True)
                last.then_inc(done, 1)

            def body(i, first):
                of = lambda x: (lambda j: x[:, j, :])
                inp = lambda x: (lambda j: prob(x, j))
                eye = lambda j: k.c("ident")
                pe.wait_ge(loaded, 48 * (i + 1))
                eight(0, inp(kk), inp(kk), kk_done)
                eight(2, inp(kk), None, kt_done, True)
                if not first:
                    pe.wait_ge(uc_done, i)
                    pe.wait_ge(wc_done, i)
                eight(1, inp(kk), inp(q), qk_done)
                eight(3, inp(v), None, vt_done, True)
                pe.wait_ge(a0_done, i + 1)
                for n in range(LEVELS):
                    for half in range(2):
                        if n >= 1:
                            pe.wait_ge(t_done, nth((LEVELS - 1) * i + n - 1, half))
                        four_of(half, 0, of(a0), eye if n == 0 else of(t_), p1_done)
                    for half in range(2):
                        pe.wait_ge(m1_done, nth(LEVELS * i + n, half))
                        if n >= 1:
                            pe.wait_ge(tt_done, nth(LEVELS * i + n - 1, half))
                        if 1 <= n < LEVELS - 1:
                            if n == 1 and half == 0:
                                pe.wait_ge(attn_done, i + 1)
                            four_of(half, 1, of(tt), of(m1), p2_done)
                    if n == 0:
                        pe.wait_ge(kd_done, i + 1)
                        pe.wait_ge(kbe_done, i + 1)
                    for half in range(2):
                        four_of(half, 2, of(m1), eye if n == 0 else of(tt), p3_done)
                pe.wait_ge(tt_done, nth(LEVELS * i + LEVELS - 1, 1))
                pe.wait_ge(vb_done, i + 1)
                eight(3, of(kbe), of(tt), w_done)
                eight(1, of(tt), of(vb), u_done)

            loop(pe, NCK // 2, body)


def gdn_states(k, conv, og, gains, ab, cols, gs, state_in, state_p, state_s, w_all, u_all, attn_all, qe_all, kd_all):
    k.recycle()
    nc, ALU, AF, f32, ps = k.nc, k.ALU, k.AF, k.f32, k.ps
    assert NCK == 2 * GH
    with ExitStack() as ctx:
        def sb(name, shape):
            return ctx.enter_context(nc.sbuf_tensor(k.name(name), shape, f32))

        def sem(name):
            return k.semaphore(k.name(name))

        s = sb("state", [128, 2, GH, 128])
        se = sb("state_decayed", [128, GH, 128])
        vn = sb("v_new", [128, 2, GH, 128])
        gate = sb("gdn_gate", [128, GH, NT])
        sq, r, y, out = (sb(n, [128, 2, GH, 128]) for n in ("gn_sq", "gn_r", "gn_y", "gn_out"))
        st = sb("sample_states", [128, GH, S, 128])
        qkv = sb("sample_qkv", [128, 3 * GH, S])
        kb, vb = sb("sample_k_scaled", [128, GH, S]), sb("sample_v_scaled", [128, GH, S])
        s_done, ws_done, vn_done, ds_done, se_done, o_done, p_stored, gate_in = (
            sem(n) for n in ("s", "ws", "vn", "ds", "se", "o", "p_st", "gate_in"))
        sq_done, ss_done, log_done, r_done, y_done, out_done = (sem(n) for n in ("sq", "ss", "log", "r", "y", "out"))
        qkv_in, scaled_done, decayed, rows_done, st_done, so_done, st_stored = (
            sem(n) for n in ("qkv_in", "scaled", "decayed", "rows", "st", "so", "st_st"))
        st_in = [sem(f"st_in{h}") for h in range(GH)]
        out_stored = [sem("out_st0"), sem("out_st1")]
        samples_out = ps[:, 4, 0:GH * S].rearrange("p (h s) -> p h s", h=GH)

        def width(c):
            return CHUNK if c < NCK else S

        def chunk_out(c):
            return ps[:, 1 + c % 2, :].rearrange("p (h n) -> p h n", h=GH) if c < NCK else samples_out

        def sums(c):
            return ps[:, 7, 0:GH * width(c)].rearrange("p (h n) -> p h n", h=GH)

        block = ctx.enter_context(nc.Block())

        @block.sync
        def _(sp):
            def store_out(c):
                sp.wait_ge(out_done, c + 1)
                sp.dma_start(og[GH:2 * GH, :, CHUNK * c:CHUNK * c + width(c)].rearrange("t p n -> p t n"),
                             out[:, c % 2, :, 0:width(c)]).then_inc(out_stored[c % 2], 16)

            def store_states(h):
                sp.wait_ge(st_done, 2 * h + 2)
                sp.dma_start(state_s[:, h].rearrange("s p n -> p s n"), st[:, h]).then_inc(st_stored, 16)

            sp.dma_start(qkv[:, :, :], conv[:, :, T:NT].rearrange("t p n -> p t n")).then_inc(qkv_in, 16)
            sp.dma_start(st[:, 0], state_in[:, 0].rearrange("s p n -> p s n")).then_inc(st_in[0], 16)
            sp.dma_start(gate[:, :, :], ab[AB_GZ:AB_GZ + GH].rearrange("t p n -> p t n")).then_inc(gate_in, 16)
            for h in range(1, GH):
                sp.dma_start(st[:, h], state_in[:, h].rearrange("s p n -> p s n")).then_inc(st_in[h], 16)
            for c in range(NCK):
                if c >= 1:
                    store_out(c - 1)
                if c % 2 and c > 1:
                    store_states(c // 2 - 1)
            store_states(GH - 1)
            sp.wait_ge(s_done, NCK + 1)
            sp.dma_start(state_p, s[:, NCK % 2]).then_inc(p_stored, 16)
            store_out(NCK - 1)
            store_out(NCK)
            sp.wait_ge(p_stored, 16)
            sp.wait_ge(st_stored, 16 * GH)
            sp.wait_ge(out_stored[0], 16 * (NCK // 2 + 1))
            sp.wait_ge(out_stored[1], 16 * (NCK // 2))

        @block.tensor
        def _(pe):
            def squares_sum(c):
                pe.wait_ge(sq_done, c + 1)
                if c >= 1:
                    pe.wait_ge(log_done, c)
                pe.matmul(sums(c), k.c("ones"), sq[:, c % 2, :, 0:width(c)], start=True, stop=True).then_inc(ss_done, 1)

            def new_values(h):
                if h == 0:
                    pe.wait_ge(scaled_done, 3)
                else:
                    pe.wait_ge(st_done, 2 * h)
                pe.wait_ge(st_in[h], 16)
                for n in range(S):
                    o = ps[:, 5 + n // 4, n % 4 * 128:n % 4 * 128 + 128]
                    pe.matmul(o, vb[:, h, n:n + 1].broadcast_to((128, 128)), k.c("ident"), start=True, stop=False)
                    last = pe.matmul(o, kb[:, h, n:n + 1].broadcast_to((128, 128)), st[:, h, n, :], start=False, stop=True)
                last.then_inc(rows_done, 1)

            def samples_output(h, half):
                pe.wait_ge(st_done, 2 * h + half + 1)
                for n in range(S // 2 * half, S // 2 * (half + 1)):
                    last = pe.matmul(ps[:, 4, S * h + n:S * h + n + 1], st[:, h, n, :], qkv[:, h, n:n + 1],
                                     start=True, stop=True)
                last.then_inc(so_done, 1)

            for c in range(NCK):
                h = c // 2
                pe.wait_ge(s_done, c + 1)
                for g in range(GH):
                    last = pe.matmul(ps[:, 0, 128 * g:128 * g + 128], w_all[:, GH * c + g, :], s[:, c % 2, g, :],
                                     start=True, stop=True)
                last.then_inc(ws_done, 1)
                if c >= 1:
                    squares_sum(c - 1)
                if h >= 1:
                    samples_output(h - 1, c % 2)
                pe.wait_ge(vn_done, c + 1)
                for g in range(GH):
                    last = pe.matmul(ps[:, 3, 128 * g:128 * g + 128], kd_all[:, GH * c + g, :], vn[:, c % 2, g, :],
                                     start=True, stop=True)
                last.then_inc(ds_done, 1)
                if c >= 2:
                    pe.wait_ge(y_done, c - 1)
                for g in range(GH):
                    o = ps[:, 1 + c % 2, 128 * g:128 * g + 128]
                    pe.matmul(o, s[:, c % 2, g, :], qe_all[:, GH * c + g, :], start=True, stop=False)
                    last = pe.matmul(o, vn[:, c % 2, g, :], attn_all[:, GH * c + g, :], start=False, stop=True)
                last.then_inc(o_done, 1)
                if c % 2 == 0:
                    new_values(h)
            for half in range(2):
                samples_output(GH - 1, half)
            squares_sum(NCK - 1)
            squares_sum(NCK)

        @block.vector
        def _(dve):
            def new_states(h, half):
                dve.wait_ge(rows_done, h + 1)
                dve.wait_ge(decayed, h + 1)
                for n in range(S // 2 * half, S // 2 * (half + 1)):
                    last = dve.scalar_tensor_tensor(st[:, h, n, :], ps[:, 5 + n // 4, n % 4 * 128:n % 4 * 128 + 128],
                                                    qkv[:, GH + h, n:n + 1], st[:, h, n, :], ALU.mult, ALU.add)
                last.then_inc(st_done, 1)

            def normed(c):
                w = width(c)
                dve.wait_ge(r_done, c + 1)
                dve.tensor_tensor(y[:, c % 2, :, 0:w], chunk_out(c), r[:, c % 2, :, 0:w], ALU.mult).then_inc(y_done, 1)
                dve.wait_ge(y_done, c + 1)
                if c == 0:
                    dve.wait_ge(gate_in, 16)
                if c >= 2:
                    dve.wait_ge(out_stored[c % 2], 16 * (c // 2))
                dve.scalar_tensor_tensor(out[:, c % 2, :, 0:w], y[:, c % 2, :, 0:w], gains[:, G_GDN:G_GDN + 1],
                                         gate[:, :, CHUNK * c:CHUNK * c + w], ALU.mult, ALU.mult).then_inc(out_done, 1)

            dve.memset(s[:, 0], 0.0).then_inc(s_done, 1)
            dve.wait_ge(qkv_in, 16)
            by_head = [gs[:, a, :].rearrange("p (h s) -> p h s", h=GH) for a in range(2)]
            dve.tensor_tensor(vb[:, :, :], qkv[:, 2 * GH:3 * GH, :], by_head[1], ALU.mult).then_inc(scaled_done, 1)
            dve.scalar_tensor_tensor(kb[:, :, :], qkv[:, GH:2 * GH, :], -1.0, by_head[0], ALU.mult,
                                     ALU.mult).then_inc(scaled_done, 1)
            dve.wait_ge(scaled_done, 2)
            dve.tensor_tensor(kb[:, :, :], kb[:, :, :], by_head[1], ALU.mult).then_inc(scaled_done, 1)
            for c in range(NCK):
                dve.wait_ge(ws_done, c + 1)
                if c >= 2:
                    dve.wait_ge(o_done, c - 1)
                dve.tensor_tensor(vn[:, c % 2], u_all[:, GH * c:GH * c + GH, :],
                                  ps[:, 0, :].rearrange("p (h n) -> p h n", h=GH), ALU.subtract).then_inc(vn_done, 1)
                if c % 2 == 0 and c > 0:
                    new_states(c // 2 - 1, 1)
                dve.wait_ge(ds_done, c + 1)
                dve.wait_ge(se_done, c + 1)
                if c >= 1:
                    dve.wait_ge(o_done, c)
                dve.tensor_tensor(s[:, (c + 1) % 2], se[:, :, :], ps[:, 3, :].rearrange("p (h n) -> p h n", h=GH),
                                  ALU.add).then_inc(s_done, 1)
                if c >= 1:
                    normed(c - 1)
                if c % 2:
                    new_states(c // 2, 0)
            new_states(GH - 1, 1)
            normed(NCK - 1)
            normed(NCK)

        @block.gpsimd
        def _(pool):
            for c in range(NCK):
                pool.wait_ge(s_done, c + 1)
                pool.tensor_tensor(se[:, :, :], s[:, c % 2],
                                   cols[:, 3, GH * c:GH * c + GH, None].broadcast_to((128, GH, 128)),
                                   ALU.mult).then_inc(se_done, 1)
                if c % 2:
                    h = c // 2
                    pool.wait_ge(rows_done, h + 1)
                    pool.tensor_tensor(st[:, h], st[:, h], gs[:, 0, S * h:S * h + S, None].broadcast_to((128, S, 128)),
                                       ALU.mult).then_inc(decayed, 1)

        @block.scalar
        def _(act):
            def squares(c):
                act.wait_ge(*((o_done, c + 1) if c < NCK else (so_done, 2 * GH)))
                if c >= 2:
                    act.wait_ge(ss_done, c - 1)
                act.activation(sq[:, c % 2, :, 0:width(c)], chunk_out(c), AF.Square).then_inc(sq_done, 1)

            def inverse_root(c):
                rr = r[:, c % 2, :, 0:width(c)]
                act.wait_ge(ss_done, c + 1)
                if c >= 2:
                    act.wait_ge(y_done, c - 1)
                act.activation(rr, sums(c), AF.Ln, bias=k.c("eps"), scale=1.0 / 128).then_inc(log_done, 1)
                act.wait_ge(log_done, c + 1)
                act.activation(rr, rr, AF.Exp, scale=-0.5).then_inc(r_done, 1)

            act.preload_act_table_set("natural_log_exp_and_others")
            for c in range(NCK):
                squares(c)
                if c >= 1:
                    inverse_root(c - 1)
            squares(NCK)
            inverse_root(NCK - 1)
            inverse_root(NCK)


def cross_attend(k, xq, kv, kv0, mem_k, mem_v, s0, og):
    k.recycle()
    nc, ALU, AF, f32, ps = k.nc, k.ALU, k.AF, k.f32, k.ps
    NB = 4
    BT = NB * 128
    PER = T // BT
    NBATCH = XH * PER
    MB = MEM // 128
    NR = S * XH
    NKV = 4
    SCALE = XD ** -0.5
    HALF = D // 2
    MID = NBATCH // 2
    PV_SLOTS = [(MID, 2)] + [(n, j) for n in range(MID + 1, NBATCH) for j in range(3)]
    assert len(PV_SLOTS) >= S and 2 * MID == S
    with ExitStack() as ctx:
        def sb(name, shape):
            return ctx.enter_context(nc.sbuf_tensor(k.name(name), shape, f32))

        def sem(name):
            return k.semaphore(k.name(name))

        q = sb("xa_q", [128, 2, 2, T])
        kk, vt = sb("xa_k", [128, 2, 2, MEM]), sb("xa_vt", [128, 2, 2, MEM])
        v = sb("xa_v", [128, MB, XD])
        p = sb("xa_p", [128, 2, NB, MEM])
        pt = sb("xa_pt", [128, MB, BT])
        mx, nmx, sm, rs = (sb(n, [128, 2, NB]) for n in ("xa_mx", "xa_nmx", "xa_sum", "xa_rs"))
        o = sb("xa_o", [128, 2, 2, BT])
        head_in, stored = ([sem(f"{n}{u}") for u in range(2)] for n in ("head_in", "stored"))
        (vt_done, v_done, s_done, mx_done, nmx_done, e_done, rs_done, p_done, t_done, pt_done, o_done, oc_done) = (
            sem(n) for n in ("vt", "v", "s", "mx", "nmx", "e", "rs", "p", "t", "pt", "o", "oc"))
        qs = sb("xs_q", [128, KT, S])
        cached = sb("xs_kv", [128, NKV, MB, D])
        prod = sb("xs_prod", [128, MB, D])
        z = sb("xs_z", [128, MB, NR])
        zt = sb("xs_zt", [NR, MEM])
        smx, snmx, ssm, srs = (sb(n, [NR, 1]) for n in ("xs_mx", "xs_nmx", "xs_sum", "xs_rs"))
        spt = sb("xs_pt", [128, MB, S, NR + XH])
        om = sb("xs_masked", [2 * NR, HALF])
        so = sb("xs_o", [128, KT, S])
        cached_in = [sem(f"cached{j}") for j in range(NKV)]
        (q_in, rows_done, dot_done, zt_done, smx_done, snmx_done, se_done, srs_done, sp_done, st_done, spt_done,
         pv_done, om_done, col_done, so_done, so_stored, zeroed) = (
            sem(n) for n in ("q_in", "rows", "dot", "zt", "smx", "snmx", "se", "srs", "sp", "st", "spt", "pv", "om",
                             "col", "so", "so_st", "zeroed"))
        block = ctx.enter_context(nc.Block())

        @block.sync
        def _(sp):
            def head(h):
                u = h % 2
                if h >= 2:
                    sp.wait_ge(s_done, PER * (h - 1))
                    sp.wait_ge(vt_done, h - 1)
                for dst, src in ((q, xq[2 * h:2 * h + 2, :, 0:T]), (kk, kv[kv0 + 2 * h:kv0 + 2 * h + 2]),
                                 (vt, kv[kv0 + 8 + 2 * h:kv0 + 8 + 2 * h + 2])):
                    sp.dma_start(dst[:, u], src.rearrange("t p n -> p t n")).then_inc(head_in[u], 16)

            def cache(i):
                if i >= S + NKV:
                    sp.wait_ge(pv_done, i - S - NKV + 1)
                elif i >= NKV:
                    sp.wait_ge(dot_done, i - NKV + 1)
                src = mem_k[s0 + i] if i < S else mem_v[s0 + i - S]
                sp.dma_start(cached[:, i % NKV], src.rearrange("(b p) n -> p b n", p=128)).then_inc(cached_in[i % NKV], 16)

            def store(n):
                sp.wait_ge(oc_done, n + 1)
                sp.dma_start(og[2 * (n // PER):2 * (n // PER) + 2, :, BT * (n % PER):BT * (n % PER) + BT]
                             .rearrange("t p n -> p t n"), o[:, n % 2]).then_inc(stored[n % 2], 16)

            head(0)
            sp.dma_start(qs[:, :, :], xq[:, :, T:NT].rearrange("t p n -> p t n")).then_inc(q_in, 16)
            cache(0)
            cache(1)
            head(1)
            cache(2)
            cache(3)
            for n in range(NBATCH):
                if n >= 1:
                    store(n - 1)
                if n % PER == 0 and 2 <= n // PER + 1 < XH:
                    head(n // PER + 1)
                for j in range(2):
                    if NKV + 2 * n + j < 2 * S:
                        cache(NKV + 2 * n + j)
            store(NBATCH - 1)
            sp.wait_ge(so_done, 1)
            sp.dma_start(og[0:KT, :, T:NT].rearrange("t p n -> p t n"), so[:, :, :]).then_inc(so_stored, 16)
            sp.wait_ge(so_stored, 16)
            for u in range(2):
                sp.wait_ge(stored[u], 16 * (NBATCH // 2))

        @block.tensor
        def _(pe):
            def scores(n):
                h = n // PER
                if n % PER == 0:
                    pe.wait_ge(head_in[h % 2], 48 * (h // 2 + 1))
                if n >= 1:
                    pe.wait_ge(e_done, NB * n)
                for b in range(NB):
                    a = BT * (n % PER) + 128 * b
                    for j in range(2):
                        last = pe.matmul(ps[:, b // 2, MEM * (b % 2):MEM * (b % 2) + MEM], q[:, h % 2, j, a:a + 128],
                                         kk[:, h % 2, j, :], start=(j == 0), stop=(j == 1))
                last.then_inc(s_done, 1)

            def values(h):
                if h >= 1:
                    pe.wait_ge(oc_done, PER * h)
                for m in range(MB):
                    for j in range(2):
                        last = pe.transpose(ps[:, 4, (2 * m + j) * 128:(2 * m + j) * 128 + 128],
                                            vt[:, h % 2, j, 128 * m:128 * m + 128], k.c("ident"))
                last.then_inc(vt_done, 1)

            def transposes(n):
                pe.wait_ge(p_done, n + 1)
                if n >= 1:
                    pe.wait_ge(pt_done, n)
                for m in range(MB):
                    for b in range(NB):
                        last = pe.transpose(ps[:, 2 + m, 128 * b:128 * b + 128], p[:, n % 2, b, 128 * m:128 * m + 128],
                                            k.c("ident"))
                last.then_inc(t_done, 1)

            def outputs(n):
                pe.wait_ge(pt_done, n + 1)
                if n % PER == 0:
                    pe.wait_ge(v_done, n // PER + 1)
                if n >= 1:
                    pe.wait_ge(oc_done, n)
                for j in range(2):
                    for m in range(MB):
                        last = pe.matmul(ps[:, 4 + j, :], v[:, m, 128 * j:128 * j + 128], pt[:, m, :], start=(m == 0),
                                         stop=(m == MB - 1))
                last.then_inc(o_done, 1)

            def rows(s):
                if s == 0:
                    pe.wait_ge(q_in, 16)
                else:
                    pe.wait_ge(dot_done, s)
                for f in range(KT):
                    last = pe.matmul(ps[:, 6 + f // 4, f % 4 * 128:f % 4 * 128 + 128],
                                     qs[:, f, s:s + 1].broadcast_to((128, 128)), k.c("ident"), start=True, stop=True)
                last.then_inc(rows_done, 1)

            def sample_weights_in():
                pe.wait_ge(dot_done, S)
                for m in range(MB):
                    last = pe.transpose(ps[0:NR, 6, 128 * m:128 * m + 128], z[:, m, :], k.c("ident"))
                last.then_inc(zt_done, 1)

            def sample_weights_out():
                pe.wait_ge(sp_done, 1)
                for m in range(MB):
                    last = pe.transpose(ps[:, 7, NR * m:NR * m + NR], zt[:, 128 * m:128 * m + 128],
                                        k.c("ident")[0:NR, 0:NR])
                last.then_inc(st_done, 1)

            def weighted(s):
                pe.wait_ge(cached_in[(S + s) % NKV], 16 * ((S + s) // NKV + 1))
                if s == 0:
                    pe.wait_ge(spt_done, 1)
                for m in range(MB):
                    block = spt[:, m, :, :].rearrange("p s w -> p (s w)")[:, NR * s:NR * s + NR]
                    for c in range(2):
                        last = pe.matmul(ps[NR * c:NR * c + NR, 6, :], block,
                                         cached[:, s % NKV, m, HALF * c:HALF * c + HALF], start=(s == 0 and m == 0),
                                         stop=(s == S - 1 and m == MB - 1), skip_group_check=True)
                last.then_inc(pv_done, 1)

            def columns():
                pe.wait_ge(om_done, 1)
                for f in range(KT):
                    c = f // 4
                    last = pe.matmul(ps[:, 7, S * f:S * f + S], om[:, f % 4 * 128:f % 4 * 128 + 128],
                                     k.c("xs_pick")[0:2 * NR, S * c:S * c + S], start=True, stop=True)
                last.then_inc(col_done, 1)

            def beside(n, j):
                if n < MID and j != 1:
                    rows(2 * n + j // 2)
                if n == MID and j == 0:
                    sample_weights_in()
                if n == MID and j == 1:
                    sample_weights_out()
                if (n, j) in PV_SLOTS and PV_SLOTS.index((n, j)) < S:
                    weighted(PV_SLOTS.index((n, j)))

            scores(0)
            for n in range(NBATCH):
                if n % PER == 0:
                    values(n // PER)
                if n + 1 < NBATCH:
                    scores(n + 1)
                beside(n, 0)
                transposes(n)
                beside(n, 1)
                outputs(n)
                beside(n, 2)
            columns()

        @block.vector
        def _(dve):
            def maxima(n):
                dve.wait_ge(s_done, n + 1)
                if n >= 2:
                    dve.wait_ge(e_done, NB * (n - 1))
                dve.tensor_reduce(mx[:, n % 2, :], ps[:, 0:2, :].rearrange("p b (c m) -> p (b c) m", c=2), k.AX.X,
                                  ALU.max).then_inc(mx_done, 1)
                dve.wait_ge(mx_done, n + 1)
                dve.tensor_scalar(nmx[:, n % 2, :], mx[:, n % 2, :], -SCALE, None, ALU.mult).then_inc(nmx_done, 1)

            def weights(n):
                dve.wait_ge(e_done, NB * (n + 1))
                dve.reciprocal(rs[:, n % 2, :], sm[:, n % 2, :]).then_inc(rs_done, 1)
                dve.wait_ge(rs_done, n + 1)
                dve.tensor_tensor(p[:, n % 2], p[:, n % 2], rs[:, n % 2, :, None].broadcast_to((128, NB, MEM)),
                                  ALU.mult).then_inc(p_done, 1)

            def dots(s):
                dve.wait_ge(cached_in[s % NKV], 16 * (s // NKV + 1))
                dve.wait_ge(rows_done, s + 1)
                if s >= 1:
                    dve.wait_ge(dot_done, s)
                for m in range(MB):
                    for h in range(XH):
                        f = slice(XD * h, XD * h + XD)
                        last = dve.scalar_tensor_tensor(prod[:, m, f], cached[:, s % NKV, m, f], 1.0,
                                                        ps[:, 6 + h // 2, XD * (h % 2):XD * (h % 2) + XD], ALU.mult,
                                                        ALU.mult, accum_out=z[:, m, XH * s + h:XH * s + h + 1])
                last.then_inc(dot_done, 1)

            def sample_max():
                dve.wait_ge(zt_done, 1)
                dve.tensor_reduce(smx[:, :], ps[0:NR, 6, 0:MEM], k.AX.X, ALU.max).then_inc(smx_done, 1)
                dve.wait_ge(smx_done, 1)
                dve.tensor_scalar(snmx[:, :], smx[:, :], -SCALE, None, ALU.mult).then_inc(snmx_done, 1)

            def sample_weights():
                dve.wait_ge(se_done, 1)
                dve.reciprocal(srs[:, :], ssm[:, :]).then_inc(srs_done, 1)
                dve.wait_ge(srs_done, 1)
                dve.tensor_scalar(zt[:, :], zt[:, :], srs[:, :], None, ALU.mult).then_inc(sp_done, 1)

            def beside(n, j):
                if n < MID and j != 1:
                    dots(2 * n + j // 2)
                if n == MID and j == 0:
                    sample_max()
                    sample_weights()

            dve.memset(spt[:, :, :, :], 0.0).then_inc(zeroed, 1)
            maxima(0)
            weights(0)
            for n in range(NBATCH):
                if n + 1 < NBATCH:
                    maxima(n + 1)
                beside(n, 0)
                if n + 1 < NBATCH:
                    weights(n + 1)
                beside(n, 1)
                beside(n, 2)
            dve.wait_ge(pv_done, S)
            dve.tensor_tensor(om[:, :], ps[0:2 * NR, 6, :], k.c("xs_diag")[0:2 * NR, :], ALU.mult).then_inc(om_done, 1)

        @block.scalar
        def _(act):
            def exponentials(n):
                act.wait_ge(nmx_done, n + 1)
                if n >= 2:
                    act.wait_ge(t_done, n - 1)
                for b in range(NB):
                    act.activation(p[:, n % 2, b, :], ps[:, b // 2, MEM * (b % 2):MEM * (b % 2) + MEM], AF.Exp,
                                   bias=nmx[:, n % 2, b:b + 1], scale=SCALE,
                                   accum_out=sm[:, n % 2, b:b + 1]).then_inc(e_done, 1)

            def copy_out(n):
                act.wait_ge(o_done, n + 1)
                if n >= 2:
                    act.wait_ge(stored[n % 2], 16 * (n // 2))
                act.copy(o[:, n % 2], ps[:, 4:6, :]).then_inc(oc_done, 1)

            def beside(n, j):
                if n == MID and j == 0:
                    act.wait_ge(snmx_done, 1)
                    act.activation(zt[:, :], ps[0:NR, 6, 0:MEM], AF.Exp, bias=snmx[:, :], scale=SCALE,
                                   accum_out=ssm[:, :]).then_inc(se_done, 1)
                if n == MID and j == 1:
                    act.wait_ge(st_done, 1)
                    act.wait_ge(zeroed, 1)
                    act.copy(spt[:, :, :, 0:XH], ps[:, 7, 0:MB * NR].rearrange("p (m s h) -> p m s h", m=MB, s=S)
                             ).then_inc(spt_done, 1)

            exponentials(0)
            for n in range(NBATCH):
                if n >= 1:
                    copy_out(n - 1)
                if n % PER == 0:
                    act.wait_ge(vt_done, n // PER + 1)
                    act.copy(v[:, :, :].rearrange("p m d -> p (m d)"), ps[:, 4, :]).then_inc(v_done, 1)
                if n + 1 < NBATCH:
                    exponentials(n + 1)
                beside(n, 0)
                act.wait_ge(t_done, n + 1)
                act.copy(pt[:, :, :], ps[:, 2:4, :]).then_inc(pt_done, 1)
                beside(n, 1)
                beside(n, 2)
            copy_out(NBATCH - 1)
            act.wait_ge(col_done, 1)
            act.copy(so[:, :, :].rearrange("p f s -> p (f s)"), ps[:, 7, 0:KT * S]).then_inc(so_done, 1)


def rotary_tiles(k, ctx):
    def sb(name):
        return ctx.enter_context(k.nc.sbuf_tensor(k.name(name), [128, 2, NT], k.f32))

    return sb("rope"), sb("rot_x"), sb("rot_t"), sb("ret_q"), sb("ret_k")


def rotate(k, pool, cc, h, cs, x, t, q, kk, before=None):
    ALU = k.ALU
    x_in, parts, done = (k.semaphore(k.name(n)) for n in ("rot_in", "rot_products", "rotated"))
    n = 0
    for j, (t0, dst) in enumerate(((C_Q, q), (C_K, kk))):
        if before:
            before(j)
        if j:
            pool.wait_ge(done, 2)
        pool.dma_start(x[:, :, :], cc[t0 + 2 * h:t0 + 2 * h + 2].rearrange("t p n -> p t n")).then_inc(x_in, 16)
        pool.wait_ge(x_in, 16 * (j + 1))
        for half, (a, b, op) in enumerate(((0, 1, ALU.subtract), (1, 0, ALU.add))):
            if n:
                pool.wait_ge(done, n // 2)
            pool.tensor_tensor(t[:, 0], x[:, a], cs[:, 0, :], ALU.mult).then_inc(parts, 1)
            pool.tensor_tensor(t[:, 1], x[:, b], cs[:, 1, :], ALU.mult).then_inc(parts, 1)
            n += 2
            pool.wait_ge(parts, n)
            pool.tensor_tensor(dst[:, half, :], t[:, 0], t[:, 1], op).then_inc(done, 1)


def first_rotation(k, pool, stored, cc, rope, tiles):
    def before(j):
        for u in range(2):
            pool.wait_ge(stored[u], 16 * ((C_Q, C_K)[j] // 2 + 1))

    table = k.semaphore(k.name("table"))
    pool.dma_start(tiles[0][:, :, :], rope).then_inc(table, 16)
    pool.wait_ge(table, 16)
    rotate(k, pool, cc, 0, *tiles, before=before)


def retention(k, cc, og, gains, ret_const, state_in, state_p, state_s, tiles):
    nc, f32 = k.nc, k.f32
    cs, x, t, *first = tiles
    with ExitStack() as ctx:
        qk = [first, [ctx.enter_context(nc.sbuf_tensor(k.name(n), [128, 2, NT], f32)) for n in ("ret_q", "ret_k")]]
        for h in range(RH):
            retention_head(k, cc, h, ret_const, *qk[h % 2], og, gains, state_in, state_p, state_s,
                           (cs, x, t, *qk[(h + 1) % 2]) if h + 1 < RH else None)


def retention_head(k, cc, h, ret_const, q, kk, og, gains, state_in, state_p, state_s, rotation):
    k.recycle()
    nc, ALU, AF, f32, ps = k.nc, k.ALU, k.AF, k.f32, k.ps
    NSL = 4
    NV = 4
    DV = 4
    assert NCK == S
    with ExitStack() as ctx:
        def sb(name, shape):
            return ctx.enter_context(nc.sbuf_tensor(k.name(name), shape, f32))

        def sem(name):
            return k.semaphore(k.name(name))

        rc = sb("ret_c", [128, RETC_W])
        vt = sb("ret_vt", [128, NV, DV, 128])
        v = sb("ret_v", [128, 2, 512])
        kz = sb("ret_kz", [128, 2, 2, 128])
        qx = sb("ret_qx", [128, 2, 2, 128])
        inner = sb("ret_inner", [128, 2, 128])
        s = sb("ret_s", [128, 2, 2, 512])
        gate = sb("ret_gate", [128, DV, NT])
        sq, y, out = (sb(n, [128, 2, DV, 128]) for n in ("ret_sq", "ret_y", "ret_out"))
        r = sb("ret_r", [128, 2, 128])
        vs, ks = sb("rs_v", [128, DV, S]), sb("rs_k", [128, 2, S])
        old = sb("rs_old", [128, NSL, 2, 512])
        new = sb("rs_new", [128, 2, 2, 512])
        c_in, gate_in, vs_in, p_stored = (sem(n) for n in ("c_in", "gate_in", "vs_in", "p_stored"))
        v_in = [sem(f"v_in{u}") for u in range(NV)]
        out_stored, new_stored = ([sem(f"{n}{u}") for u in range(2)] for n in ("out_st", "new_st"))
        old_in = [sem(f"old{j}") for j in range(NSL)]
        i_done, in_done, kt_done, kz_done, vt_done, v_done, qx_done, o_done, ds_done, s_done = (
            sem(n) for n in ("i", "inner", "kt", "kz", "vt", "v", "qx", "o", "ds", "s"))
        sq_done, ss_done, log_done, r_done, y_done, out_done = (sem(n) for n in ("sq", "ss", "log", "r", "y", "out"))
        ks_done, rows_done, scaled, new_done, so_done = (sem(n) for n in ("ks", "rows", "scaled", "new", "so"))
        SO = 128
        SS = 256
        samples_out = ps[:, 0, SO:SO + DV * S].rearrange("p (s d) -> p d s", d=DV)

        def width(c):
            return CHUNK if c < NCK else S

        def chunk_out(c):
            return ps[:, 3 + c % 2, :].rearrange("p (d n) -> p d n", d=DV) if c < NCK else samples_out

        block = ctx.enter_context(nc.Block())

        @block.sync
        def _(sp):
            def values(c):
                if c >= NV:
                    sp.wait_ge(vt_done, c - NV + 1)
                sp.dma_start(vt[:, c % NV], cc[C_V + 4 * h:C_V + 4 * h + 4, :, CHUNK * c:CHUNK * c + CHUNK]
                             .rearrange("t p n -> p t n")).then_inc(v_in[c % NV], 16)

            def state(n):
                if n >= NSL:
                    sp.wait_ge(scaled, n - NSL + 1)
                sp.dma_start(old[:, n % NSL], state_in[n, h].rearrange("t p n -> p t n")).then_inc(old_in[n % NSL], 16)

            def store_state(n):
                sp.wait_ge(new_done, 2 * n + 2)
                sp.dma_start(state_s[n, h].rearrange("t p n -> p t n"), new[:, n % 2]).then_inc(new_stored[n % 2], 16)

            def store_out(c):
                sp.wait_ge(out_done, c + 1)
                sp.dma_start(og[4 * h:4 * h + 4, :, CHUNK * c:CHUNK * c + width(c)].rearrange("t p n -> p t n"),
                             out[:, c % 2, :, 0:width(c)]).then_inc(out_stored[c % 2], 16)

            values(0)
            sp.dma_start(rc[:, :], ret_const[h]).then_inc(c_in, 16)
            values(1)
            sp.dma_start(vs[:, :, :], cc[C_V + 4 * h:C_V + 4 * h + 4, :, T:NT].rearrange("t p n -> p t n")).then_inc(vs_in, 16)
            state(0)
            values(2)
            state(1)
            sp.dma_start(gate[:, :, :], cc[C_Z + 4 * h:C_Z + 4 * h + 4].rearrange("t p n -> p t n")).then_inc(gate_in, 16)
            values(3)
            state(2)
            state(3)
            for c in range(NCK):
                if c + NV < NCK:
                    values(c + NV)
                if c + NSL < S:
                    state(c + NSL)
                store_state(c)
                if c >= 1:
                    store_out(c - 1)
            sp.wait_ge(s_done, 2 * NCK + 1)
            sp.dma_start(state_p[h].rearrange("t p n -> p t n"), s[:, NCK % 2]).then_inc(p_stored, 16)
            store_out(NCK - 1)
            store_out(NCK)
            sp.wait_ge(p_stored, 16)
            sp.wait_ge(out_stored[0], 16 * (NCK // 2 + 1))
            sp.wait_ge(out_stored[1], 16 * (NCK // 2))
            for u in range(2):
                sp.wait_ge(new_stored[u], 16 * (S // 2))

        @block.tensor
        def _(pe):
            def rows(n):
                if n >= 1:
                    pe.wait_ge(new_done, 2 * n)
                for d in range(DV):
                    last = pe.matmul(ps[:, 7, 128 * d:128 * d + 128], vs[:, d, n:n + 1].broadcast_to((128, 128)),
                                     k.c("ident"), start=True, stop=True)
                last.then_inc(rows_done, 1)

            def sample_out(n):
                pe.wait_ge(new_done, 2 * n + 2)
                for d in range(DV):
                    for t in range(2):
                        last = pe.matmul(ps[:, 0, SO + DV * n + d:SO + DV * n + d + 1], new[:, n % 2, t, 128 * d:128 * d + 128],
                                         q[:, t, T + n:T + n + 1], start=(t == 0), stop=(t == 1))
                last.then_inc(so_done, 1)

            def prepare(c):
                a, b = CHUNK * c, CHUNK * c + CHUNK
                if c >= 1:
                    pe.wait_ge(in_done, c)
                if c >= 2:
                    sample_out(c - 2)
                for t in range(2):
                    last = pe.matmul(ps[:, 0, 0:128], kk[:, t, a:b], q[:, t, a:b], start=(t == 0), stop=(t == 1))
                last.then_inc(i_done, 1)
                if c >= 1:
                    pe.wait_ge(kz_done, c)
                if c >= 3:
                    pe.wait_ge(log_done, c - 2)
                for t in range(2):
                    last = pe.transpose(ps[:, 1, 128 * t:128 * t + 128], kk[:, t, a:b], k.c("ident"))
                last.then_inc(kt_done, 1)
                if c >= 1:
                    pe.wait_ge(v_done, c)
                pe.wait_ge(v_in[c % NV], 16 * (c // NV + 1))
                for t in range(DV):
                    last = pe.transpose(ps[:, 2, 128 * t:128 * t + 128], vt[:, c % NV, t, :], k.c("ident"))
                last.then_inc(vt_done, 1)

            def squares_sum(c):
                pe.wait_ge(sq_done, c + 1)
                if c >= 1:
                    pe.wait_ge(log_done, c)
                pe.wait_ge(kz_done, min(c + 3, NCK))
                for d in range(DV):
                    last = pe.matmul(ps[:, 1, SS:SS + width(c)], k.c("ones"), sq[:, c % 2, d, 0:width(c)],
                                     start=(d == 0), stop=(d == DV - 1))
                last.then_inc(ss_done, 1)

            prepare(0)
            pe.wait_ge(vs_in, 16)
            rows(0)
            for c in range(NCK):
                if c + 1 < NCK:
                    prepare(c + 1)
                pe.wait_ge(kz_done, c + 1)
                pe.wait_ge(v_done, c + 1)
                pe.wait_ge(s_done, 2 * c + 1)
                for t in range(2):
                    last = pe.matmul(ps[:, 5 + t, :], kz[:, c % 2, t, :], v[:, c % 2, :], start=True, stop=True)
                last.then_inc(ds_done, 1)
                if c >= 1:
                    squares_sum(c - 1)
                pe.wait_ge(in_done, c + 1)
                pe.wait_ge(qx_done, c + 1)
                if c >= 2:
                    pe.wait_ge(y_done, c - 1)
                for d in range(DV):
                    o = ps[:, 3 + c % 2, 128 * d:128 * d + 128]
                    pe.matmul(o, v[:, c % 2, 128 * d:128 * d + 128], inner[:, c % 2, :], start=True, stop=False)
                    for t in range(2):
                        last = pe.matmul(o, s[:, c % 2, t, 128 * d:128 * d + 128], qx[:, c % 2, t, :], start=False,
                                         stop=(t == 1))
                last.then_inc(o_done, 1)
                if c + 1 < S:
                    rows(c + 1)
            pe.wait_ge(in_done, NCK)
            sample_out(S - 2)
            sample_out(S - 1)
            squares_sum(NCK - 1)
            squares_sum(NCK)

        @block.vector
        def _(dve):
            dve.memset(s[:, 0], 0.0).then_inc(s_done, 1)
            dve.tensor_scalar(ks[:, :, :], kk[:, :, T:NT], XD ** -0.5, None, ALU.mult).then_inc(ks_done, 1)
            dve.wait_ge(c_in, 16)

            def prepare(c):
                a, b = CHUNK * c, CHUNK * c + CHUNK
                if c >= 2:
                    dve.wait_ge(o_done, c - 1)
                dve.tensor_tensor(qx[:, c % 2], q[:, :, a:b], rc[:, None, 128:256].broadcast_to((128, 2, 128)),
                                  ALU.mult).then_inc(qx_done, 1)
                dve.wait_ge(i_done, c + 1)
                dve.tensor_tensor(inner[:, c % 2], ps[:, 0, 0:128], rc[:, 0:128], ALU.mult).then_inc(in_done, 1)

            def sample(n):
                dve.wait_ge(rows_done, n + 1)
                dve.wait_ge(scaled, n + 1)
                for t in range(2):
                    dve.scalar_tensor_tensor(new[:, n % 2, t, :], ps[:, 7, :], ks[:, t, n:n + 1], new[:, n % 2, t, :],
                                             ALU.mult, ALU.add).then_inc(new_done, 1)

            def normed(c):
                w = width(c)
                dve.wait_ge(r_done, c + 1)
                dve.tensor_tensor(y[:, c % 2, :, 0:w], chunk_out(c), r[:, c % 2, None, 0:w].broadcast_to((128, DV, w)),
                                  ALU.mult).then_inc(y_done, 1)
                dve.wait_ge(y_done, c + 1)
                if c == 0:
                    dve.wait_ge(gate_in, 16)
                if c >= 2:
                    dve.wait_ge(out_stored[c % 2], 16 * (c // 2))
                for d in range(DV):
                    gc = G_RET + d
                    last = dve.scalar_tensor_tensor(out[:, c % 2, d, 0:w], y[:, c % 2, d, 0:w], gains[:, gc:gc + 1],
                                                    gate[:, d, CHUNK * c:CHUNK * c + w], ALU.mult, ALU.mult)
                last.then_inc(out_done, 1)

            prepare(0)
            dve.wait_ge(ks_done, 1)
            for c in range(NCK):
                if c + 1 < NCK:
                    prepare(c + 1)
                dve.wait_ge(ds_done, c + 1)
                if c >= 1:
                    dve.wait_ge(o_done, c)
                dve.wait_ge(s_done, 2 * c + 1)
                for t in range(2):
                    dve.scalar_tensor_tensor(s[:, (c + 1) % 2, t, :], s[:, c % 2, t, :], rc[:, 257:258],
                                             ps[:, 5 + t, :], ALU.mult, ALU.add).then_inc(s_done, 1)
                sample(c)
                if c >= 1:
                    normed(c - 1)
            normed(NCK - 1)
            normed(NCK)

        @block.scalar
        def _(act):
            act.preload_act_table_set("natural_log_exp_and_others")
            act.wait_ge(c_in, 16)

            def prepare(c):
                if c >= 2:
                    act.wait_ge(o_done, c - 1)
                act.wait_ge(kt_done, c + 1)
                act.activation(kz[:, c % 2].rearrange("p t n -> p (t n)"), ps[:, 1, 0:256], AF.Copy,
                               scale=rc[:, 256:257]).then_inc(kz_done, 1)
                act.wait_ge(vt_done, c + 1)
                act.copy(v[:, c % 2, :], ps[:, 2, :]).then_inc(v_done, 1)

            def scale(n):
                act.wait_ge(old_in[n % NSL], 16 * (n // NSL + 1))
                if n >= 2:
                    act.wait_ge(new_stored[n % 2], 16 * (n // 2))
                    act.wait_ge(so_done, n - 1)
                act.activation(new[:, n % 2], old[:, n % NSL], AF.Copy, scale=rc[:, 258:259]).then_inc(scaled, 1)

            def squares(c):
                act.wait_ge(*((o_done, c + 1) if c < NCK else (so_done, S)))
                if c >= 2:
                    act.wait_ge(ss_done, c - 1)
                act.activation(sq[:, c % 2, :, 0:width(c)], chunk_out(c), AF.Square).then_inc(sq_done, 1)

            def inverse_root(c):
                rr = r[:, c % 2, 0:width(c)]
                act.wait_ge(ss_done, c + 1)
                if c >= 2:
                    act.wait_ge(y_done, c - 1)
                act.activation(rr, ps[:, 1, SS:SS + width(c)], AF.Ln, bias=k.c("eps"),
                               scale=1.0 / (128 * DV)).then_inc(log_done, 1)
                act.wait_ge(log_done, c + 1)
                act.activation(rr, rr, AF.Exp, scale=-0.5).then_inc(r_done, 1)

            prepare(0)
            scale(0)
            for c in range(NCK):
                if c + 1 < NCK:
                    prepare(c + 1)
                if c >= 1:
                    inverse_root(c - 1)
                if c + 1 < S:
                    scale(c + 1)
                squares(c)
            squares(NCK)
            inverse_root(NCK - 1)
            inverse_root(NCK)

        if rotation:
            @block.gpsimd
            def _(pool):
                pool.wait_ge(o_done, 1)
                rotate(k, pool, cc, h + 1, *rotation)


INPUTS = ["x_t", "mem_t", "consts", "sb_mask", "rope", "ret_const", "w_ab", "w_oab", "w_c", "w_oc", "w_xq", "w_xo",
          "w_mem", "gains", "conv_w", "sb_bias", "a_log", "dt_bias", "page_table", "cache_k", "cache_v", "gdn_state",
          "gdn_conv", "ret_state", "mem_k", "mem_v"]
OUTPUTS = {
    "y_t": (KT, 128, NT), "sb_k_t": (4, 128, NT), "sb_v_t": (4, 128, NT),
    "gdn_p": (128, GH, 128), "gdn_s": (S, GH, 128, 128),
    "conv_p": (12, 128, 3), "conv_s": (12, 128, S, 3),
    "ret_p": (RH, 2, 128, 512), "ret_s": (S, RH, 2, 128, 512),
    "mem_kv_t": (32, 128, MEM),
}
G_MIX, G_XA, G_FINAL, G_GDN, G_RET, G_W = 0, 16, 32, 40, 41, 45


def trunk_program(nc, ins, outs, upto=99):
    k = Kit()
    k.nc, k.ALU, k.AF, k.AX = nc, mybir.AluOpType, mybir.ActivationFunctionType, mybir.AxisListType
    k.f32, k.f32r = mybir.dt.float32, mybir.dt.float32r
    f32 = k.f32
    count = [0]

    def name(x):
        count[0] += 1
        return f"{x}_{count[0]}"

    k.name = name
    with ExitStack() as ctx:
        def scratch(n, shape):
            return nc.dram_tensor(n, shape, f32, kind="Internal").ap()

        ab = scratch("ab", (AB_TILES, 128, NT))
        cc = scratch("cc", (C_TILES, 128, NT))
        og = scratch("og", (16, 128, NT))
        xq = scratch("xq", (KT, 128, NT))
        conv = scratch("conv", (12, 128, NT))
        k.ps = ctx.enter_context(nc.psum_tensor("ps", [128, 8, 512], f32))
        consts = ctx.enter_context(nc.sbuf_tensor("consts_sb", [128, CONST_W], f32))
        sb_mask = ctx.enter_context(nc.sbuf_tensor("sb_mask_sb", [128, 128], f32))
        gains = ctx.enter_context(nc.sbuf_tensor("gains_sb", [128, G_W], f32))
        k.sb_mask = sb_mask
        k.c = lambda n: consts[:, CONST[n][0]:CONST[n][1]]

        def halves(tokens):
            hi = nc.sbuf_tensor(name("in_hi"), [128, KT, tokens], k.f32r)
            lo = nc.sbuf_tensor(name("in_lo"), [128, KT, tokens], k.f32r)
            return hi, lo

        AF = k.AF
        (a, b), (c, d) = halves(NT), halves(MEM)
        with a as hi, b as lo, c as m_hi, d as m_lo:
            with nc.sbuf_tensor("layer0_in", [128, KT, NT], f32) as x, nc.sbuf_tensor("layer0_sumsq", [128, NT], f32) as sumsq:
                k.x, k.sumsq = x, sumsq
                linear(k, ins["w_ab"], 0, AB_K, hi, lo, norm=(gains, G_MIX), fresh=(ins["x_t"], (
                    (gains[:, :], ins["gains"]), (consts[:, :], ins["consts"]), (sb_mask[:, :], ins["sb_mask"]))),
                    funcs=((AB_K, AF.Copy),), out=ab)
            load_split(k, ins["mem_t"], 0, m_hi, m_lo, MEM)
            weave(k, AB_K, ins["w_ab"], hi, lo, ab, ins["w_mem"], m_hi, m_lo, outs["mem_kv_t"], og, ins["cache_k"],
                  ins["cache_v"], ins["page_table"], ins["sb_bias"])
        x = ctx.enter_context(nc.sbuf_tensor("residual", [128, KT, NT], f32))
        k.x, k.sumsq = x, ctx.enter_context(nc.sbuf_tensor("sumsq", [128, NT], f32))
        if upto < 2:
            return
        sb_prompt(k, ab, og, ins["sb_bias"], [
            (x[:, :, :], ins["x_t"].rearrange("t p n -> p t n")),
            (outs["sb_k_t"], ab[AB_K:AB_K + 4]), (outs["sb_v_t"], ab[AB_V:AB_V + 4]),
            (outs["conv_p"], ab[AB_QKV:AB_QKV + 12, :, T - 3:T])])
        if upto < 4:
            return
        gdn_front(k, ab, conv, ins["conv_w"], ins["gdn_conv"], outs["conv_s"])
        gdn(k, ab, conv, og, gains, ins["a_log"], ins["dt_bias"], ins["gdn_state"], outs["gdn_p"], outs["gdn_s"])
        if upto < 5:
            return

        def project_out(w, w0, tile0, sumsq=True):
            a, b = halves(NT)
            with a as hi, b as lo:
                linear(k, w, w0, KT, hi, lo, load=(og, tile0), resid=x, sumsq=sumsq)

        def cross_attention(layer):
            a, b = halves(NT)
            with a as hi, b as lo:
                linear(k, ins["w_xq"], KT * layer, KT, hi, lo, norm=(gains, G_XA + KT * layer), funcs=((KT, AF.Copy),),
                       out=xq)
            cross_attend(k, xq, outs["mem_kv_t"], 16 * layer, ins["mem_k"], ins["mem_v"], S * layer, og)
            project_out(ins["w_xo"], KT * layer, 0)

        project_out(ins["w_oab"], 0, 0)
        cross_attention(0)
        if upto < 6:
            return
        with ExitStack() as stack:
            tiles = rotary_tiles(k, stack)
            a, b = halves(NT)
            with a as hi, b as lo:
                linear(k, ins["w_c"], 0, C_TILES, hi, lo, norm=(gains, G_MIX + KT),
                       funcs=((C_PLAIN, AF.Copy), (C_TILES - C_PLAIN, AF.Silu)), out=cc,
                       beside=lambda pool, stored: first_rotation(k, pool, stored, cc, ins["rope"], tiles))
            retention(k, cc, og, gains, ins["ret_const"], ins["ret_state"], outs["ret_p"], outs["ret_s"], tiles)
        if upto < 7:
            return
        for half in range(2):
            project_out(ins["w_oc"], KT * half, KT * half, sumsq=(half == 1))
        cross_attention(1)
        final_norm(k, gains, G_FINAL, outs["y_t"])


def weight_tiles(w):
    kk, f = w.shape
    pad = -f % 128
    if pad:
        w = np.concatenate([w, np.zeros((kk, pad), w.dtype)], axis=1)
        f += pad
    return np.ascontiguousarray(w.reshape(kk // 128, 128, f // 128, 128).transpose(2, 1, 0, 3).reshape(f // 128, 128, kk))


def to_tiles(rows):
    n, f = rows.shape
    return np.ascontiguousarray(rows.T.reshape(f // 128, 128, n))


def from_tiles(t):
    return np.ascontiguousarray(t.reshape(-1, t.shape[-1]).T)


def kernel(**inputs):
    import concourse.bacc as bacc
    from concourse.bass_utils import run_bass_kernel_spmd

    arrays = layout(inputs)
    nc = bacc.Bacc("TRN2", target_bir_lowering=False, num_devices=1)
    ins = {n: nc.dram_tensor(f"in_{n}", arrays[n].shape, mybir.dt.from_np(arrays[n].dtype), kind="ExternalInput").ap()
           for n in INPUTS}
    outs = {n: nc.dram_tensor(f"out_{n}", shape, mybir.dt.float32, kind="ExternalOutput").ap()
            for n, shape in OUTPUTS.items()}
    trunk_program(nc, ins, outs)
    r = run_bass_kernel_spmd(nc, [{f"in_{n}": arrays[n] for n in INPUTS}], core_ids=[0])
    got = {n: np.asarray(r.results[0][f"out_{n}"]) for n in OUTPUTS}
    return unpack(got)


def layout(inputs):
    i = {n: np.asarray(v) for n, v in inputs.items()}
    w = i["w_in_ab"][0]
    cuts = np.cumsum([0, 512, 512, 512, 512, 1536, 512, 4, 4])
    q, kk, v, z, qkv, gz, ga, gb = (w[:, cuts[j]:cuts[j + 1]] for j in range(8))
    gates = np.concatenate([ga, gb, np.zeros((D, 120), w.dtype)], axis=1)
    a = {}
    a["x_t"] = to_tiles(np.concatenate([i["x_prompt"][0], i["x_sample"][:, 0]], axis=0))
    a["mem_t"] = to_tiles(i["mem_prompt"][0])
    a["consts"] = constants()
    m = np.where(np.arange(128)[:, None] < np.arange(128)[None, :], 0.0, -1e30).astype(np.float32)
    a["sb_mask"] = m
    a["rope"] = rope_tables()
    a["ret_const"] = retention_tables()
    a["w_ab"] = weight_tiles(np.concatenate([q, kk, gates, v, qkv, z, gz], axis=1))
    a["w_oab"] = weight_tiles(i["w_out_ab"][0])
    a["w_c"] = weight_tiles(i["w_in_c"][0])
    a["w_oc"] = np.concatenate([weight_tiles(i["w_out_c"][0][:D]), weight_tiles(i["w_out_c"][0][D:])], axis=0)
    a["w_xq"] = np.concatenate([weight_tiles(x) for x in i["xa_wq"]], axis=0)
    a["w_xo"] = np.concatenate([weight_tiles(x) for x in i["xa_wo"]], axis=0)
    a["w_mem"] = np.concatenate([weight_tiles(x) for l in range(2) for x in (i["xa_wk"][l], i["xa_wv"][l])], axis=0)
    cols = [i["norm_mix_g"].reshape(16, 128), i["norm_xa_g"].reshape(16, 128), i["norm_final_g"].reshape(8, 128),
            i["gdn_norm_g"].reshape(1, 128), i["ret_norm_g"].reshape(4, 128)]
    a["gains"] = np.ascontiguousarray(np.concatenate(cols, axis=0).T)
    a["conv_w"] = np.ascontiguousarray(i["conv_w_gdn"][0].T.reshape(12, 128, 4).transpose(1, 0, 2))
    a["sb_bias"] = i["sb_logit_bias"]
    a["a_log"] = i["gdn_a_log"]
    a["dt_bias"] = i["gdn_dt_bias"]
    a["page_table"] = i["page_table"].reshape(1, -1).astype(np.int32)
    a["cache_k"] = i["cache_sb_k"].reshape(N_PHYS, PAGE, SBH * SBD)
    a["cache_v"] = i["cache_sb_v"].reshape(N_PHYS, PAGE, SBH * SBD)
    a["gdn_state"] = i["state_gdn"][0]
    a["gdn_conv"] = np.ascontiguousarray(i["state_gdn_conv"][0].transpose(2, 0, 1).reshape(12, 128, S, 3))
    a["ret_state"] = i["state_ret"][0].reshape(S, RH, 2, 128, 512)
    a["mem_k"] = i["cache_mem_k"].reshape(2 * S, MEM, XH * XD)
    a["mem_v"] = i["cache_mem_v"].reshape(2 * S, MEM, XH * XD)
    return {n: np.ascontiguousarray(v) for n, v in a.items()}


def unpack(got):
    y = from_tiles(got["y_t"])
    kv, vv = from_tiles(got["sb_k_t"]), from_tiles(got["sb_v_t"])
    mem = [from_tiles(got["mem_kv_t"][8 * j:8 * j + 8]) for j in range(4)]
    conv_p = got["conv_p"].reshape(1536, 3).T[None, None]
    conv_s = got["conv_s"].reshape(1536, S, 3).transpose(1, 2, 0)[None]
    return (y[:T].reshape(1, T, D), y[T:].reshape(S, 1, D),
            kv[:T].reshape(1, 1, T, SBH, SBD), vv[:T].reshape(1, 1, T, SBH, SBD),
            np.ascontiguousarray(got["gdn_p"].transpose(1, 0, 2)).reshape(1, 1, GH, 128, 128), np.ascontiguousarray(conv_p),
            got["ret_p"].reshape(1, 1, RH, 256, 512),
            np.stack([mem[0], mem[2]]).reshape(2, 1, MEM, XH, XD), np.stack([mem[1], mem[3]]).reshape(2, 1, MEM, XH, XD),
            kv[T:].reshape(1, S, 1, SBH, SBD), vv[T:].reshape(1, S, 1, SBH, SBD),
            got["gdn_s"].reshape(1, S, GH, 128, 128), np.ascontiguousarray(conv_s),
            got["ret_s"].reshape(1, S, RH, 256, 512))
```
